# Optimizing a Trainium2 kernel written in Bass

```python
import math
import jax, jax.numpy as jnp
from jax import lax
import numpy as np

D_MODEL = 1024
BATCH = 1
SEQ = 256
DEPTH = 2

GRID_W = 64
CTX_LEN = 256
EPS = 1e-6
N_MOD = 6
CONV_W = 4
RG_HEADS = 6
RG_HEAD_DIM = 128
RG_WIDTH = RG_HEADS * RG_HEAD_DIM
RG_C = 8.0
FN_GROUPS = 4
FN_GROUP_DIM = 64
FN_WIDTH = FN_GROUPS * FN_GROUP_DIM
EVEN_IN = 2 * RG_WIDTH + FN_WIDTH
EVEN_MIX = RG_WIDTH + FN_WIDTH
ML_HEADS = 4
ML_HEAD_DIM = 128
ML_WIDTH = ML_HEADS * ML_HEAD_DIM
ML_CHUNK = 128
ML_N_GATES = 2 * 2 * ML_HEADS
ML_COLS = 4 * ML_WIDTH + ML_N_GATES
MLA_HEADS = 8
MLA_NOPE = 64
MLA_ROPE = 32
MLA_V = 64
MLA_Q_LORA = 384
MLA_KV_LORA = 256
MLA_WIDTH = MLA_HEADS * MLA_V
MLA_COLS = MLA_Q_LORA + MLA_KV_LORA + MLA_ROPE
ODD_IN = ML_COLS + MLA_COLS
ODD_MIX = ML_WIDTH + MLA_WIDTH
ATTN_BLOCK = 128
ROPE_THETA = 10000.0
PEER_HEADS = 8
PEER_KEY_DIM = 256
PEER_N_KEYS = 128
PEER_N_EXPERTS = PEER_N_KEYS * PEER_N_KEYS
PEER_TOPK = 16
PEER_BLOCK = 128
N_EVEN = (DEPTH + 1) // 2
N_ODD = DEPTH // 2

kernel_name = "hybrid_rglru_fnet_mlstm_mla_peer_dit"

f32 = jnp.float32

def rmsnorm(x, g):
    xf = x.astype(f32)
    y = xf * lax.rsqrt(jnp.mean(xf * xf, axis=-1, keepdims=True) + EPS)
    return (y * g.astype(f32)).astype(x.dtype)

def modulate(h, shift, scale):
    return h * (1.0 + scale) + shift

def centred_dwconv(x, w, b):
    T = x.shape[1]
    lo = CONV_W // 2
    xp = jnp.pad(x, ((0, 0), (lo, CONV_W - 1 - lo), (0, 0)))
    y = xp[:, 0:T] * w[0]
    for j in range(1, CONV_W):
        y = y + xp[:, j:j + T] * w[j]
    return y + b

def linear_scan(a, u, h0):
    def comb(l, r):
        return (l[0] * r[0], r[0] * l[1] + r[1])
    A, Bc = lax.associative_scan(comb, (a, u), axis=1)
    h = A * h0[:, None, :] + Bc
    return h, h[:, -1]

def rglru_direction(xc, wa, ba, wx, bx, lam, h0):
    B_, T, _ = xc.shape
    xh = xc.reshape(B_, T, RG_HEADS, RG_HEAD_DIM)
    r = jax.nn.sigmoid(jnp.einsum('bthd,hde->bthe', xh, wa).reshape(B_, T, RG_WIDTH) + ba)
    i = jax.nn.sigmoid(jnp.einsum('bthd,hde->bthe', xh, wx).reshape(B_, T, RG_WIDTH) + bx)
    log_a = -RG_C * r * jax.nn.softplus(-lam)
    a = jnp.exp(log_a)
    u = jnp.sqrt(-jnp.expm1(2.0 * log_a)) * (i * xc)
    return linear_scan(a, u, h0)

def rglru_mixer(xr_ctx, xr_lat, conv_w, conv_b, wa, ba, wx, bx, lam):
    xc_ctx = centred_dwconv(xr_ctx, conv_w, conv_b).astype(f32)
    xc_lat = centred_dwconv(xr_lat, conv_w, conv_b).astype(f32)
    B_ = xr_lat.shape[0]
    out_ctx = jnp.zeros_like(xc_ctx)
    out_lat = jnp.zeros_like(xc_lat)
    for d in range(2):
        fl = (lambda t: jnp.flip(t, axis=1)) if d else (lambda t: t)
        h0 = jnp.zeros((B_, RG_WIDTH), f32)
        h_c, h_end = rglru_direction(fl(xc_ctx), wa[d], ba[d], wx[d], bx[d], lam[d], h0)
        h_l, _ = rglru_direction(fl(xc_lat), wa[d], ba[d], wx[d], bx[d], lam[d], h_end)
        out_ctx = out_ctx + fl(h_c)
        out_lat = out_lat + fl(h_l)
    return out_ctx, out_lat

def fourier_mixer(xf, w, b):
    B_, T, _ = xf.shape
    xg = xf.astype(f32).reshape(B_, T, FN_GROUPS, FN_GROUP_DIM)
    z = jnp.fft.fft2(xg, axes=(1, 3), norm='ortho').real
    return jnp.einsum('btgd,gde->btge', z, w).reshape(B_, T, FN_WIDTH) + b

def even_mixer(u_ctx, u_lat, w_in, w_out, conv_w, conv_b, wa, ba, wx, bx, lam, fw, fb, need_ctx_out):
    R = RG_WIDTH
    p_ctx = u_ctx @ w_in
    p_lat = u_lat @ w_in
    rnn_ctx, rnn_lat = rglru_mixer(p_ctx[..., :R], p_lat[..., :R], conv_w, conv_b, wa, ba, wx, bx, lam)

    def merge(p, rnn):
        y_a = rnn.astype(p.dtype) * jax.nn.gelu(p[..., R:2 * R])
        y_b = fourier_mixer(p[..., 2 * R:], fw, fb).astype(p.dtype)
        return jnp.concatenate([y_a, y_b], axis=-1) @ w_out

    y_lat = merge(p_lat, rnn_lat)
    y_ctx = merge(p_ctx, rnn_ctx) if need_ctx_out else None
    return y_ctx, y_lat

def mlstm_chunkwise(q, k, v, ig, lf, state):
    B_, H, T, Dh = q.shape
    nc = T // ML_CHUNK
    L = ML_CHUNK

    def chunks(t):
        return jnp.moveaxis(t.reshape((B_, H, nc, L) + t.shape[3:]), 2, 0)

    causal = jnp.tril(jnp.ones((L, L), dtype=bool))

    def step(carry, inp):
        C, n, m = carry
        q_, k_, v_, i_, f_ = inp
        b = jnp.cumsum(f_, axis=-1)
        Dm = jnp.where(causal, b[..., :, None] - b[..., None, :] + i_[..., None, :], -jnp.inf)
        inter = b + m[..., None]
        m_row = jnp.maximum(jnp.max(Dm, axis=-1), inter)
        s = jnp.einsum('bhld,bhsd->bhls', q_, k_) * jnp.exp(Dm - m_row[..., None])
        w_inter = jnp.exp(inter - m_row)
        num = jnp.einsum('bhls,bhsd->bhld', s, v_) + w_inter[..., None] * jnp.einsum('bhde,bhle->bhld', C, q_)
        den = jnp.sum(s, axis=-1) + w_inter * jnp.einsum('bhe,bhle->bhl', n, q_)
        h = num / jnp.maximum(jnp.abs(den), jnp.exp(-m_row))[..., None]
        bL = b[..., -1]
        log_wk = bL[..., None] - b + i_
        m_new = jnp.maximum(bL + m, jnp.max(log_wk, axis=-1))
        wk = jnp.exp(log_wk - m_new[..., None])
        decay = jnp.exp(bL + m - m_new)
        C_new = decay[..., None, None] * C + jnp.einsum('bhs,bhsd,bhse->bhde', wk, v_, k_)
        n_new = decay[..., None] * n + jnp.einsum('bhs,bhse->bhe', wk, k_)
        return (C_new, n_new, m_new), h

    state, hs = lax.scan(step, state, (chunks(q), chunks(k), chunks(v), chunks(ig), chunks(lf)))
    return jnp.moveaxis(hs, 0, 2).reshape(B_, H, T, Dh), state

def mlstm_prep(p, conv_w, conv_b, gate_b):
    B_, T, _ = p.shape
    W = ML_WIDTH
    qk = jax.nn.silu(centred_dwconv(p[..., :2 * W], conv_w, conv_b))

    def heads(t):
        return t.reshape(B_, T, ML_HEADS, ML_HEAD_DIM).transpose(0, 2, 1, 3).astype(f32)

    q = heads(qk[..., :W]) * (ML_HEAD_DIM ** -0.5)
    k = heads(qk[..., W:])
    v = heads(p[..., 2 * W:3 * W])
    o = p[..., 3 * W:4 * W]
    g = (p[..., 4 * W:4 * W + ML_N_GATES] + gate_b).astype(f32).reshape(B_, T, 2, 2, ML_HEADS)
    g = g.transpose(2, 3, 0, 4, 1)
    return q, k, v, o, g[:, 0], jax.nn.log_sigmoid(g[:, 1])

def mlstm_mixer(p_ctx, p_lat, conv_w, conv_b, gate_b, head_g, need_ctx_out):
    qc, kc, vc, oc, igc, lfc = mlstm_prep(p_ctx, conv_w, conv_b, gate_b)
    ql, kl, vl, ol, igl, lfl = mlstm_prep(p_lat, conv_w, conv_b, gate_b)
    B_ = p_lat.shape[0]
    h_ctx = jnp.zeros_like(vc)
    h_lat = jnp.zeros_like(vl)
    for d in range(2):
        fl = (lambda t: jnp.flip(t, axis=2)) if d else (lambda t: t)
        st0 = (jnp.zeros((B_, ML_HEADS, ML_HEAD_DIM, ML_HEAD_DIM), f32),
               jnp.zeros((B_, ML_HEADS, ML_HEAD_DIM), f32),
               jnp.zeros((B_, ML_HEADS), f32))
        hc, st = mlstm_chunkwise(fl(qc), fl(kc), fl(vc), fl(igc[d]), fl(lfc[d]), st0)
        hl, _ = mlstm_chunkwise(fl(ql), fl(kl), fl(vl), fl(igl[d]), fl(lfl[d]), st)
        h_ctx = h_ctx + fl(hc)
        h_lat = h_lat + fl(hl)

    def readout(h, o):
        T = h.shape[2]
        hn = rmsnorm(h, head_g.reshape(1, ML_HEADS, 1, ML_HEAD_DIM))
        hn = hn.transpose(0, 2, 1, 3).reshape(B_, T, ML_WIDTH)
        return jax.nn.sigmoid(o) * hn.astype(o.dtype)

    y_lat = readout(h_lat, ol)
    y_ctx = readout(h_ctx, oc) if need_ctx_out else None
    return y_ctx, y_lat

def axial_rope_angles(row, col):
    half = MLA_ROPE // 2
    inv = ROPE_THETA ** (-jnp.arange(0, half, 2, dtype=f32) / half)
    ang = jnp.concatenate([row[:, None] * inv, col[:, None] * inv], axis=-1)
    return jnp.cos(ang), jnp.sin(ang)

def apply_rot(x, cos, sin):
    x1, x2 = x[..., 0::2], x[..., 1::2]
    return jnp.stack([x1 * cos - x2 * sin, x1 * sin + x2 * cos], axis=-1).reshape(x.shape).astype(x.dtype)

def mla_prep(p, q_norm_g, w_uq, kv_norm_g, w_ukv):
    B_, T, _ = p.shape
    cq = rmsnorm(p[..., :MLA_Q_LORA], q_norm_g)
    q = (cq @ w_uq).reshape(B_, T, MLA_HEADS, MLA_NOPE + MLA_ROPE)
    ckv = rmsnorm(p[..., MLA_Q_LORA:MLA_Q_LORA + MLA_KV_LORA], kv_norm_g)
    kv = (ckv @ w_ukv).reshape(B_, T, MLA_HEADS, MLA_NOPE + MLA_V)
    k_rope = p[..., MLA_Q_LORA + MLA_KV_LORA:]
    return q[..., :MLA_NOPE], q[..., MLA_NOPE:], kv[..., :MLA_NOPE], k_rope, kv[..., MLA_NOPE:]

def mla_attend(q_nope, q_rope, k_nope, k_rope, v):
    B_, Tq, H, _ = q_nope.shape
    nb = Tq // ATTN_BLOCK
    scale = (MLA_NOPE + MLA_ROPE) ** -0.5

    def blocks(t):
        return t.reshape(B_, nb, ATTN_BLOCK, H, t.shape[-1]).swapaxes(0, 1)

    def one_block(qs):
        qn, qr = qs
        s = jnp.einsum('bqhd,bkhd->bhqk', qn, k_nope) + jnp.einsum('bqhd,bkd->bhqk', qr, k_rope)
        pr = jax.nn.softmax(s.astype(f32) * scale, axis=-1).astype(v.dtype)
        return jnp.einsum('bhqk,bkhd->bqhd', pr, v)

    out = lax.map(one_block, (blocks(q_nope), blocks(q_rope)))
    return out.swapaxes(0, 1).reshape(B_, Tq, H * MLA_V)

def mla_mixer(p_ctx, p_lat, q_norm_g, w_uq, kv_norm_g, w_ukv, cos, sin, need_ctx_out):
    qn_c, qr_c, kn_c, kr_c, v_c = mla_prep(p_ctx, q_norm_g, w_uq, kv_norm_g, w_ukv)
    qn_l, qr_l, kn_l, kr_l, v_l = mla_prep(p_lat, q_norm_g, w_uq, kv_norm_g, w_ukv)
    qr_l = apply_rot(qr_l, cos[:, None, :], sin[:, None, :])
    kr_l = apply_rot(kr_l, cos, sin)
    kn = jnp.concatenate([kn_c, kn_l], axis=1)
    kr = jnp.concatenate([kr_c, kr_l], axis=1)
    v = jnp.concatenate([v_c, v_l], axis=1)
    y_lat = mla_attend(qn_l, qr_l, kn, kr, v)
    y_ctx = mla_attend(qn_c, qr_c, kn_c, kr_c, v_c) if need_ctx_out else None
    return y_ctx, y_lat

def odd_mixer(u_ctx, u_lat, w_in, w_out, conv_w, conv_b, gate_b, head_g,
              q_norm_g, w_uq, kv_norm_g, w_ukv, cos, sin, need_ctx_out):
    p_ctx = u_ctx @ w_in
    p_lat = u_lat @ w_in
    ml_ctx, ml_lat = mlstm_mixer(p_ctx[..., :ML_COLS], p_lat[..., :ML_COLS], conv_w, conv_b, gate_b, head_g, need_ctx_out)
    at_ctx, at_lat = mla_mixer(p_ctx[..., ML_COLS:], p_lat[..., ML_COLS:], q_norm_g, w_uq, kv_norm_g, w_ukv, cos, sin, need_ctx_out)
    y_lat = jnp.concatenate([ml_lat, at_lat], axis=-1) @ w_out
    y_ctx = (jnp.concatenate([ml_ctx, at_ctx], axis=-1) @ w_out) if need_ctx_out else None
    return y_ctx, y_lat

def peer_ffn(h, w_q, keys, u, v):
    B_, T, D = h.shape
    tok = h.reshape(-1, PEER_BLOCK, D)

    def one_block(xb):
        q = (xb @ w_q).reshape(PEER_BLOCK, PEER_HEADS, 2, PEER_KEY_DIM // 2)
        s = jnp.einsum('thpd,phkd->thpk', q, keys).astype(f32)
        vals, idx = lax.top_k(s, PEER_TOPK)
        cand = (vals[:, :, 0, :, None] + vals[:, :, 1, None, :]).reshape(PEER_BLOCK, PEER_HEADS, PEER_TOPK * PEER_TOPK)
        cidx = (idx[:, :, 0, :, None] * PEER_N_KEYS + idx[:, :, 1, None, :]).reshape(PEER_BLOCK, PEER_HEADS, PEER_TOPK * PEER_TOPK)
        top_s, pos = lax.top_k(cand, PEER_TOPK)
        e = jnp.take_along_axis(cidx, pos, axis=-1)
        g = jax.nn.softmax(top_s, axis=-1)
        ue = jnp.take(u, e, axis=0)
        ve = jnp.take(v, e, axis=0)
        act = jax.nn.gelu(jnp.einsum('thkd,td->thk', ue, xb))
        return jnp.einsum('thk,thkd->td', (g * act).astype(ve.dtype), ve)

    return lax.map(one_block, tok).reshape(B_, T, D)

def setup_inputs(seed: int = 0) -> dict:
    key = jax.random.key(seed)
    ks = iter(jax.random.split(key, 48))

    def nrm(shape, scale):
        return jax.random.normal(next(ks), shape, f32) * scale

    def gain(shape):
        return 1.0 + nrm(shape, 0.05)

    D = D_MODEL
    x = nrm((BATCH, SEQ, D), 1.0)
    c = nrm((BATCH, D), 1.0)
    ctx = nrm((BATCH, CTX_LEN, D), 1.0)
    c_ctx = nrm((D,), 1.0)
    mod_w = nrm((DEPTH, D, N_MOD * D), 0.5 * D ** -0.5)
    mod_b = nrm((DEPTH, N_MOD * D), 0.02)
    norm_mix_g = gain((DEPTH, D))
    norm_ffn_g = gain((DEPTH, D))
    ev_w_in = nrm((N_EVEN, D, EVEN_IN), D ** -0.5)
    ev_w_out = nrm((N_EVEN, EVEN_MIX, D), EVEN_MIX ** -0.5)
    rg_conv_w = nrm((N_EVEN, CONV_W, RG_WIDTH), 0.5)
    rg_conv_b = nrm((N_EVEN, RG_WIDTH), 0.02)
    rg_wa = nrm((N_EVEN, 2, RG_HEADS, RG_HEAD_DIM, RG_HEAD_DIM), RG_HEAD_DIM ** -0.5)
    rg_ba = nrm((N_EVEN, 2, RG_WIDTH), 0.02)
    rg_wx = nrm((N_EVEN, 2, RG_HEADS, RG_HEAD_DIM, RG_HEAD_DIM), RG_HEAD_DIM ** -0.5)
    rg_bx = nrm((N_EVEN, 2, RG_WIDTH), 0.02)
    a8 = jax.random.uniform(next(ks), (N_EVEN, 2, RG_WIDTH), f32, 0.9, 0.999)
    a = a8 ** (1.0 / RG_C)
    rg_lam = jnp.log(a) - jnp.log1p(-a)
    fn_w = nrm((N_EVEN, FN_GROUPS, FN_GROUP_DIM, FN_GROUP_DIM), FN_GROUP_DIM ** -0.5)
    fn_b = nrm((N_EVEN, FN_WIDTH), 0.02)
    od_w_in = nrm((N_ODD, D, ODD_IN), D ** -0.5)
    od_w_out = nrm((N_ODD, ODD_MIX, D), ODD_MIX ** -0.5)
    ml_conv_w = nrm((N_ODD, CONV_W, 2 * ML_WIDTH), 0.5)
    ml_conv_b = nrm((N_ODD, 2 * ML_WIDTH), 0.02)
    f_bias = 3.0 + 3.0 * jax.random.uniform(next(ks), (N_ODD, 2, 1, ML_HEADS), f32)
    i_bias = nrm((N_ODD, 2, 1, ML_HEADS), 0.1)
    ml_gate_b = jnp.concatenate([i_bias, f_bias], axis=2).reshape(N_ODD, ML_N_GATES)
    ml_head_g = gain((N_ODD, ML_WIDTH))
    mla_q_norm_g = gain((N_ODD, MLA_Q_LORA))
    mla_w_uq = nrm((N_ODD, MLA_Q_LORA, MLA_HEADS * (MLA_NOPE + MLA_ROPE)), MLA_Q_LORA ** -0.5)
    mla_kv_norm_g = gain((N_ODD, MLA_KV_LORA))
    mla_w_ukv = nrm((N_ODD, MLA_KV_LORA, MLA_HEADS * (MLA_NOPE + MLA_V)), MLA_KV_LORA ** -0.5)
    peer_w_q = nrm((DEPTH, D, PEER_HEADS * PEER_KEY_DIM), D ** -0.5)
    peer_keys = nrm((DEPTH, 2, PEER_HEADS, PEER_N_KEYS, PEER_KEY_DIM // 2), (PEER_KEY_DIM // 2) ** -0.5)
    peer_u = nrm((DEPTH, PEER_N_EXPERTS, D), D ** -0.5)
    peer_v = nrm((DEPTH, PEER_N_EXPERTS, D), 0.5)
    final_g = gain((D,))
    return {"x": x, "c": c, "ctx": ctx, "c_ctx": c_ctx, "mod_w": mod_w, "mod_b": mod_b,
            "norm_mix_g": norm_mix_g, "norm_ffn_g": norm_ffn_g, "ev_w_in": ev_w_in, "ev_w_out": ev_w_out,
            "rg_conv_w": rg_conv_w, "rg_conv_b": rg_conv_b, "rg_wa": rg_wa, "rg_ba": rg_ba,
            "rg_wx": rg_wx, "rg_bx": rg_bx, "rg_lam": rg_lam, "fn_w": fn_w, "fn_b": fn_b,
            "od_w_in": od_w_in, "od_w_out": od_w_out, "ml_conv_w": ml_conv_w, "ml_conv_b": ml_conv_b,
            "ml_gate_b": ml_gate_b, "ml_head_g": ml_head_g, "mla_q_norm_g": mla_q_norm_g,
            "mla_w_uq": mla_w_uq, "mla_kv_norm_g": mla_kv_norm_g, "mla_w_ukv": mla_w_ukv,
            "peer_w_q": peer_w_q, "peer_keys": peer_keys, "peer_u": peer_u, "peer_v": peer_v,
            "final_g": final_g}

def reference(x, c, ctx, c_ctx, mod_w, mod_b, norm_mix_g, norm_ffn_g, ev_w_in, ev_w_out,
              rg_conv_w, rg_conv_b, rg_wa, rg_ba, rg_wx, rg_bx, rg_lam, fn_w, fn_b,
              od_w_in, od_w_out, ml_conv_w, ml_conv_b, ml_gate_b, ml_head_g, mla_q_norm_g,
              mla_w_uq, mla_kv_norm_g, mla_w_ukv, peer_w_q, peer_keys, peer_u, peer_v, final_g):
    T = x.shape[1]
    ROWS = T // GRID_W
    row = jnp.repeat(jnp.arange(ROWS, dtype=f32), GRID_W)
    col = jnp.tile(jnp.arange(GRID_W, dtype=f32), ROWS)
    cos, sin = axial_rope_angles(row, col)
    sc = jax.nn.silu(c)
    sctx = jax.nn.silu(c_ctx)
    h_lat, h_ctx = x, ctx
    for l in range(DEPTH):
        need_ctx = l < DEPTH - 1
        m_lat = jnp.split((sc @ mod_w[l] + mod_b[l])[:, None, :], N_MOD, axis=-1)
        m_ctx = jnp.split((sctx @ mod_w[l] + mod_b[l])[None, None, :], N_MOD, axis=-1)
        u_lat = modulate(rmsnorm(h_lat, norm_mix_g[l]), m_lat[0], m_lat[1])
        u_ctx = modulate(rmsnorm(h_ctx, norm_mix_g[l]), m_ctx[0], m_ctx[1])
        j = l // 2
        if l % 2 == 0:
            y_ctx, y_lat = even_mixer(u_ctx, u_lat, ev_w_in[j], ev_w_out[j], rg_conv_w[j], rg_conv_b[j],
                                      rg_wa[j], rg_ba[j], rg_wx[j], rg_bx[j], rg_lam[j], fn_w[j], fn_b[j], need_ctx)
        else:
            y_ctx, y_lat = odd_mixer(u_ctx, u_lat, od_w_in[j], od_w_out[j], ml_conv_w[j], ml_conv_b[j],
                                     ml_gate_b[j], ml_head_g[j], mla_q_norm_g[j], mla_w_uq[j],
                                     mla_kv_norm_g[j], mla_w_ukv[j], cos, sin, need_ctx)
        h_lat = h_lat + m_lat[2] * y_lat
        f_lat = modulate(rmsnorm(h_lat, norm_ffn_g[l]), m_lat[3], m_lat[4])
        h_lat = h_lat + m_lat[5] * peer_ffn(f_lat, peer_w_q[l], peer_keys[l], peer_u[l], peer_v[l])
        if need_ctx:
            h_ctx = h_ctx + m_ctx[2] * y_ctx
            f_ctx = modulate(rmsnorm(h_ctx, norm_ffn_g[l]), m_ctx[3], m_ctx[4])
            h_ctx = h_ctx + m_ctx[5] * peer_ffn(f_ctx, peer_w_q[l], peer_keys[l], peer_u[l], peer_v[l])
    return rmsnorm(h_lat, final_g)


_drawn_inputs = setup_inputs


def setup_inputs(seed=0):
    import zlib

    import numpy as np

    out = dict(_drawn_inputs(seed))
    spreads = {}
    factors = {'rg_ba': 8.0,
     'rg_bx': 7.412,
     'fn_b': 8.0,
     'ml_conv_b': 26.023,
     'ml_head_g': 19.48,
     'mla_q_norm_g': 8.0,
     'mla_w_uq': 2.754,
     'mla_kv_norm_g': 8.0}
    for name, (base, spread) in spreads.items():
        noise = np.random.default_rng([zlib.crc32(name.encode()), seed]).standard_normal(out[name].shape)
        drawn = base * np.exp(spread * noise) if base else spread * noise
        out[name] = __import__('jax').numpy.asarray(drawn.astype(out[name].dtype))
    for name, factor in factors.items():
        out[name] = (out[name] * factor).astype(out[name].dtype)
    return out
```

```python
import math
from contextlib import ExitStack

import concourse.bass as bass
import numpy as np
from concourse import mybir

ALU = mybir.AluOpType
ACT = mybir.ActivationFunctionType
F32 = mybir.dt.float32
I32 = mybir.dt.int32
U32 = mybir.dt.uint32
AX = mybir.AxisListType.X

P = 128
D = 1024
KT = D // P
SEG = 256
T = 2 * SEG
EPS = 1e-6
N_MOD = 6
CONV_W = 4
RG_H = 6
EV_J = 14
ML_H = 4
MLA_H = 8
NOPE, ROPE, VD = 64, 32, 64
QD = NOPE + ROPE
Q_LORA, KV_LORA = 384, 256
PH = 8
NK = 128
TOPK = 16
SLOTS = PH * TOPK
PIECE_J = 4
PIECES = 2 * N_MOD * KT // PIECE_J
MOD_RING = 3
U_RING, V_RING = 8, 4
LAG = 20
NEG = -3.0e38
GATE_ROWS = 100
HALF_ROWS = 36
GELU_C = 0.044715
GELU_S = math.sqrt(2.0 / math.pi)


def offsets(spec):
    out, at = {}, 0
    for name, *shape in spec:
        out[name] = (at, shape)
        at += math.prod(shape)
    return out, at


COLS, N_COLS = offsets([
    ("cond", KT, 2), ("mod_b", 2, N_MOD * KT), ("norm_g", 2, 2, KT), ("final_g", KT),
    ("rg_conv_w", RG_H, CONV_W), ("rg_conv_b", RG_H), ("rg_ba", 2, RG_H), ("rg_bx", 2, RG_H),
    ("rg_lam", 2, RG_H), ("fn_b", 2), ("ml_conv_w", 8, CONV_W), ("ml_conv_b", 8),
    ("ml_gate_b", 1), ("ml_head_g", ML_H), ("q_norm_g", Q_LORA // P), ("kv_norm_g", KV_LORA // P)])
CONSTS, N_CONSTS = offsets([
    ("ident", P), ("chan_dft", 2, P), ("time_dft", 2, 2, SEG), ("rope_cos", SEG),
    ("rope_sin", SEG), ("rope_swap", QD), ("causal", 2, 2, SEG), ("pick", 2 * ML_H, P),
    ("iota", TOPK)])
EVEN, N_EVEN = offsets([("rg_w", 2, 2, RG_H, P), ("fn_w", 2, 64)])
ODD_PARTS = [("q", 512), ("k", 512), ("v", 512), ("o", 512), ("cq", Q_LORA), ("ckv", KV_LORA),
             ("krope", QD), ("gates", GATE_ROWS)]


def field(tensor, table, name):
    at, shape = table[name]
    ap = tensor[:, at:at + math.prod(shape)]
    if len(shape) > 1:
        names = "abcd"[:len(shape)]
        ap = ap.rearrange(f"p ({' '.join(names)}) -> p {' '.join(names)}",
                          **{n: s for n, s in zip(names, shape)})
    return ap


class Steps:

    def __init__(self, engine, semaphore):
        self.engine, self.semaphore, self.n, self.base = engine, semaphore, 0, 0

    def __call__(self, instruction):
        self.n += 1
        instruction.then_inc(self.semaphore, 1)
        self.engine.wait_ge(self.semaphore, self.base + self.n)


class Norm:

    def __init__(self, name, sem, src, squares, bank, work, out, tokens, blocks, eps_of=None):
        self.src, self.squares, self.bank, self.work, self.out = src, squares, bank, work, out
        self.tokens, self.blocks = tokens, blocks
        self.squared = sem(f"{name}_squared")
        self.summed = sem(f"{name}_summed")
        self.mean = sem(f"{name}_mean")
        self.root = sem(f"{name}_root")
        self.scaled = sem(f"{name}_scaled")
        self.ready = sem(f"{name}_ready")

    def act_squares(self, act):
        for d in range(self.blocks):
            if d >= 2:
                act.wait_ge(self.summed, d - 1)
            act.activation(self.squares[:, d % 2, 0:self.tokens], self.src(d),
                           ACT.Square).then_inc(self.squared, 1)

    def pe_sums(self, pe, ones):
        for d in range(self.blocks):
            pe.wait_ge(self.squared, d + 1)
            pe.matmul(self.bank, ones, self.squares[:, d % 2, 0:self.tokens], start=(d == 0),
                      stop=(d == self.blocks - 1)).then_inc(self.summed, 1)

    def dve_mean(self, dve):
        dve.wait_ge(self.summed, self.blocks)
        dve.tensor_scalar(self.work, self.bank, 1.0 / (self.blocks * P), EPS, ALU.mult,
                          ALU.add).then_inc(self.mean, 1)

    def act_root(self, act):
        act.wait_ge(self.mean, 1)
        act.activation(self.work, self.work, ACT.Sqrt).then_inc(self.root, 1)

    def dve_scale(self, dve, steps):
        dve.wait_ge(self.root, 1)
        steps(dve.reciprocal(self.work, self.work))
        for d in range(self.blocks):
            dve.tensor_tensor(self.out(d), self.src(d), self.work, ALU.mult).then_inc(self.scaled, 1)

    def act_affine(self, act, parts, scale, shift):
        for d in range(self.blocks):
            act.wait_ge(self.scaled, d + 1)
            for n, part in enumerate(parts):
                at = self.out(d)[:, part]
                if shift is None:
                    last = act.activation(at, at, ACT.Copy, scale=scale(d, n))
                else:
                    last = act.activation(at, at, ACT.Identity, scale=scale(d, n), bias=shift(d, n))
            last.then_inc(self.ready, 1)


def softplus_tail(dve, steps, e, z, z2, p):
    steps(dve.tensor_scalar(z, e, 2.0, None, ALU.add))
    steps(dve.reciprocal(z, z))
    steps(dve.tensor_tensor(z, z, e, ALU.mult))
    steps(dve.tensor_tensor(z2, z, z, ALU.mult))
    steps(dve.tensor_scalar(p, z2, 1.0 / 17.0, None, ALU.mult))
    for k in (15, 13, 11, 9, 7, 5, 3):
        steps(dve.scalar_tensor_tensor(out=p, in0=p, scalar=1.0 / k, in1=z2, op0=ALU.add, op1=ALU.mult))
    steps(dve.scalar_tensor_tensor(out=p, in0=p, scalar=1.0, in1=z, op0=ALU.add, op1=ALU.mult))
    steps(dve.tensor_scalar(p, p, 2.0, None, ALU.mult))


def backbone(nc, hT0, cols_in, consts_in, mod_w, ev_in, ev_out, even_in, od, w_uq,
             w_uk, w_uv, od_out, peer_q, peer_keys, peer_u, peer_v, out):
    with ExitStack() as ctx:
        def sb(name, shape, dt=F32):
            return ctx.enter_context(nc.sbuf_tensor(name, shape, dt))

        phase_sems = []

        def sem(name):
            phase_sems.append(nc.alloc_semaphore(name=name))
            return phase_sems[-1]

        def end_phase():
            nc.clear_and_free_semaphores(phase_sems)
            nc.all_engine_barrier()
            phase_sems.clear()

        ps = ctx.enter_context(nc.psum_tensor("banks", [P, 8, 512], F32))

        hT = sb("hT", [P, KT, T])
        uT = sb("uT", [P, KT, T])
        cols = sb("cols", [P, N_COLS])
        consts = sb("consts", [P, N_CONSTS])
        ones = sb("ones", [P, P])
        modc = sb("modc", [P, 2, N_MOD, KT, 2])
        gain = sb("gain", [P, 2, 2, KT, 2])
        squares = sb("squares", [P, 2, T])
        rms = sb("rms", [P, T])

        def col(name):
            return field(cols, COLS, name)

        def const(name):
            return field(consts, CONSTS, name)

        ident = const("ident")
        loaded = sem("tables_loaded")
        ones_set = sem("ones_set")
        mod_steps = sem("mod_steps")
        dve_steps = sem("even_dve_steps")
        act_steps = sem("even_act_steps")

        even_stack = ExitStack()

        def esb(name, shape):
            return even_stack.enter_context(nc.sbuf_tensor(name, shape, F32))

        w_in = esb("ev_w_in", [P, 7, KT, 2 * P])
        w_out = esb("ev_w_out", [P, KT, D])
        even_w = esb("even_w", [P, N_EVEN])
        silu = esb("silu", [P, KT, 2])
        early = esb("early", [P, MOD_RING * KT * PIECE_J * P])

        def view(base, at, *shape):
            n = math.prod(shape)
            names = "abcd"[:len(shape)]
            return base[:, at:at + n].rearrange(
                f"p ({' '.join(names)}) -> p {' '.join(names)}",
                **{x: s for x, s in zip(names, shape)}), at + n

        mod_ring, _ = view(early, 0, MOD_RING, KT, PIECE_J * P)
        at = 0
        xpad, at = view(early, at, RG_H, 2, SEG + CONV_W - 1)
        h_fwd, _ = view(early, 0, RG_H, T)
        xc, at = view(early, at, RG_H, T)
        gate, at = view(early, at, RG_H, T)
        xf, at = view(early, at, 2, T)
        dft_w, at = view(early, at, 2, 2, P)
        sp, at = view(early, at, 8, 2 * RG_H)
        half_b, at = view(early, at, 2, 2 * RG_H)
        w_in_flat = w_in[:, :, :, :].rearrange("p a b c -> p (a b c)")
        at = 0
        decay_t, at = view(w_in_flat, at, RG_H, T)
        drive, at = view(w_in_flat, at, RG_H, T)
        root_t, at = view(w_in_flat, at, RG_H, T)
        decay, at = view(w_in_flat, at, RG_H, T)
        xw, at = view(w_in_flat, at, 4, 2, 2 * P)
        mixT = uT

        piece_loaded = [sem(f"mod_piece_loaded{r}") for r in range(MOD_RING)]
        piece_used = sem("mod_piece_used")
        w_in_loaded = [sem(f"ev_w_in_loaded{c}") for c in range(7)]
        w_out_loaded = sem("ev_w_out_loaded")
        cond_tanh = sem("cond_tanh")
        silu_ready = sem("silu_ready")
        mod_ready = sem("mod_ready")

        mod_ps = ps[:, 7, 0:2 * N_MOD * KT * 2]

        with nc.Block() as block:
            @block.sync
            def _(sp_eng):
                sp_eng.dma_start(cols[:], cols_in).then_inc(loaded, 16)
                for r in range(MOD_RING):
                    sp_eng.dma_start(mod_ring[:, r], mod_w[r]).then_inc(piece_loaded[r], 16)
                sp_eng.dma_start(hT[:], hT0).then_inc(loaded, 16)
                sp_eng.dma_start(consts[:], consts_in).then_inc(loaded, 16)
                sp_eng.dma_start(even_w[:], even_in).then_inc(loaded, 16)
                for c in range(7):
                    sp_eng.dma_start(w_in[:, c], ev_in[c]).then_inc(w_in_loaded[c], 16)
                sp_eng.dma_start(w_out[:], ev_out).then_inc(w_out_loaded, 16)
                with sp_eng.Fori(1, PIECES // MOD_RING) as it:
                    for r in range(MOD_RING):
                        sp_eng.wait_ge(piece_used, it * MOD_RING + (r + 1 - MOD_RING))
                        sp_eng.dma_start(
                            mod_ring[:, r],
                            mod_w[bass.ds(it * MOD_RING + r, 1)].rearrange("o p a b -> p (o a) b")
                        ).then_inc(piece_loaded[r], 16)

            @block.scalar
            def _(act):
                act.wait_ge(loaded, 64)
                act.activation(silu[:], col("cond"), ACT.Tanh, scale=0.5).then_inc(cond_tanh, 1)

            @block.vector
            def _(dve):
                steps = Steps(dve, mod_steps)
                dve.memset(ones[:], 1.0).then_inc(ones_set, 1)
                dve.wait_ge(cond_tanh, 1)
                steps(dve.scalar_tensor_tensor(out=silu[:], in0=silu[:], scalar=1.0, in1=col("cond"),
                                               op0=ALU.add, op1=ALU.mult))
                dve.tensor_scalar(silu[:], silu[:], 0.5, None, ALU.mult).then_inc(silu_ready, 1)
                dve.wait_ge(piece_used, PIECES)
                m = modc[:].rearrange("p l w k s -> p (l w k) s")
                steps(dve.tensor_tensor(
                    m, mod_ps.rearrange("p (a s) -> p a s", s=2),
                    col("mod_b").rearrange("p l a -> p (l a)").unsqueeze(2).to_broadcast([P, 2 * N_MOD * KT, 2]),
                    ALU.add))
                for l in range(2):
                    for half in range(2):
                        last = dve.scalar_tensor_tensor(
                            out=gain[:, l, half], in0=modc[:, l, 3 * half + 1], scalar=1.0,
                            in1=col("norm_g")[:, l, half].unsqueeze(2).to_broadcast([P, KT, 2]),
                            op0=ALU.add, op1=ALU.mult)
                        last.then_inc(mod_ready, 1)

            @block.tensor
            def _(pe):
                pe.wait_ge(silu_ready, 1)
                with pe.Fori(0, PIECES // MOD_RING) as it:
                    for r in range(MOD_RING):
                        pe.wait_ge(piece_loaded[r], it * 16 + 16)
                        for jj in range(PIECE_J):
                            to = mod_ps[:, bass.ds((it * MOD_RING + r) * (2 * PIECE_J) + 2 * jj, 2)]
                            for k in range(KT):
                                last = pe.matmul(to, mod_ring[:, r, k, jj * P:(jj + 1) * P],
                                                 silu[:, k], start=(k == 0), stop=(k == KT - 1))
                        last.then_inc(piece_used, 1)
                pe.wait_ge(mod_ready, 4)

        mix0 = Norm("mix0", sem, lambda d: hT[:, d, :], squares, ps[:, 0, :], rms[:],
                    lambda d: uT[:, d, :], T, KT)
        projected = sem("even_projected")
        taken = sem("even_taken")
        pads_set = sem("even_pads_set")
        xc_ready = sem("xc_ready")
        lam_exp = sem("lam_exp")
        lam_abs = sem("lam_abs")
        sp_ready = sem("softplus_ready")
        gate_product = sem("gate_product")
        gate_taken = sem("gate_taken")
        roots = sem("rg_roots")
        direction_done = sem("rg_direction_done")
        fourier_product = sem("fourier_product")
        dft_w_ready = sem("dft_w_ready")
        xw_ready = sem("xw_ready")
        y_four_ready = sem("fourier_out_ready")
        mix_ready = sem("rg_mix_ready")
        even_out = sem("even_out_product")
        even_added = sem("even_added")
        segs = [slice(0, SEG), slice(SEG, T)]
        BANK = [1, 2, 3, 4]

        with nc.Block() as block:
            @block.scalar
            def _(act):
                steps = Steps(act, act_steps)
                mix0.act_squares(act)
                mix0.act_root(act)
                mix0.act_affine(act, segs, lambda d, s: gain[:, 0, 0, d, s:s + 1],
                                lambda d, s: modc[:, 0, 0, d, s:s + 1])
                act.wait_ge(lam_abs, 1)
                act.activation(sp[:, 1], sp[:, 1], ACT.Exp, scale=-1.0).then_inc(lam_exp, 1)
                act.wait_ge(pads_set, 1)
                for j in range(EV_J):
                    act.wait_ge(projected, j + 1)
                    bank = ps[:, BANK[j % 4], :]
                    if j < RG_H:
                        last = act.activation(xpad[:, j, :, 2:2 + SEG],
                                              bank.rearrange("p (s t) -> p s t", s=2), ACT.Copy)
                    elif j < 2 * RG_H:
                        last = act.activation(gate[:, j - RG_H], bank, ACT.Gelu_apprx_tanh)
                    else:
                        last = act.activation(xf[:, j - 2 * RG_H], bank, ACT.Copy)
                    last.then_inc(taken, 1)
                act.wait_ge(sp_ready, 1)

                def gates(d):
                    for n in range(2 * RG_H):
                        h, kind = n // 2, n % 2
                        act.wait_ge(gate_product, 2 * RG_H * d + n + 1)
                        bank = ps[:, BANK[n % 4], :]
                        i = RG_H * d + h
                        if kind == 0:
                            act.activation(decay_t[:, h], bank, ACT.Tanh, scale=0.5,
                                           bias=half_b[:, 0, i:i + 1]).then_inc(gate_taken, 1)
                            act.wait_ge(gate_taken, 2 * RG_H * d + n + 1)
                            steps(act.activation(decay_t[:, h], decay_t[:, h], ACT.Tanh,
                                                 scale=sp[:, 7, i:i + 1], bias=sp[:, 7, i:i + 1]))
                        else:
                            act.activation(drive[:, h], bank, ACT.Tanh, scale=0.5,
                                           bias=half_b[:, 1, i:i + 1]).then_inc(gate_taken, 1)
                    act.activation(root_t, decay_t, ACT.Sqrt).then_inc(roots, 1)

                gates(0)
                for n in range(8):
                    act.wait_ge(fourier_product, 2 + n)
                    act.activation(xw[:, n % 4, n // 4], ps[:, 5 + n % 2, 0:2 * P],
                                   ACT.Copy).then_inc(xw_ready, 1)
                for n in range(4):
                    j, s = n // 2, n % 2
                    act.wait_ge(fourier_product, 10 + n)
                    act.activation(mixT[:, RG_H + j, segs[s]], ps[:, 5 + n % 2, 0:SEG], ACT.Identity,
                                   bias=col("fn_b")[:, j:j + 1]).then_inc(y_four_ready, 1)
                act.wait_ge(direction_done, 1)
                gates(1)

            @block.vector
            def _(dve):
                steps = Steps(dve, dve_steps)
                lam = col("rg_lam").rearrange("p d h -> p (d h)")
                steps(dve.tensor_scalar(sp[:, 0], lam, -1.0, 0.0, ALU.mult, ALU.max))
                dve.scalar_tensor_tensor(out=sp[:, 1], in0=lam, scalar=-1.0, in1=lam, op0=ALU.mult,
                                         op1=ALU.max).then_inc(lam_abs, 1)
                for n, b in enumerate(("rg_ba", "rg_bx")):
                    steps(dve.tensor_scalar(half_b[:, n], col(b).rearrange("p d h -> p (d h)"), 0.5,
                                            None, ALU.mult))
                steps(dve.memset(xpad[:, :, :, 0:2], 0.0))
                steps(dve.memset(dft_w[:], 0.0))
                dve.memset(xpad[:, :, :, 2 + SEG:], 0.0).then_inc(pads_set, 1)
                mix0.dve_mean(dve)
                mix0.dve_scale(dve, steps)
                dve.wait_ge(lam_exp, 1)
                softplus_tail(dve, steps, sp[:, 1], sp[:, 2], sp[:, 3], sp[:, 4])
                steps(dve.tensor_tensor(sp[:, 4], sp[:, 4], sp[:, 0], ALU.add))
                dve.tensor_scalar(sp[:, 7], sp[:, 4], 2.0, None, ALU.mult).then_inc(sp_ready, 1)
                dve.wait_ge(pads_set, 1)
                w = col("rg_conv_w")
                for h in range(RG_H):
                    dve.wait_ge(taken, h + 1)
                    at = xc[:, h].rearrange("p (s t) -> p s t", s=2)
                    steps(dve.tensor_scalar(at, xpad[:, h, :, 0:SEG], w[:, h, 0:1],
                                            col("rg_conv_b")[:, h:h + 1], ALU.mult, ALU.add))
                    for i in range(1, CONV_W):
                        last = dve.scalar_tensor_tensor(out=at, in0=xpad[:, h, :, i:i + SEG],
                                                        scalar=w[:, h, i:i + 1], in1=at, op0=ALU.mult,
                                                        op1=ALU.add)
                        if i < CONV_W - 1:
                            steps(last)
                    last.then_inc(xc_ready, 1)
                dve.wait_ge(fourier_product, 1)
                small = ps[:, 5, 0:256].rearrange("p (j m e) -> p j m e", j=2, m=2)
                for g in range(2):
                    rows = slice(64 * g, 64 * g + 64)
                    dve.tensor_copy(dft_w[rows, :, :, 64 * g:64 * g + 64], small[rows]).then_inc(dft_w_ready, 1)

                def direction(d):
                    xc_all, out_h = xc[:], (h_fwd if d == 0 else root_t)
                    dve.wait_ge(gate_taken, 2 * RG_H * (d + 1))
                    steps(dve.scalar_tensor_tensor(out=drive, in0=drive, scalar=1.0, in1=xc_all,
                                                   op0=ALU.add, op1=ALU.mult))
                    dve.wait_ge(roots, d + 1)
                    steps(dve.tensor_scalar(decay, decay_t, 1.0, None, ALU.add))
                    steps(dve.reciprocal(decay, decay))
                    steps(dve.tensor_tensor(drive, drive, root_t, ALU.mult))
                    steps(dve.tensor_tensor(drive, drive, decay, ALU.mult))
                    steps(dve.tensor_scalar(decay, decay, 2.0, -1.0, ALU.mult, ALU.add))
                    for h in range(RG_H):
                        if d == 0:
                            steps(dve.tensor_tensor_scan(out=out_h[:, h], data0=decay[:, h],
                                                         data1=drive[:, h], initial=0.0,
                                                         op0=ALU.mult, op1=ALU.add))
                        else:
                            for s, first in ((0, 0.0), (1, out_h[:, h, 0:1])):
                                steps(dve.tensor_tensor_scan(
                                    out=out_h[:, h, segs[s]][:, ::-1], data0=decay[:, h, segs[s]][:, ::-1],
                                    data1=drive[:, h, segs[s]][:, ::-1], initial=first,
                                    op0=ALU.mult, op1=ALU.add))

                direction(0)
                dve.memset(sp[:, 5], 0.0).then_inc(direction_done, 1)
                direction(1)
                for h in range(RG_H):
                    steps(dve.tensor_tensor(root_t[:, h], root_t[:, h], h_fwd[:, h], ALU.add))
                    dve.tensor_tensor(mixT[:, h], root_t[:, h], gate[:, h], ALU.mult).then_inc(mix_ready, 1)
                for n in range(KT):
                    dve.wait_ge(even_out, n + 1)
                    for s in range(2):
                        last = dve.scalar_tensor_tensor(
                            out=hT[:, n, segs[s]], in0=ps[:, BANK[n % 4], segs[s]],
                            scalar=modc[:, 0, 2, n, s:s + 1], in1=hT[:, n, segs[s]], op0=ALU.mult,
                            op1=ALU.add)
                    last.then_inc(even_added, 1)

            @block.tensor
            def _(pe):
                pe.wait_ge(ones_set, 1)
                mix0.pe_sums(pe, ones[:])
                for j in range(EV_J):
                    if j % 2 == 0:
                        pe.wait_ge(w_in_loaded[j // 2], 16)
                    if j >= 4:
                        pe.wait_ge(taken, j - 3)
                    for k in range(KT):
                        if j == 0:
                            pe.wait_ge(mix0.ready, k + 1)
                        last = pe.matmul(ps[:, BANK[j % 4], :], w_in[:, j // 2, k, j % 2 * P:j % 2 * P + P],
                                         uT[:, k], start=(k == 0), stop=(k == KT - 1))
                    last.then_inc(projected, 1)
                for j in range(2):
                    for m in range(2):
                        last = pe.matmul(ps[:, 5, (2 * j + m) * 64:(2 * j + m) * 64 + 64],
                                         const("chan_dft")[:, m], field(even_w, EVEN, "fn_w")[:, j],
                                         start=True, stop=True)
                last.then_inc(fourier_product, 1)
                rg_w = field(even_w, EVEN, "rg_w")

                def gates(d):
                    for n in range(2 * RG_H):
                        h, kind = n // 2, n % 2
                        if n >= 4 or d == 1:
                            pe.wait_ge(gate_taken, 2 * RG_H * d + n - 3)
                        pe.matmul(ps[:, BANK[n % 4], :], rg_w[:, kind, d, h], xc[:, h], start=True,
                                  stop=True).then_inc(gate_product, 1)

                pe.wait_ge(taken, EV_J)
                pe.wait_ge(xc_ready, RG_H)
                gates(0)
                pe.wait_ge(dft_w_ready, 2)
                for n in range(8):
                    j, tt = n // 4, n % 4
                    if n >= 2:
                        pe.wait_ge(xw_ready, n - 1)
                    pe.matmul(ps[:, 5 + n % 2, 0:2 * P], xf[:, j, tt * P:(tt + 1) * P],
                              dft_w[:, j].rearrange("p m e -> p (m e)"), start=True,
                              stop=True).then_inc(fourier_product, 1)
                pe.wait_ge(xw_ready, 8)
                for n in range(4):
                    j, s = n // 2, n % 2
                    if n >= 2:
                        pe.wait_ge(y_four_ready, n - 1)
                    for tl in range(2):
                        for m in range(2):
                            last = pe.matmul(ps[:, 5 + n % 2, 0:SEG], xw[:, 2 * s + tl, j, m * P:(m + 1) * P],
                                             const("time_dft")[:, m, tl], start=(tl + m == 0),
                                             stop=(tl + m == 2))
                    last.then_inc(fourier_product, 1)
                gates(1)
                pe.wait_ge(gate_taken, 4 * RG_H)
                pe.wait_ge(w_out_loaded, 16)
                pe.wait_ge(y_four_ready, 4)
                pe.wait_ge(mix_ready, RG_H)
                for n in range(KT):
                    if n >= 4:
                        pe.wait_ge(even_added, n - 3)
                    for k in range(KT):
                        last = pe.matmul(ps[:, BANK[n % 4], :], w_out[:, k, n * P:(n + 1) * P], mixT[:, k],
                                         start=(k == 0), stop=(k == KT - 1))
                    last.then_inc(even_out, 1)
        even_stack.close()
        end_phase()

        def peer(layer, first_token, tiles):
            name = f"peer{layer}"
            stack = ExitStack()

            def psb(what, shape, dt=F32):
                return stack.enter_context(nc.sbuf_tensor(f"{name}_{what}", shape, dt))

            def psem(what):
                return sem(f"{name}_{what}")

            segments = segs if first_token == 0 else [slice(0, SEG)]
            seg_of = 0 if first_token == 0 else 1
            n_tokens = tiles * P
            w_q = psb("w_q", [P, 4, KT, 4 * P])
            keys = psb("keys", [P, PH, 2, NK])
            u_rows = psb("u_rows", [P, U_RING, D])
            v_rows = psb("v_rows", [P, V_RING, D])
            diag = psb("diag", [P, TOPK, P])
            xs = psb("xs", [P, KT, P])
            q_sb = psb("q", [P, 2, P])
            scores = psb("scores", [P, PH, 2, NK])
            vals = psb("vals", [P, 2, TOPK])
            ids = psb("ids", [P, 2, TOPK], U32)
            ids_f = psb("ids_f", [P, 2, TOPK])
            sums = psb("sums", [P, TOPK, TOPK])
            top = psb("top", [P, TOPK])
            pos = psb("pos", [P, TOPK], U32)
            pair = psb("pair", [P, 2, TOPK], U32)
            pair_f = psb("pair_f", [P, 2, TOPK])
            hot = psb("hot", [P, 2, TOPK, TOPK])
            picked = psb("picked", [P, 2, TOPK])
            expert = psb("expert", [P, PH, TOPK], I32)
            soft = psb("soft", [P, TOPK + 4])
            g_half = psb("g_half", [P, PH, TOPK])
            dot = psb("dot", [P, TOPK])
            gelu_t = psb("gelu_t", [P, 2, TOPK])
            xg = psb("xg", [P, TOPK])
            weight = psb("weight", [P, PH, TOPK])

            w_q_loaded = [psem(f"w_q_loaded{c}") for c in range(4)]
            keys_loaded = psem("keys_loaded")
            u_landed = [psem(f"u_landed{r}") for r in range(U_RING)]
            v_landed = [psem(f"v_landed{r}") for r in range(V_RING)]
            turn = psem("turn")
            pause = psem("pause")
            own = psem("choice_steps")
            dve_steps = psem("dve_steps")
            staged = psem("staged")
            q_product, q_taken = psem("q_product"), psem("q_taken")
            s_product, s_taken = psem("s_product"), psem("s_taken")
            scores_used = psem("scores_used")
            soft_in, soft_out = psem("soft_in"), psem("soft_out")
            expert_ready = psem("expert_ready")
            dots_done = psem("dots_done")
            gelu_in, gelu_out = psem("gelu_in"), psem("gelu_out")
            weight_ready = psem("weight_ready")
            diag_ready = psem("diag_ready")
            v_added = psem("v_added")
            f_ready = psem("f_ready")
            sum_taken = psem("sum_taken")
            y_turned = psem("y_turned")
            y_added = psem("y_added")

            f_tok = ps[:, 0:2, :].rearrange("p a b -> p (a b)")
            acc = ps[:, 2:4, :]
            q_ps, s_ps = ps[:, 4, 0:2 * P], ps[:, 5, 0:2 * NK]
            norm = Norm(f"{name}_norm", sem, lambda d: hT[:, d, first_token:first_token + n_tokens],
                        squares, ps[:, 6, 0:n_tokens], rms[:, 0:n_tokens],
                        lambda d: uT[:, d, first_token:first_token + n_tokens], n_tokens, KT)

            def tokens_of(t):
                return bass.ds(t * P + first_token, P)

            with nc.Block() as block:
                @block.sync
                def _(sp_eng):
                    for c in range(4):
                        sp_eng.dma_start(w_q[:, c], peer_q[layer, c]).then_inc(w_q_loaded[c], 16)
                        if c == 0:
                            sp_eng.dma_start(keys[:], peer_keys[layer]).then_inc(keys_loaded, 16)

                @block.gpsimd
                def _(pool):
                    def gather_u(t, s):
                        if s % TOPK == 0:
                            pool.wait_ge(expert_ready, t * PH + (s // TOPK + 1))
                            pool.sem_inc(turn, 1)
                        pool.wait_ge(dots_done, t * SLOTS + (s + 1))
                        pool.sem_inc(turn, 1)
                        pool.indirect_dma_start(
                            out=u_rows[:, s % U_RING, :], out_offset=None, in_=peer_u[layer],
                            in_offset=bass.IndirectOffsetOnAxis(
                                ap=expert[:, s // TOPK, s % TOPK:s % TOPK + 1], axis=0)
                        ).then_inc(u_landed[s % U_RING], 16)

                    def gather_v(t, s):
                        pool.wait_ge(v_added, t * SLOTS + (s + 1 + SLOTS - V_RING))
                        pool.sem_inc(turn, 1)
                        pool.indirect_dma_start(
                            out=v_rows[:, s % V_RING, :], out_offset=None, in_=peer_v[layer],
                            in_offset=bass.IndirectOffsetOnAxis(
                                ap=expert[:, s // TOPK, s % TOPK:s % TOPK + 1], axis=0)
                        ).then_inc(v_landed[s % V_RING], 16)

                    def tile(t, more):
                        for s in range(SLOTS):
                            if s + LAG < SLOTS:
                                gather_u(t, s + LAG)
                            elif more:
                                gather_u(t + 1, s + LAG - SLOTS)
                            gather_v(t, s)

                    for s in range(LAG):
                        gather_u(0, s)
                    with pool.Fori(0, tiles - 1) as t:
                        tile(t, True)
                    tile(tiles - 1, False)

                @block.scalar
                def _(act):
                    norm.act_squares(act)
                    norm.act_root(act)
                    norm.act_affine(act, segments,
                                    lambda d, s: gain[:, layer, 1, d, s + seg_of:s + seg_of + 1],
                                    lambda d, s: modc[:, layer, 3, d, s + seg_of:s + seg_of + 1])

                    def stage(t):
                        act.activation(xs[:], uT[:, :, tokens_of(t)], ACT.Copy).then_inc(staged, 1)

                    def take_q(n):
                        act.wait_ge(q_product, n + 1)
                        act.activation(q_sb[:].rearrange("p a b -> p (a b)"), q_ps, ACT.Copy).then_inc(q_taken, 1)

                    def take_scores(n, h):
                        act.wait_ge(scores_used, n + 1)
                        act.wait_ge(s_product, n + 1)
                        act.activation(scores[:, h].rearrange("p a b -> p (a b)"), s_ps, ACT.Copy).then_inc(s_taken, 1)

                    def soften(n):
                        act.wait_ge(soft_in, n + 1)
                        act.activation(soft[:, 0:TOPK], top[:], ACT.Exp, bias=soft[:, TOPK:TOPK + 1],
                                       accum_out=soft[:, TOPK + 1:TOPK + 2]).then_inc(soft_out, 1)

                    def tile(t, more):
                        for j in range(PH):
                            if j == 5 and more:
                                act.wait_ge(q_product, t * PH + PH)
                                act.wait_ge(f_ready, t + 1)
                                stage(t + 1)
                            act.wait_ge(gelu_in, t * PH + (j + 1))
                            act.activation(gelu_t[:, 1], gelu_t[:, 0], ACT.Tanh, scale=GELU_S).then_inc(gelu_out, 1)
                            for k in range(TOPK):
                                s = j * TOPK + k
                                if k == 0:
                                    act.wait_ge(weight_ready, t * PH + (j + 1))
                                if k == 3 and (j < 5 or more):
                                    take_q(t * PH + (j + 3))
                                if k == 4 and (j < 6 or more):
                                    soften(t * PH + (j + 2))
                                if k == 6 and (j < 5 or more):
                                    take_scores(t * PH + (j + 3), (j + 3) % PH)
                                act.wait_ge(v_added, t * SLOTS + (s + 1 + SLOTS - TOPK))
                                act.activation(diag[:, k], ident, ACT.Copy,
                                               scale=weight[:, j, k:k + 1]).then_inc(diag_ready, 1)
                        act.wait_ge(v_added, t * SLOTS + 2 * SLOTS)
                        at = uT[:, :, tokens_of(t)]
                        for half in range(2):
                            last = act.activation(at[:, 4 * half:4 * half + 4, :],
                                                  acc[:, half].rearrange("p (a b) -> p a b", a=4), ACT.Copy)
                        last.then_inc(sum_taken, 1)

                    act.wait_ge(norm.ready, KT)
                    stage(0)
                    for n in range(3):
                        take_q(n)
                        take_scores(n, n)
                        if n > 0:
                            soften(n - 1)
                    with act.Fori(0, tiles - 1) as t:
                        tile(t, True)
                    tile(tiles - 1, False)

                @block.vector
                def _(dve):
                    steps = Steps(dve, dve_steps)
                    dve.sem_inc(dots_done, U_RING)
                    dve.sem_inc(scores_used, PH)
                    norm.dve_mean(dve)
                    norm.dve_scale(dve, steps)

                    def top16(chain, src, values, indices):
                        chain(dve.max(values[:, 0:8], src))
                        chain(dve.max_index(indices[:, 0:8], values[:, 0:8], src))
                        chain(dve.match_replace(src, values[:, 0:8], src, NEG))
                        chain(dve.max(values[:, 8:16], src))
                        return dve.max_index(indices[:, 8:16], values[:, 8:16], src)

                    def choose(chain, n, h):
                        dve.wait_ge(s_taken, n + 1)
                        dve.wait_ge(v_added, n * TOPK + (TOPK + SLOTS - SLOTS))
                        dve.sem_inc(pause, 1)
                        chain(top16(chain, scores[:, h, 0], vals[:, 0], ids[:, 0]))
                        top16(chain, scores[:, h, 1], vals[:, 1], ids[:, 1]).then_inc(scores_used, 1)
                        dve.wait_ge(scores_used, n + (PH + 1))
                        chain(dve.tensor_tensor(
                            sums[:], vals[:, 0].unsqueeze(2).to_broadcast([P, TOPK, TOPK]),
                            vals[:, 1].unsqueeze(1).to_broadcast([P, TOPK, TOPK]), ALU.add))
                        chain(top16(chain, sums[:].rearrange("p a b -> p (a b)"), top[:], pos[:]))
                        dve.tensor_scalar(soft[:, TOPK:TOPK + 1], top[:, 0:1], -1.0, None,
                                          ALU.mult).then_inc(soft_in, 1)
                        chain(dve.tensor_single_scalar(pair[:, 0], pos[:], 4, ALU.logical_shift_right))
                        chain(dve.tensor_single_scalar(pair[:, 1], pos[:], TOPK - 1, ALU.bitwise_and))
                        chain(dve.tensor_copy(pair_f[:], pair[:]))
                        chain(dve.tensor_copy(ids_f[:], ids[:]))
                        full = [P, 2, TOPK, TOPK]
                        chain(dve.tensor_tensor(
                            hot[:], pair_f[:].unsqueeze(3).to_broadcast(full),
                            const("iota").unsqueeze(1).unsqueeze(1).to_broadcast(full), ALU.is_equal))
                        chain(dve.tensor_tensor(hot[:], hot[:], ids_f[:].unsqueeze(2).to_broadcast(full), ALU.mult))
                        chain(dve.tensor_reduce(picked[:], hot[:], AX, ALU.add))
                        dve.scalar_tensor_tensor(out=expert[:, h], in0=picked[:, 0], scalar=float(NK),
                                                 in1=picked[:, 1], op0=ALU.mult,
                                                 op1=ALU.add).then_inc(expert_ready, 1)
                        dve.wait_ge(soft_out, n + 1)
                        chain(dve.reciprocal(soft[:, TOPK + 2:TOPK + 3], soft[:, TOPK + 1:TOPK + 2]))
                        chain(dve.tensor_scalar(g_half[:, h], soft[:, 0:TOPK], soft[:, TOPK + 2:TOPK + 3],
                                                0.5, ALU.mult, ALU.mult))

                    def tile(chain, t, more):
                        for j in range(PH):
                            if j == 0:
                                dve.wait_ge(f_ready, t + 1)
                            for k in range(TOPK):
                                s = j * TOPK + k
                                r = s % U_RING
                                dve.wait_ge(u_landed[r], t * (16 * SLOTS // U_RING) + 16 * (s // U_RING + 1))
                                dve.tensor_tensor_reduce(
                                    out=u_rows[:, r], in0=u_rows[:, r], in1=f_tok, scale=1.0, scalar=0.0,
                                    op0=ALU.mult, op1=ALU.add, accum_out=dot[:, k:k + 1]).then_inc(dots_done, 1)
                            dve.wait_ge(dots_done, t * SLOTS + ((j + 1) * TOPK + U_RING))
                            chain(dve.tensor_tensor(gelu_t[:, 0], dot[:], dot[:], ALU.mult))
                            chain(dve.tensor_scalar(gelu_t[:, 0], gelu_t[:, 0], GELU_C, 1.0, ALU.mult, ALU.add))
                            dve.tensor_tensor(gelu_t[:, 0], gelu_t[:, 0], dot[:], ALU.mult).then_inc(gelu_in, 1)
                            chain(dve.tensor_tensor(xg[:], dot[:], g_half[:, j], ALU.mult))
                            dve.wait_ge(gelu_out, t * PH + (j + 1))
                            dve.scalar_tensor_tensor(out=weight[:, j], in0=gelu_t[:, 1], scalar=1.0, in1=xg[:],
                                                     op0=ALU.add, op1=ALU.mult).then_inc(weight_ready, 1)
                            if j < 6 or more:
                                choose(chain, t * PH + (j + 2), (j + 2) % PH)

                    chain = Steps(dve, own)
                    for n in range(2):
                        choose(chain, n, n)
                    with dve.Fori(0, tiles - 1) as t:
                        dve.sem_clear(own)
                        tile(Steps(dve, own), t, True)
                    dve.sem_clear(own)
                    tile(Steps(dve, own), tiles - 1, False)
                    for t in range(tiles):
                        for d in range(KT):
                            dve.wait_ge(y_turned, t * 2 + d // 4 + 1)
                            at = hT[:, d, first_token + t * P:first_token + (t + 1) * P]
                            side = seg_of + t // 2
                            last = dve.scalar_tensor_tensor(
                                out=at, in0=ps[:, 4 + (2 * t + d // 4) % 4, d % 4 * P:d % 4 * P + P],
                                scalar=modc[:, layer, 5, d, side:side + 1], in1=at, op0=ALU.mult,
                                op1=ALU.add)
                            if d % 4 == 3:
                                last.then_inc(y_added, 1)

                @block.tensor
                def _(pe):
                    pe.sem_inc(v_added, SLOTS)
                    pe.sem_inc(sum_taken, 1)
                    norm.pe_sums(pe, ones[:])

                    def query(n, h, free):
                        if free is not None:
                            pe.wait_ge(q_taken, free)
                        for half in range(2):
                            hp = 2 * h + half
                            for k in range(KT):
                                last = pe.matmul(q_ps[:, half * P:half * P + P],
                                                 w_q[:, hp // 4, k, hp % 4 * P:hp % 4 * P + P], xs[:, k],
                                                 start=(k == 0), stop=(k == KT - 1))
                        last.then_inc(q_product, 1)

                    def score(n, h, free):
                        pe.wait_ge(q_taken, n + 1)
                        if free is not None:
                            pe.wait_ge(s_taken, free)
                        for half in range(2):
                            last = pe.matmul(s_ps[:, half * NK:half * NK + NK], q_sb[:, half], keys[:, h, half],
                                             start=True, stop=True)
                        last.then_inc(s_product, 1)

                    def by_token(t):
                        for d in range(KT):
                            last = pe.transpose(f_tok[:, d * P:(d + 1) * P], xs[:, d], ident)
                        last.then_inc(f_ready, 1)

                    def tile(t, more):
                        for j in range(PH):
                            for k in range(TOPK):
                                s = j * TOPK + k
                                r = s % V_RING
                                if s == 0:
                                    pe.wait_ge(sum_taken, t + 1)
                                pe.wait_ge(v_landed[r], t * (16 * SLOTS // V_RING) + 16 * (s // V_RING + 1))
                                pe.wait_ge(diag_ready, t * SLOTS + (s + 1))
                                for half in range(2):
                                    last = pe.matmul(acc[:, half], diag[:, k], v_rows[:, r, half * 512:half * 512 + 512],
                                                     start=(s == 0), stop=(s == SLOTS - 1))
                                last.then_inc(v_added, 1)
                                if k == 2 and (j < 5 or more):
                                    if j == 5:
                                        pe.wait_ge(staged, t + 2)
                                    query(t * PH + (j + 3), (j + 3) % PH, t * PH + (j + 3))
                                if k == 5 and (j < 5 or more):
                                    score(t * PH + (j + 3), (j + 3) % PH, t * PH + (j + 3))
                            if j == 6 and more:
                                pe.wait_ge(dots_done, t * SLOTS + (SLOTS + U_RING))
                                by_token(t + 1)

                    pe.wait_ge(staged, 1)
                    pe.wait_ge(keys_loaded, 16)
                    by_token(0)
                    for n in range(3):
                        pe.wait_ge(w_q_loaded[n // 2], 16)
                        query(n, n, n if n else None)
                        score(n, n, n if n else None)
                    for c in (2, 3):
                        pe.wait_ge(w_q_loaded[c], 16)
                    with pe.Fori(0, tiles - 1) as t:
                        tile(t, True)
                    tile(tiles - 1, False)
                    pe.wait_ge(sum_taken, tiles + 1)
                    for n in range(2 * tiles):
                        if n >= 4:
                            pe.wait_ge(y_added, n - 3)
                        t = n // 2
                        for i in range(4):
                            last = pe.transpose(
                                ps[:, 4 + n % 4, i * P:i * P + P],
                                uT[:, n % 2 * 4 + i, first_token + t * P:first_token + (t + 1) * P], ident)
                        last.then_inc(y_turned, 1)
                    pe.wait_ge(y_added, 2 * tiles)
            stack.close()
            end_phase()

        peer(0, 0, T // P)
        odd_stack = ExitStack()

        def osb(name, shape):
            return odd_stack.enter_context(nc.sbuf_tensor(name, shape, F32))

        N_LAT = SEG
        width = dict(ODD_PARTS)
        part_at, at = {}, 0
        for part, n in ODD_PARTS:
            part_at[part] = at
            at += KT * n
        od_w = osb("od_w", [P, at])
        uq_w = osb("uq_w", [P, Q_LORA // P, MLA_H * QD])
        uk_w = osb("uk_w", [P, KV_LORA // P, MLA_H, NOPE])
        uv_w = osb("uv_w", [P, KV_LORA // P, MLA_H * VD])
        work = osb("odd_work", [P, 10600])

        def od_part(part):
            at = part_at[part]
            return od_w[:, at:at + KT * width[part]].rearrange("p (k n) -> p k n", k=KT)

        at = 0
        PADDED = SEG + CONV_W - 1
        q_pad, at = view(work, at, ML_H, PADDED)
        k_pad, at = view(work, at, ML_H, 2, PADDED)
        after_pads = at
        v_tok, at = view(work, at, T // P, ML_H * P)
        o_tanh, at = view(work, at, ML_H, N_LAT)
        cq, at = view(work, at, Q_LORA // P, N_LAT)
        ckv, at = view(work, at, KV_LORA // P, T)
        k_rot, at = view(work, at, T)
        v_att, at = view(work, at, T // P, MLA_H * VD)
        g_in, g_forget = squares[:, 0], squares[:, 1]
        probs, at = view(work, 0, 2, T)
        h_sum, at = view(work, at, ML_H, N_LAT)
        cq_rms, at = view(work, at, N_LAT)
        den_abs, at = view(work, at, N_LAT)
        assert at <= after_pads
        base = part_at["v"]
        qs_ml, at = view(od_w, base, ML_H, N_LAT)
        ks_ml, at = view(od_w, at, ML_H, T)
        th, at = view(od_w, at, 2, T)
        chain_b, at = view(od_w, at, 8, T)
        assert at <= part_at["cq"]
        weights_ml, at = view(od_w, part_at["cq"], 2, T // P, N_LAT)
        k_att, at = view(od_w, at, 2, T)
        q_att, at = view(od_w, at, 2, N_LAT)
        q_raw, at = view(od_w, at, 2, N_LAT)
        q_sin, at = view(od_w, at, 2, N_LAT)
        c_col, at = view(od_w, at, T // P, HALF_ROWS)
        soft_a, at = view(od_w, at, 2, 4)
        h_rec, at = view(od_w, at, N_LAT)
        assert at <= part_at["gates"] + KT * width["gates"], at
        w_out2 = od_w[:, 0:KT * D].rearrange("p (k n) -> p k n", k=KT)
        uT_flat = uT[:].rearrange("p a b -> p (a b)")
        mix2, at = view(uT_flat, 0, KT, N_LAT)
        probs_t, at = view(uT_flat, at, 2, T // P, N_LAT)

        part_loaded = {part: sem(f"od_{part}_loaded") for part, _ in ODD_PARTS}
        mla_loaded = sem("mla_weights_loaded")
        w_out2_loaded = sem("od_out_loaded")
        mix1 = Norm("mix1", sem, lambda d: hT[:, d, :], squares, ps[:, 0, :], rms[:],
                    lambda d: uT[:, d, :], T, KT)
        kv_norm = Norm("kv_norm", sem, lambda d: ckv[:, d], squares, ps[:, 0, :], rms[:],
                       lambda d: ckv[:, d], T, KV_LORA // P)
        q_norm = Norm("q_norm", sem, lambda d: cq[:, d], squares, ps[:, 7, 0:N_LAT], cq_rms,
                      lambda d: cq[:, d], N_LAT, Q_LORA // P)
        UNITS = ([("gates", 0)] + [("k", i) for i in range(ML_H)] + [("q", i) for i in range(ML_H)]
                 + [("ckv", i) for i in range(2)] + [("krope", 0)] + [("cq", i) for i in range(3)]
                 + [("v", i) for i in range(T // P)] + [("o", i) for i in range(ML_H)])
        LAT_ONLY = ("q", "cq", "o")
        unit_done = {u: n + 1 for n, u in enumerate(UNITS)}
        unit_out, unit_taken = sem("od_unit_out"), sem("od_unit_taken")
        pads2 = sem("od_pads_set")
        forget_abs, forget_exp = sem("forget_abs"), sem("forget_exp")
        conv_done, conv_tanh, qk_ready = sem("ml_conv_done"), sem("ml_conv_tanh"), sem("ml_qk_ready")
        c_ready, c_turned, c_col_ready = sem("ml_c_ready"), sem("ml_c_turned"), sem("ml_c_col_ready")
        stab_in, stab_ready = sem("ml_stab_in"), sem("ml_stab_ready")
        key_swapped, key_ready = sem("key_swapped"), sem("key_ready")
        va_out, va_ready = sem("v_att_out"), sem("v_att_ready")
        ml_scores, ml_spread = sem("ml_scores"), sem("ml_spread")
        ml_arg, ml_exp, ml_weights = sem("ml_arg"), sem("ml_exp"), sem("ml_weights")
        ml_sums, ml_abs, ml_head = sem("ml_sums"), sem("ml_abs"), sem("ml_head")
        out_sq, out_ss, out_ms, out_root = (sem("ml_out_squares"), sem("ml_out_summed"),
                                            sem("ml_out_mean"), sem("ml_out_root"))
        ml_mixed = sem("ml_mixed")
        uq_out, q_raw_ready, q_swapped, q_ready = (sem("uq_out"), sem("q_raw_ready"),
                                                   sem("q_swapped"), sem("q_ready"))
        uk_out, k_nope_ready, k_rope_ready = sem("uk_out"), sem("k_nope_ready"), sem("k_rope_ready")
        att_scores, att_max, att_exp, att_probs = (sem("att_scores"), sem("att_max"), sem("att_exp"),
                                                   sem("att_probs"))
        att_turned, att_kept, att_out, att_mixed = (sem("att_turned"), sem("att_kept"),
                                                    sem("att_out"), sem("att_mixed"))
        odd_out, odd_added = sem("odd_out_product"), sem("odd_added")
        dve_steps, act_steps = sem("odd_dve_steps"), sem("odd_act_steps")
        LAT = slice(SEG, T)
        ML_SCALE = 0.25 * P ** -0.5
        ATT_SCALE = QD ** -0.5
        M_UNITS = 2 * ML_H

        with nc.Block() as block:
            @block.sync
            def _(sp_eng):
                for part in ("gates", "k", "q", "ckv", "krope", "cq", "v", "o"):
                    at = part_at[part]
                    sp_eng.dma_start(od_w[:, at:at + KT * width[part]],
                                     od[:, at:at + KT * width[part]]).then_inc(part_loaded[part], 16)
                sp_eng.dma_start(uv_w[:], w_uv.rearrange("p k h e -> p k (h e)")).then_inc(mla_loaded, 16)
                sp_eng.dma_start(uk_w[:], w_uk).then_inc(mla_loaded, 16)
                sp_eng.dma_start(uq_w[:], w_uq).then_inc(mla_loaded, 16)
                sp_eng.wait_ge(unit_out, unit_done["q", ML_H - 1])
                sp_eng.dma_start(w_out2, od_out).then_inc(w_out2_loaded, 16)

            @block.gpsimd
            def _(pool):
                for h in range(MLA_H):
                    if h == 0:
                        pool.wait_ge(key_ready, 1)
                    if h >= 2:
                        pool.wait_ge(att_scores, 2 * (h - 1))
                    pool.tensor_copy(k_att[NOPE:QD, h % 2], k_rot[NOPE:QD]).then_inc(k_rope_ready, 1)

            @block.scalar
            def _(act):
                steps = Steps(act, act_steps)
                mix1.act_squares(act)
                mix1.act_root(act)
                mix1.act_affine(act, segs, lambda d, s: gain[:, 1, 0, d, s:s + 1],
                                lambda d, s: modc[:, 1, 0, d, s:s + 1])
                act.wait_ge(pads2, 2)
                gate_b = col("ml_gate_b")
                for n, (part, i) in enumerate(UNITS):
                    act.wait_ge(unit_out, n + 1)
                    bank = ps[:, BANK[n % 4], :]
                    if part == "gates":
                        act.activation(g_in[0:HALF_ROWS], bank[0:HALF_ROWS], ACT.Identity,
                                       bias=gate_b[0:HALF_ROWS])
                        last = act.activation(g_forget[0:HALF_ROWS], bank[64:GATE_ROWS], ACT.Identity,
                                              bias=gate_b[64:GATE_ROWS])
                    elif part == "k":
                        last = act.activation(k_pad[:, i, :, 2:2 + SEG],
                                              bank.rearrange("p (s t) -> p s t", s=2), ACT.Copy)
                    elif part == "q":
                        last = act.activation(q_pad[:, i, 2:2 + SEG], bank[:, 0:N_LAT], ACT.Copy)
                    elif part == "ckv":
                        last = act.activation(ckv[:, i], bank, ACT.Copy)
                    elif part == "krope":
                        last = act.activation(k_rot[0:QD], bank[0:QD], ACT.Copy)
                    elif part == "cq":
                        last = act.activation(cq[:, i], bank[:, 0:N_LAT], ACT.Copy)
                    elif part == "v":
                        last = act.activation(v_tok[:, i], bank, ACT.Copy)
                    else:
                        last = act.activation(o_tanh[:, i], bank[:, 0:N_LAT], ACT.Tanh, scale=0.5)
                    last.then_inc(unit_taken, 1)
                act.wait_ge(forget_abs, 1)
                at = chain_b[0:HALF_ROWS, 0]
                act.activation(at, at, ACT.Exp, scale=-1.0).then_inc(forget_exp, 1)
                for n in range(2 * ML_H):
                    act.wait_ge(conv_done, n + 1)
                    if n >= 2:
                        act.wait_ge(qk_ready, n - 1)
                    size = T if n < ML_H else N_LAT
                    src = ks_ml[:, n] if n < ML_H else qs_ml[:, n - ML_H]
                    act.activation(th[:, n % 2, 0:size], src, ACT.Tanh, scale=0.5).then_inc(conv_tanh, 1)
                act.wait_ge(stab_in, 1)
                at = chain_b[0:HALF_ROWS, 7, N_LAT:T]
                act.activation(at, at, ACT.Exp).then_inc(stab_ready, 1)
                kv_norm.act_squares(act)
                kv_norm.act_root(act)
                kv_norm.act_affine(act, [slice(0, T)], lambda d, _: col("kv_norm_g")[:, d:d + 1], None)
                act.wait_ge(kv_norm.summed, KV_LORA // P)
                q_norm.act_squares(act)
                q_norm.act_root(act)
                q_norm.act_affine(act, [slice(0, N_LAT)], lambda d, _: col("q_norm_g")[:, d:d + 1], None)
                for tt in range(T // P):
                    act.wait_ge(va_out, tt + 1)
                    act.activation(v_att[:, tt], ps[:, BANK[tt], :], ACT.Copy).then_inc(va_ready, 1)

                def ml_e(m):
                    act.wait_ge(ml_arg, m + 1)
                    at = weights_ml[:, m % 2]
                    act.activation(at, at, ACT.Exp).then_inc(ml_exp, 1)

                ml_e(0)
                for m in range(M_UNITS):
                    if m + 1 < M_UNITS:
                        ml_e(m + 1)
                    act.wait_ge(ml_sums, m + 1)
                    if m >= 1:
                        act.wait_ge(ml_head, m)
                    act.activation(den_abs, ps[:, 3 + m % 2, N_LAT:T], ACT.Abs).then_inc(ml_abs, 1)
                act.wait_ge(ml_head, M_UNITS)
                act.activation(squares[:].rearrange("p a b -> p (a b)"),
                               h_sum.rearrange("p a b -> p (a b)"), ACT.Square).then_inc(out_sq, 1)
                act.wait_ge(out_ms, 2)
                for i in range(2):
                    act.activation(weights_ml[:, i, 0:2].rearrange("p a b -> p (a b)"),
                                   weights_ml[:, i, 0:2].rearrange("p a b -> p (a b)"),
                                   ACT.Sqrt).then_inc(out_root, 1)

                def prepare(h):
                    act.wait_ge(uq_out, h + 1)
                    if h >= 2:
                        act.wait_ge(q_ready, h - 1)
                    act.activation(q_raw[0:QD, h % 2], ps[0:QD, 1, 0:N_LAT], ACT.Copy).then_inc(q_raw_ready, 1)
                    act.wait_ge(uk_out, h + 1)
                    if h >= 2:
                        act.wait_ge(att_scores, 2 * (h - 1))
                    act.activation(k_att[0:NOPE, h % 2], ps[0:NOPE, 2, :], ACT.Copy).then_inc(k_nope_ready, 1)

                prepare(0)
                for h in range(MLA_H):
                    for qt in range(2):
                        n = 2 * h + qt
                        act.wait_ge(att_max, n + 1)
                        if n >= 2:
                            act.wait_ge(att_turned, n - 1)
                        act.activation(probs[:, qt], ps[:, 3 + qt, :], ACT.Exp, scale=ATT_SCALE,
                                       bias=soft_a[:, qt, 1:2], accum_out=soft_a[:, qt, 2:3]).then_inc(att_exp, 1)
                    if h + 1 < MLA_H:
                        prepare(h + 1)
                    for qt in range(2):
                        n = 2 * h + qt
                        act.wait_ge(att_turned, n + 1)
                        if h >= 2:
                            act.wait_ge(att_out, h - 1)
                        act.activation(probs_t[:, h % 2, :, qt * P:(qt + 1) * P],
                                       ps[:, 5 + qt, :].rearrange("p (a b) -> p a b", a=4),
                                       ACT.Copy).then_inc(att_kept, 1)
                    act.wait_ge(att_out, h + 1)
                    act.activation(mix2[VD * (h % 2):VD * (h % 2) + VD, ML_H + h // 2],
                                   ps[0:VD, 7, 0:N_LAT], ACT.Copy).then_inc(att_mixed, 1)

            @block.vector
            def _(dve):
                steps = Steps(dve, dve_steps)
                mix1.dve_mean(dve)
                mix1.dve_scale(dve, steps)
                q4, k4 = q_pad, k_pad
                steps(dve.memset(q4[:, :, 0:2], 0.0))
                steps(dve.memset(k4[:, :, :, 0:2], 0.0))
                dve.memset(q4[:, :, 2 + SEG:], 0.0).then_inc(pads2, 1)
                dve.memset(k4[:, :, :, 2 + SEG:], 0.0).then_inc(pads2, 1)
                rows = slice(0, HALF_ROWS)
                e, z, z2, lf, run, c, m_run, ns = (chain_b[rows, i] for i in range(8))
                dve.wait_ge(unit_taken, len(UNITS))
                gf, gi = g_forget[rows], g_in[rows]
                dve.scalar_tensor_tensor(out=e, in0=gf, scalar=-1.0, in1=gf, op0=ALU.mult,
                                         op1=ALU.max).then_inc(forget_abs, 1)
                dve.wait_ge(pads2, 2)
                for n in range(2 * ML_H):
                    i = n % ML_H
                    w = col("ml_conv_w")
                    blk = ML_H + i if n < ML_H else i
                    if n < ML_H:
                        to = ks_ml[:, i].rearrange("p (s t) -> p s t", s=2)
                        src = lambda a: k4[:, i, :, a:a + SEG]
                    else:
                        to = qs_ml[:, i]
                        src = lambda a: q4[:, i, a:a + SEG]
                    steps(dve.tensor_scalar(to, src(0), w[:, blk, 0:1], col("ml_conv_b")[:, blk:blk + 1],
                                            ALU.mult, ALU.add))
                    for a in range(1, CONV_W):
                        last = dve.scalar_tensor_tensor(out=to, in0=src(a), scalar=w[:, blk, a:a + 1],
                                                        in1=to, op0=ALU.mult, op1=ALU.add)
                        if a < CONV_W - 1:
                            steps(last)
                    last.then_inc(conv_done, 1)
                dve.wait_ge(forget_exp, 1)
                softplus_tail(dve, steps, e, z, z2, lf)
                steps(dve.scalar_tensor_tensor(out=lf, in0=gf, scalar=0.0, in1=lf, op0=ALU.min,
                                               op1=ALU.subtract))
                steps(dve.memset(e, 1.0))
                back = slice(32, HALF_ROWS)
                steps(dve.tensor_tensor_scan(out=run, data0=e, data1=lf, initial=0.0, op0=ALU.mult,
                                             op1=ALU.add))
                B = chain_b[:, 4]
                for s, first in ((0, 0.0), (1, B[back, 0:1])):
                    steps(dve.tensor_tensor_scan(
                        out=B[back, segs[s]][:, ::-1], data0=chain_b[back, 0, segs[s]][:, ::-1],
                        data1=chain_b[back, 3, segs[s]][:, ::-1], initial=first, op0=ALU.mult, op1=ALU.add))
                dve.tensor_tensor(c, gi, run, ALU.subtract).then_inc(c_ready, 1)
                dve.wait_ge(c_ready, 1)
                steps(dve.tensor_tensor_scan(out=m_run, data0=c, data1=c, initial=NEG, op0=ALU.max,
                                             op1=ALU.max))
                M, C = chain_b[:, 6], chain_b[:, 5]
                for s, first in ((0, NEG), (1, M[back, 0:1])):
                    steps(dve.tensor_tensor_scan(
                        out=M[back, segs[s]][:, ::-1], data0=C[back, segs[s]][:, ::-1],
                        data1=C[back, segs[s]][:, ::-1], initial=first, op0=ALU.max, op1=ALU.max))
                steps(dve.tensor_scalar(ns[:, 0:N_LAT], m_run[:, LAT], -1.0, None, ALU.mult))
                steps(dve.tensor_tensor(ns[:, LAT], ns[:, 0:N_LAT], run[:, LAT], ALU.subtract))
                dve.tensor_scalar(ns[:, LAT], ns[:, LAT], 80.0, None, ALU.min).then_inc(stab_in, 1)
                for n in range(2 * ML_H):
                    dve.wait_ge(conv_tanh, n + 1)
                    size = T if n < ML_H else N_LAT
                    at = ks_ml[:, n] if n < ML_H else qs_ml[:, n - ML_H]
                    dve.scalar_tensor_tensor(out=at, in0=th[:, n % 2, 0:size], scalar=1.0, in1=at,
                                             op0=ALU.add, op1=ALU.mult).then_inc(qk_ready, 1)
                dve.wait_ge(c_turned, 1)
                dve.tensor_copy(c_col, ps[:, 5, 0:4 * HALF_ROWS].rearrange("p (a b) -> p a b", a=4)
                                ).then_inc(c_col_ready, 1)
                dve.wait_ge(key_swapped, 1)
                steps(dve.tensor_tensor(q_sin[0:QD, 0], ps[0:QD, 6, 0:N_LAT], const("rope_sin")[0:QD], ALU.mult))
                steps(dve.tensor_tensor(k_rot[0:QD, LAT], k_rot[0:QD, LAT], const("rope_cos")[0:QD], ALU.mult))
                dve.tensor_tensor(k_rot[0:QD, LAT], k_rot[0:QD, LAT], q_sin[0:QD, 0],
                                  ALU.add).then_inc(key_ready, 1)
                dve.wait_ge(key_ready, 1)
                kv_norm.dve_mean(dve)
                kv_norm.dve_scale(dve, steps)
                q_norm.dve_mean(dve)
                q_norm.dve_scale(dve, steps)
                dve.wait_ge(c_col_ready, 1)

                def ml_d(m):
                    h, d = m // 2, m % 2
                    dve.wait_ge(ml_spread, m + 1)
                    if m >= 2:
                        dve.wait_ge(ml_sums, m - 1)
                    for kt in range(T // P):
                        row = 32 * d + h
                        last = dve.tensor_scalar(weights_ml[:, m % 2, kt], ps[:, 1 + m % 2, 0:N_LAT],
                                                 c_col[:, kt, row:row + 1], 0.0, ALU.add, ALU.min)
                    last.then_inc(ml_arg, 1)

                def ml_p(m):
                    h, d = m // 2, m % 2
                    dve.wait_ge(ml_exp, m + 1)
                    dve.wait_ge(ml_scores, h + 1)
                    at = weights_ml[:, m % 2].rearrange("p a b -> p (a b)")
                    steps(dve.scalar_tensor_tensor(
                        out=at, in0=ps[:, 6:8, :].rearrange("p a b -> p (a b)"), scalar=ML_SCALE, in1=at,
                        op0=ALU.mult, op1=ALU.mult))
                    late = weights_ml[:, m % 2, 2:4]
                    dve.tensor_tensor(late, late, const("causal")[:, d], ALU.mult).then_inc(ml_weights, 1)

                def ml_h(m):
                    h, d = m // 2, m % 2
                    dve.wait_ge(ml_abs, m + 1)
                    steps(dve.tensor_tensor(h_rec, den_abs, ps[:, 1 + m % 2, N_LAT:T], ALU.max))
                    steps(dve.reciprocal(h_rec, h_rec))
                    to = h_sum[:, h] if d == 0 else h_rec
                    if d == 0:
                        dve.tensor_tensor(to, ps[:, 3 + m % 2, 0:N_LAT], h_rec, ALU.mult).then_inc(ml_head, 1)
                    else:
                        steps(dve.tensor_tensor(to, ps[:, 3 + m % 2, 0:N_LAT], h_rec, ALU.mult))
                        dve.tensor_tensor(h_sum[:, h], h_sum[:, h], h_rec, ALU.add).then_inc(ml_head, 1)
                    dve.wait_ge(ml_head, m + 1)

                ml_d(0)
                for m in range(M_UNITS):
                    ml_p(m)
                    if m >= 1:
                        ml_h(m - 1)
                    if m + 1 < M_UNITS:
                        ml_d(m + 1)
                ml_h(M_UNITS - 1)
                dve.wait_ge(out_ss, 2)
                for i in range(2):
                    dve.tensor_scalar(weights_ml[:, i, 0:2].rearrange("p a b -> p (a b)"),
                                      ps[:, 5 if i == 0 else 0, :], 4.0 / P, 4.0 * EPS, ALU.mult,
                                      ALU.add).then_inc(out_ms, 1)
                dve.wait_ge(out_root, 2)
                for i in range(2):
                    at = weights_ml[:, i, 0:2]
                    steps(dve.reciprocal(at, at))
                    for j in range(2):
                        h = 2 * i + j
                        steps(dve.scalar_tensor_tensor(out=h_sum[:, h], in0=h_sum[:, h],
                                                       scalar=col("ml_head_g")[:, h:h + 1], in1=at[:, j],
                                                       op0=ALU.mult, op1=ALU.mult))
                        dve.scalar_tensor_tensor(out=mix2[:, h], in0=o_tanh[:, h], scalar=1.0,
                                                 in1=h_sum[:, h], op0=ALU.add,
                                                 op1=ALU.mult).then_inc(ml_mixed, 1)

                def rotate(h):
                    dve.wait_ge(q_swapped, h + 1)
                    if h >= 2:
                        dve.wait_ge(att_scores, 2 * (h - 1))
                    b = h % 2
                    steps(dve.tensor_tensor(q_sin[0:QD, b], ps[0:QD, 0, 0:N_LAT], const("rope_sin")[0:QD], ALU.mult))
                    steps(dve.tensor_tensor(q_att[0:QD, b], q_raw[0:QD, b], const("rope_cos")[0:QD], ALU.mult))
                    dve.tensor_tensor(q_att[0:QD, b], q_att[0:QD, b], q_sin[0:QD, b], ALU.add).then_inc(q_ready, 1)
                    dve.wait_ge(q_ready, h + 1)

                rotate(0)
                for h in range(MLA_H):
                    for qt in range(2):
                        n = 2 * h + qt
                        dve.wait_ge(att_scores, n + 1)
                        steps(dve.reduce_max(soft_a[:, qt, 0:1], ps[:, 3 + qt, :], AX))
                        dve.tensor_scalar(soft_a[:, qt, 1:2], soft_a[:, qt, 0:1], -ATT_SCALE, None,
                                          ALU.mult).then_inc(att_max, 1)
                    if h + 1 < MLA_H:
                        rotate(h + 1)
                    for qt in range(2):
                        n = 2 * h + qt
                        dve.wait_ge(att_exp, n + 1)
                        steps(dve.reciprocal(soft_a[:, qt, 3:4], soft_a[:, qt, 2:3]))
                        dve.tensor_scalar(probs[:, qt], probs[:, qt], soft_a[:, qt, 3:4], None,
                                          ALU.mult).then_inc(att_probs, 1)
                for n in range(KT):
                    dve.wait_ge(odd_out, n + 1)
                    dve.scalar_tensor_tensor(
                        out=hT[:, n, LAT], in0=ps[:, BANK[n % 4], 0:N_LAT],
                        scalar=modc[:, 1, 2, n, 1:2], in1=hT[:, n, LAT], op0=ALU.mult,
                        op1=ALU.add).then_inc(odd_added, 1)

            @block.tensor
            def _(pe):
                mix1.pe_sums(pe, ones[:])
                for n, (part, i) in enumerate(UNITS):
                    if i == 0:
                        pe.wait_ge(part_loaded[part], 16)
                    if n >= 4:
                        pe.wait_ge(unit_taken, n - 3)
                    w = od_part(part)
                    rows = min(P, width[part])
                    tokens = LAT if part in LAT_ONLY else slice(0, T)
                    for k in range(KT):
                        if n == 0:
                            pe.wait_ge(mix1.ready, k + 1)
                        if part == "v":
                            last = pe.matmul(ps[:, BANK[n % 4], :], uT[:, k, i * P:(i + 1) * P], w[:, k],
                                             start=(k == 0), stop=(k == KT - 1))
                        else:
                            size = tokens.stop - tokens.start
                            last = pe.matmul(ps[0:rows, BANK[n % 4], 0:size],
                                             w[:, k, i * P:i * P + rows], uT[:, k, tokens],
                                             start=(k == 0), stop=(k == KT - 1))
                    last.then_inc(unit_out, 1)
                pe.wait_ge(unit_taken, len(UNITS))
                pe.matmul(ps[0:QD, 6, 0:N_LAT], const("rope_swap")[0:QD], k_rot[0:QD, LAT], start=True,
                          stop=True).then_inc(key_swapped, 1)
                pe.wait_ge(c_ready, 1)
                for kt in range(T // P):
                    last = pe.transpose(ps[:, 5, kt * HALF_ROWS:(kt + 1) * HALF_ROWS],
                                        chain_b[0:HALF_ROWS, 5, kt * P:(kt + 1) * P],
                                        ident[0:HALF_ROWS, 0:HALF_ROWS])
                last.then_inc(c_turned, 1)
                kv_norm.pe_sums(pe, ones[:])
                q_norm.pe_sums(pe, ones[:])
                pe.wait_ge(mla_loaded, 48)
                pe.wait_ge(kv_norm.ready, KV_LORA // P)
                for tt in range(T // P):
                    for k in range(KV_LORA // P):
                        last = pe.matmul(ps[:, BANK[tt], :], ckv[:, k, tt * P:(tt + 1) * P], uv_w[:, k],
                                         start=(k == 0), stop=(k == KV_LORA // P - 1))
                    last.then_inc(va_out, 1)

                def spread(m):
                    if m >= 2:
                        pe.wait_ge(ml_head, m - 1)
                    i = ML_H * (m % 2) + m // 2
                    pe.matmul(ps[:, 1 + m % 2, :], const("pick")[0:HALF_ROWS, i], chain_b[0:HALF_ROWS, 7],
                              start=True, stop=True).then_inc(ml_spread, 1)

                def ml_score(h):
                    if h >= 1:
                        pe.wait_ge(ml_weights, 2 * h)
                    for kt in range(T // P):
                        last = pe.matmul(ps[:, 6 + kt // 2, kt % 2 * N_LAT:kt % 2 * N_LAT + N_LAT],
                                         ks_ml[:, h, kt * P:(kt + 1) * P], qs_ml[:, h], start=True, stop=True)
                    last.then_inc(ml_scores, 1)

                pe.wait_ge(va_ready, T // P)
                pe.wait_ge(stab_ready, 1)
                pe.wait_ge(qk_ready, 2 * ML_H)
                pe.wait_ge(key_ready, 1)
                pe.wait_ge(q_norm.ready, Q_LORA // P)
                spread(0)
                ml_score(0)
                spread(1)
                for m in range(M_UNITS):
                    h = m // 2
                    pe.wait_ge(ml_weights, m + 1)
                    if m >= 2:
                        pe.wait_ge(ml_head, m - 1)
                    for to, lhs in ((slice(0, N_LAT), None), (LAT, ones[:])):
                        for kt in range(T // P):
                            last = pe.matmul(ps[:, 3 + m % 2, to],
                                             v_tok[:, kt, h * P:(h + 1) * P] if lhs is None else lhs,
                                             weights_ml[:, m % 2, kt], start=(kt == 0), stop=(kt == T // P - 1))
                    last.then_inc(ml_sums, 1)
                    if m % 2 == 1 and h + 1 < ML_H:
                        ml_score(h + 1)
                    if m + 2 < M_UNITS:
                        spread(m + 2)
                pe.wait_ge(out_sq, 1)
                for i in range(2):
                    pe.matmul(ps[:, 5 if i == 0 else 0, :], ones[:], squares[:, i], start=True,
                              stop=True).then_inc(out_ss, 1)

                def prepare_q(h):
                    if h >= 1:
                        pe.wait_ge(q_raw_ready, h)
                    for k in range(Q_LORA // P):
                        last = pe.matmul(ps[0:QD, 1, 0:N_LAT], uq_w[:, k, h * QD:(h + 1) * QD], cq[:, k],
                                         start=(k == 0), stop=(k == Q_LORA // P - 1))
                    last.then_inc(uq_out, 1)
                    if h >= 1:
                        pe.wait_ge(k_nope_ready, h)
                    for k in range(KV_LORA // P):
                        last = pe.matmul(ps[0:NOPE, 2, :], uk_w[:, k, h], ckv[:, k],
                                         start=(k == 0), stop=(k == KV_LORA // P - 1))
                    last.then_inc(uk_out, 1)

                def swap_q(h):
                    pe.wait_ge(q_raw_ready, h + 1)
                    if h >= 1:
                        pe.wait_ge(q_ready, h)
                    pe.matmul(ps[0:QD, 0, 0:N_LAT], const("rope_swap")[0:QD], q_raw[0:QD, h % 2],
                              start=True, stop=True).then_inc(q_swapped, 1)

                pe.wait_ge(out_ms, 2)
                pe.wait_ge(ml_head, M_UNITS)
                prepare_q(0)
                swap_q(0)
                for h in range(MLA_H):
                    pe.wait_ge(q_ready, h + 1)
                    pe.wait_ge(k_nope_ready, h + 1)
                    pe.wait_ge(k_rope_ready, h + 1)
                    for qt in range(2):
                        if h >= 1:
                            pe.wait_ge(att_exp, 2 * (h - 1) + qt + 1)
                        pe.matmul(ps[:, 3 + qt, :], q_att[0:QD, h % 2, qt * P:(qt + 1) * P],
                                  k_att[0:QD, h % 2], start=True, stop=True).then_inc(att_scores, 1)
                    if h + 1 < MLA_H:
                        prepare_q(h + 1)
                        swap_q(h + 1)
                    for qt in range(2):
                        n = 2 * h + qt
                        pe.wait_ge(att_probs, n + 1)
                        if h >= 1:
                            pe.wait_ge(att_kept, n - 1)
                        for kt in range(T // P):
                            last = pe.transpose(ps[:, 5 + qt, kt * P:(kt + 1) * P],
                                                probs[:, qt, kt * P:(kt + 1) * P], ident)
                        last.then_inc(att_turned, 1)
                    pe.wait_ge(att_kept, 2 * h + 2)
                    if h >= 1:
                        pe.wait_ge(att_mixed, h)
                    for kt in range(T // P):
                        last = pe.matmul(ps[0:VD, 7, 0:N_LAT], v_att[:, kt, h * VD:(h + 1) * VD],
                                         probs_t[:, h % 2, kt], start=(kt == 0), stop=(kt == T // P - 1))
                    last.then_inc(att_out, 1)
                pe.wait_ge(w_out2_loaded, 16)
                pe.wait_ge(ml_mixed, ML_H)
                pe.wait_ge(att_mixed, MLA_H)
                pe.wait_ge(att_exp, 2 * MLA_H)
                for n in range(KT):
                    if n >= 4:
                        pe.wait_ge(odd_added, n - 3)
                    for k in range(KT):
                        last = pe.matmul(ps[:, BANK[n % 4], 0:N_LAT], w_out2[:, k, n * P:(n + 1) * P],
                                         mix2[:, k], start=(k == 0), stop=(k == KT - 1))
                    last.then_inc(odd_out, 1)
        odd_stack.close()
        end_phase()

        peer(1, SEG, SEG // P)

        last_norm = Norm("last", sem, lambda d: hT[:, d, LAT], squares, ps[:, 0, 0:N_LAT],
                         rms[:, 0:N_LAT], lambda d: uT[:, d, LAT], N_LAT, KT)
        stored = sem("stored")
        dve_steps = sem("last_dve_steps")
        with nc.Block() as block:
            @block.scalar
            def _(act):
                last_norm.act_squares(act)
                last_norm.act_root(act)
                last_norm.act_affine(act, [slice(0, N_LAT)], lambda d, _: col("final_g")[:, d:d + 1], None)

            @block.vector
            def _(dve):
                steps = Steps(dve, dve_steps)
                last_norm.dve_mean(dve)
                last_norm.dve_scale(dve, steps)

            @block.tensor
            def _(pe):
                last_norm.pe_sums(pe, ones[:])

            @block.sync
            def _(sp_eng):
                for half in range(2):
                    blocks = slice(4 * half, 4 * half + 4)
                    sp_eng.wait_ge(last_norm.ready, 4 * half + 4)
                    sp_eng.dma_start(out[:, blocks], uT[:, blocks, LAT]).then_inc(stored, 16)
                sp_eng.wait_ge(stored, 32)


def blocks_of(v):
    return v.reshape(-1, P).T


def rows_of(w):
    return np.ascontiguousarray(w.reshape(-1, P, w.shape[-1]).transpose(1, 0, 2))


def constants():
    c = np.zeros((P, N_CONSTS), np.float32)

    def put(name, value):
        at, shape = CONSTS[name]
        value = np.asarray(value, np.float64)
        value = value.reshape(value.shape[0], -1)
        c[:value.shape[0], at:at + value.shape[1]] = value

    put("ident", np.eye(P))
    a = 2 * np.pi * (np.outer(np.arange(64), np.arange(64)) % 64) / 64
    put("chan_dft", np.concatenate([np.kron(np.eye(2), np.cos(a)), np.kron(np.eye(2), np.sin(a))], 1))
    a = 2 * np.pi * (np.outer(np.arange(SEG), np.arange(SEG)) % SEG) / SEG
    both = np.stack([np.cos(a), -np.sin(a)]) / 128.0
    put("time_dft", both.reshape(2, 2, P, SEG).transpose(2, 0, 1, 3))
    half = ROPE // 2
    inv = (np.float32(10000.0) ** (-np.arange(0, half, 2, dtype=np.float32) / np.float32(half))).astype(np.float32)
    row = np.repeat(np.arange(SEG // 64, dtype=np.float32), 64)
    colu = np.tile(np.arange(64, dtype=np.float32), SEG // 64)
    ang = np.concatenate([row[:, None] * inv, colu[:, None] * inv], axis=-1).astype(np.float32)
    cos, sin = np.ones((QD, SEG)), np.zeros((QD, SEG))
    cos[NOPE:] = np.repeat(np.cos(ang.astype(np.float64)).T, 2, axis=0)
    sin[NOPE:] = np.repeat(np.sin(ang.astype(np.float64)).T, 2, axis=0)
    put("rope_cos", cos)
    put("rope_sin", sin)
    swap = np.zeros((QD, QD))
    for i in range(NOPE, QD, 2):
        swap[i + 1, i] = -1.0
        swap[i, i + 1] = 1.0
    put("rope_swap", swap)
    s, t = np.arange(SEG)[:, None], np.arange(SEG)[None, :]
    masks = np.stack([s <= t, s >= t]).astype(np.float64)
    put("causal", masks.reshape(2, 2, P, SEG).transpose(2, 0, 1, 3))
    pick = np.zeros((P, 2 * ML_H, P))
    for i in range(2 * ML_H):
        pick[32 * (i // ML_H) + i % ML_H, i] = 1.0
    put("pick", pick)
    put("iota", np.broadcast_to(np.arange(TOPK), (P, TOPK)))
    return c


def lay_out(x, c, ctx, c_ctx, mod_w, mod_b, norm_mix_g, norm_ffn_g, ev_w_in, ev_w_out, rg_conv_w,
            rg_conv_b, rg_wa, rg_ba, rg_wx, rg_bx, rg_lam, fn_w, fn_b, od_w_in, od_w_out,
            ml_conv_w, ml_conv_b, ml_gate_b, ml_head_g, mla_q_norm_g, mla_w_uq, mla_kv_norm_g,
            mla_w_ukv, peer_w_q, peer_keys, peer_u, peer_v, final_g):
    cols = np.zeros((P, N_COLS), np.float32)

    def put(name, value):
        at, shape = COLS[name]
        value = value.reshape(value.shape[0], -1)
        cols[:value.shape[0], at:at + value.shape[1]] = value

    put("cond", np.stack([blocks_of(c_ctx), blocks_of(c[0])], 2))
    put("mod_b", blocks_of(mod_b))
    put("norm_g", np.stack([norm_mix_g, norm_ffn_g], 1).reshape(-1, P).T)
    put("final_g", blocks_of(final_g))
    put("rg_conv_w", rg_conv_w[0].reshape(CONV_W, RG_H, P).transpose(2, 1, 0))
    put("rg_conv_b", blocks_of(rg_conv_b))
    put("rg_ba", blocks_of(rg_ba))
    put("rg_bx", blocks_of(rg_bx))
    put("rg_lam", blocks_of(rg_lam))
    put("fn_b", blocks_of(fn_b))
    put("ml_conv_w", ml_conv_w[0].reshape(CONV_W, 8, P).transpose(2, 1, 0))
    put("ml_conv_b", blocks_of(ml_conv_b))
    put("ml_head_g", blocks_of(ml_head_g))
    put("q_norm_g", blocks_of(mla_q_norm_g))
    put("kv_norm_g", blocks_of(mla_kv_norm_g))
    gb = np.zeros((GATE_ROWS, 1), np.float32)
    b = ml_gate_b.reshape(2, 2, ML_H)
    for d in range(2):
        for kind in range(2):
            at = 64 * kind + 32 * d
            gb[at:at + ML_H, 0] = b[d, kind]
    put("ml_gate_b", gb)

    even = np.zeros((P, N_EVEN), np.float32)
    at, _ = EVEN["fn_w"]
    even[:, :at] = np.stack([rg_wa[0], rg_wx[0]]).transpose(3, 0, 1, 2, 4).reshape(P, -1)
    even[:, at:] = fn_w[0].reshape(2, P, 64).transpose(1, 0, 2).reshape(P, -1)

    w = od_w_in[0]
    parts, at = {}, 0
    for name, n in ODD_PARTS[:4]:
        parts[name] = w[:, at:at + n]
        at += n
    gates = w[:, at:at + 16].reshape(D, 2, 2, ML_H)
    at += 16
    for name, n in ODD_PARTS[4:6]:
        parts[name] = w[:, at:at + n]
        at += n
    krope = np.zeros((D, QD), np.float32)
    krope[:, NOPE:] = w[:, at:]
    parts["krope"] = krope
    g = np.zeros((D, GATE_ROWS), np.float32)
    for kind in range(2):
        for d in range(2):
            g[:, 64 * kind + 32 * d:64 * kind + 32 * d + ML_H] = gates[:, d, kind]
    parts["gates"] = g
    od = np.concatenate([rows_of(parts[name]).reshape(P, -1) for name, _ in ODD_PARTS], 1)

    tokens = np.concatenate([ctx[0], x[0]], 0)
    ukv = rows_of(mla_w_ukv[0]).reshape(P, KV_LORA // P, MLA_H, NOPE + VD)
    return {
        "hT0": rows_of(np.ascontiguousarray(tokens.T)),
        "cols_in": cols,
        "consts_in": constants(),
        "mod_w": np.ascontiguousarray(
            mod_w.reshape(2, KT, P, N_MOD * KT // PIECE_J, PIECE_J * P).transpose(0, 3, 2, 1, 4)
        ).reshape(PIECES, P, KT, PIECE_J * P),
        "ev_in": np.ascontiguousarray(ev_w_in[0].reshape(KT, P, 7, 2 * P).transpose(2, 1, 0, 3)),
        "ev_out": rows_of(ev_w_out[0]),
        "even_in": even,
        "od": np.ascontiguousarray(od),
        "w_uq": rows_of(mla_w_uq[0]),
        "w_uk": np.ascontiguousarray(ukv[..., :NOPE]),
        "w_uv": np.ascontiguousarray(ukv[..., NOPE:]),
        "od_out": rows_of(od_w_out[0]),
        "peer_q": np.ascontiguousarray(
            peer_w_q.reshape(2, KT, P, 4, 4 * P).transpose(0, 3, 2, 1, 4)),
        "peer_keys": np.ascontiguousarray(peer_keys.transpose(0, 4, 2, 1, 3)),
        "peer_u0": peer_u[0], "peer_u1": peer_u[1], "peer_v0": peer_v[0], "peer_v1": peer_v[1],
    }


def kernel(**inputs):
    import concourse.bacc as _bacc
    from concourse import mybir as _mybir
    from concourse.bass_utils import run_bass_kernel_spmd as _run
    nc = _bacc.Bacc("TRN2", target_bir_lowering=False, num_devices=1)
    data = lay_out(**{name: np.asarray(value) for name, value in inputs.items()})
    args, arrays = {}, {}
    for name, value in data.items():
        arrays[f"in_{name}_dram"] = value
        args[name] = nc.dram_tensor(f"in_{name}_dram", value.shape, _mybir.dt.from_np(value.dtype),
                                    kind="ExternalInput").ap()
    out = nc.dram_tensor("out_0_dram", (P, KT, SEG), F32, kind="ExternalOutput").ap()
    args["peer_u"] = [args.pop("peer_u0"), args.pop("peer_u1")]
    args["peer_v"] = [args.pop("peer_v0"), args.pop("peer_v1")]
    backbone(nc, out=out, **args)
    got = _run(nc, [arrays], core_ids=[0]).results[0]["out_0_dram"]
    return np.ascontiguousarray(got.transpose(1, 0, 2).reshape(D, SEG).T).reshape(1, SEG, D)
```

```python
import math
from contextlib import ExitStack

import concourse.bass as bass
import numpy as np
from concourse import mybir

ALU = mybir.AluOpType
ACT = mybir.ActivationFunctionType
F32 = mybir.dt.float32
I32 = mybir.dt.int32
U32 = mybir.dt.uint32
AX = mybir.AxisListType.X

P = 128
D = 1024
KT = D // P
SEG = 256
T = 2 * SEG
EPS = 1e-6
N_MOD = 6
CONV_W = 4
RG_H = 6
EV_J = 14
ML_H = 4
MLA_H = 8
NOPE, ROPE, VD = 64, 32, 64
QD = NOPE + ROPE
Q_LORA, KV_LORA = 384, 256
PH = 8
NK = 128
TOPK = 16
SLOTS = PH * TOPK
PIECE_J = 4
PIECES = 2 * N_MOD * KT // PIECE_J
MOD_RING = 2
U_RING, V_RING = 8, 4
LAG = 20
NEG = -3.0e38
GATE_ROWS = 100
HALF_ROWS = 36
GELU_C = 0.044715
GELU_S = math.sqrt(2.0 / math.pi)


def offsets(spec):
    out, at = {}, 0
    for name, *shape in spec:
        out[name] = (at, shape)
        at += math.prod(shape)
    return out, at


COLS, N_COLS = offsets([
    ("cond", KT, 2), ("mod_b", 2, N_MOD * KT), ("norm_g", 2, 2, KT), ("final_g", KT),
    ("rg_conv_w", RG_H, CONV_W), ("rg_conv_b", RG_H), ("rg_ba", 2, RG_H), ("rg_bx", 2, RG_H),
    ("rg_lam", 2, RG_H), ("fn_b", 2), ("ml_conv_w", 8, CONV_W), ("ml_conv_b", 8),
    ("ml_gate_b", 1), ("ml_head_g", ML_H), ("q_norm_g", Q_LORA // P), ("kv_norm_g", KV_LORA // P)])
CONSTS, N_CONSTS = offsets([
    ("ident", P), ("chan_dft", 2, P), ("time_dft", 2, 2, SEG), ("rope_cos", SEG),
    ("rope_sin", SEG), ("rope_swap", QD), ("causal", 2, 2, SEG), ("pick", 2 * ML_H, P),
    ("iota", TOPK)])
EVEN, N_EVEN = offsets([("rg_w", 2, 2, RG_H, P), ("fn_w", 2, 64)])
ODD_PARTS = [("q", 512), ("k", 512), ("v", 512), ("o", 512), ("cq", Q_LORA), ("ckv", KV_LORA),
             ("krope", QD), ("gates", GATE_ROWS)]


def field(tensor, table, name):
    at, shape = table[name]
    ap = tensor[:, at:at + math.prod(shape)]
    if len(shape) > 1:
        names = "abcd"[:len(shape)]
        ap = ap.rearrange(f"p ({' '.join(names)}) -> p {' '.join(names)}",
                          **{n: s for n, s in zip(names, shape)})
    return ap


class Steps:

    def __init__(self, engine, semaphore):
        self.engine, self.semaphore, self.n, self.base = engine, semaphore, 0, 0

    def __call__(self, instruction):
        self.n += 1
        instruction.then_inc(self.semaphore, 1)
        self.engine.wait_ge(self.semaphore, self.base + self.n)


class Norm:

    def __init__(self, name, sem, src, squares, bank, work, out, tokens, blocks, eps_of=None):
        self.src, self.squares, self.bank, self.work, self.out = src, squares, bank, work, out
        self.tokens, self.blocks = tokens, blocks
        self.squared = sem(f"{name}_squared")
        self.summed = sem(f"{name}_summed")
        self.mean = sem(f"{name}_mean")
        self.root = sem(f"{name}_root")
        self.scaled = sem(f"{name}_scaled")
        self.ready = sem(f"{name}_ready")

    def act_squares(self, act):
        for d in range(self.blocks):
            if d >= 2:
                act.wait_ge(self.summed, d - 1)
            act.activation(self.squares[:, d % 2, 0:self.tokens], self.src(d),
                           ACT.Square).then_inc(self.squared, 1)

    def pe_sums(self, pe, ones):
        for d in range(self.blocks):
            pe.wait_ge(self.squared, d + 1)
            pe.matmul(self.bank, ones, self.squares[:, d % 2, 0:self.tokens], start=(d == 0),
                      stop=(d == self.blocks - 1)).then_inc(self.summed, 1)

    def dve_mean(self, dve):
        dve.wait_ge(self.summed, self.blocks)
        dve.tensor_scalar(self.work, self.bank, 1.0 / (self.blocks * P), EPS, ALU.mult,
                          ALU.add).then_inc(self.mean, 1)

    def act_root(self, act):
        act.wait_ge(self.mean, 1)
        act.activation(self.work, self.work, ACT.Sqrt).then_inc(self.root, 1)

    def dve_scale(self, dve, steps):
        dve.wait_ge(self.root, 1)
        steps(dve.reciprocal(self.work, self.work))
        for d in range(self.blocks):
            dve.tensor_tensor(self.out(d), self.src(d), self.work, ALU.mult).then_inc(self.scaled, 1)

    def act_affine(self, act, parts, scale, shift):
        for d in range(self.blocks):
            act.wait_ge(self.scaled, d + 1)
            for n, part in enumerate(parts):
                at = self.out(d)[:, part]
                if shift is None:
                    last = act.activation(at, at, ACT.Copy, scale=scale(d, n))
                else:
                    last = act.activation(at, at, ACT.Identity, scale=scale(d, n), bias=shift(d, n))
            last.then_inc(self.ready, 1)


def softplus_tail(dve, steps, e, z, z2, p):
    steps(dve.tensor_scalar(z, e, 2.0, None, ALU.add))
    steps(dve.reciprocal(z, z))
    steps(dve.tensor_tensor(z, z, e, ALU.mult))
    steps(dve.tensor_tensor(z2, z, z, ALU.mult))
    steps(dve.tensor_scalar(p, z2, 1.0 / 17.0, None, ALU.mult))
    for k in (15, 13, 11, 9, 7, 5, 3):
        steps(dve.scalar_tensor_tensor(out=p, in0=p, scalar=1.0 / k, in1=z2, op0=ALU.add, op1=ALU.mult))
    steps(dve.scalar_tensor_tensor(out=p, in0=p, scalar=1.0, in1=z, op0=ALU.add, op1=ALU.mult))
    steps(dve.tensor_scalar(p, p, 2.0, None, ALU.mult))


def backbone(nc, hT0, cols_in, consts_in, mod_w, ev_in, ev_out, even_in, od, w_uq,
             w_uk, w_uv, od_out, peer_q, peer_keys, peer_u, peer_v, out):
    with ExitStack() as ctx:
        def sb(name, shape, dt=F32):
            return ctx.enter_context(nc.sbuf_tensor(name, shape, dt))

        phase_sems = []

        def sem(name):
            phase_sems.append(nc.alloc_semaphore(name=name))
            return phase_sems[-1]

        def end_phase():
            nc.clear_and_free_semaphores(phase_sems)
            nc.all_engine_barrier()
            phase_sems.clear()

        ps = ctx.enter_context(nc.psum_tensor("banks", [P, 8, 512], F32))

        hT = sb("hT", [P, KT, T])
        uT = sb("uT", [P, KT, T])
        cols = sb("cols", [P, N_COLS])
        consts = sb("consts", [P, N_CONSTS])
        ones = sb("ones", [P, P])
        modc = sb("modc", [P, 2, N_MOD, KT, 2])
        gain = sb("gain", [P, 2, 2, KT, 2])
        squares = sb("squares", [P, 2, T])
        rms = sb("rms", [P, T])

        def col(name):
            return field(cols, COLS, name)

        def const(name):
            return field(consts, CONSTS, name)

        ident = const("ident")
        loaded = sem("tables_loaded")
        ones_set = sem("ones_set")
        dve_steps = sem("even_dve_steps")
        act_steps = sem("even_act_steps")

        even_stack = ExitStack()

        def esb(name, shape):
            return even_stack.enter_context(nc.sbuf_tensor(name, shape, F32))

        w_in = esb("ev_w_in", [P, 7, KT, 2 * P])
        even_w = esb("even_w", [P, N_EVEN])
        silu = esb("silu", [P, KT, 2])
        mod_ring = esb("mod_ring", [P, MOD_RING, KT, PIECE_J * P])
        mod_rows = esb("mod_rows", [2, 2, PIECE_J * P])
        mixer = esb("even_mixer", [P, 10908])

        def view(base, at, *shape):
            n = math.prod(shape)
            names = "abcd"[:len(shape)]
            return base[:, at:at + n].rearrange(
                f"p ({' '.join(names)}) -> p {' '.join(names)}",
                **{x: s for x, s in zip(names, shape)}), at + n

        at = 0
        xpad, at = view(mixer, at, RG_H, 2, SEG + CONV_W - 1)
        decay_fwd, _ = view(mixer, 0, RG_H, T)
        xc, at = view(mixer, at, RG_H, T)
        gate, at = view(mixer, at, RG_H, T)
        w_out, _ = view(mixer, 0, KT, D)
        xf, at = view(mixer, at, 2, T)
        dft_w, at = view(mixer, at, 2, 2, P)
        sp, at = view(mixer, at, 8, 2 * RG_H)
        half_b, at = view(mixer, at, 2, 2 * RG_H)
        assert at <= 10908 and KT * D <= RG_H * (2 * (SEG + CONV_W - 1) + 2 * T)
        w_in_flat = w_in[:, :, :, :].rearrange("p a b c -> p (a b c)")
        at = 0
        root, at = view(w_in_flat, at, RG_H, T)
        h_fwd, at = view(w_in_flat, at, RG_H, T)
        assert at <= (RG_H // 2) * KT * 2 * P
        h_back, at = view(w_in_flat, at, RG_H, T)
        decay_back, at = view(w_in_flat, at, RG_H, T)
        xw, at = view(w_in_flat, at, 4, 2, 2 * P)
        mixT = uT
        segs = [slice(0, SEG), slice(SEG, T)]
        BANK = [1, 2, 3, 4]
        FIRST = 2 * 2
        UNITS0 = [("proj", j) for j in range(RG_H + 1)]
        for h in range(RG_H):
            UNITS0 += [("gate", 0, h, 0), ("gate", 0, h, 1), ("proj", RG_H + 1 + h)]
        UNITS0 += [("proj", EV_J - 1)] + [("chan", n) for n in range(8)] + [("time", n) for n in range(4)]
        UNITS0 += [("gate", 1, h, kind) for h in range(RG_H) for kind in range(2)]
        unit0 = {u: n + 1 for n, u in enumerate(UNITS0)}
        AFTER = {("proj", RG_H + 1 + i): 1 for i in range(RG_H + 1)}
        AFTER.update({("chan", 7): 1, ("time", 3): 1, ("gate", 1, 2, 1): 2})

        piece_loaded = [sem(f"mod_piece_loaded{r}") for r in range(MOD_RING)]
        rows_out, rows_taken, mod_turned = sem("mod_rows_out"), sem("mod_rows_taken"), sem("mod_turned")
        w_in_loaded = [sem(f"ev_w_in_loaded{c}") for c in range(7)]
        w_out_loaded = sem("ev_w_out_loaded")
        h_loaded, even_w_loaded = sem("hT_loaded"), sem("even_w_loaded")
        consts_loaded = sem("consts_loaded")
        cond_tanh, silu_ready, mod_ready = sem("cond_tanh"), sem("silu_ready"), sem("mod_ready")
        mix0 = Norm("mix0", sem, lambda d: hT[:, d, :], squares, ps[:, 0, :], rms[:],
                    lambda d: uT[:, d, :], T, KT)
        unit0_out, unit0_taken = sem("even_unit_out"), sem("even_unit_taken")
        pads_set = sem("even_pads_set")
        xc_ready = sem("xc_ready")
        lam_exp, lam_abs, sp_ready = sem("lam_exp"), sem("lam_abs"), sem("softplus_ready")
        roots, root_used = sem("rg_roots"), sem("rg_root_used")
        small_product, dft_w_ready = sem("dft_w_product"), sem("dft_w_ready")
        mix_ready = sem("rg_mix_ready")
        even_out, even_added = sem("even_out_product"), sem("even_added")

        mod_ps = ps[:, 7, 0:2 * N_MOD * KT * 2]
        rows_ps = [ps[0:2, 5, :], ps[0:2, 6, :]]
        GROUP = RG_H // 2

        with nc.Block() as block:
            @block.sync
            def _(sp_eng):
                def piece(i):
                    if i >= MOD_RING:
                        sp_eng.wait_ge(rows_out, i + 1 - MOD_RING)
                    sp_eng.dma_start(mod_ring[:, i % MOD_RING], mod_w[i]).then_inc(
                        piece_loaded[i % MOD_RING], 16)

                sp_eng.dma_start(cols[:], cols_in).then_inc(loaded, 16)
                piece(0)
                piece(1)
                sp_eng.dma_start(hT[:], hT0).then_inc(h_loaded, 16)
                sp_eng.dma_start(consts[:], consts_in).then_inc(consts_loaded, 16)
                for c in range(7):
                    if c in (0, 1):
                        piece(2 + c)
                    sp_eng.dma_start(w_in[:, c], ev_in[c]).then_inc(w_in_loaded[c], 16)
                    if c == 2:
                        sp_eng.dma_start(even_w[:], even_in).then_inc(even_w_loaded, 16)
                for i in range(FIRST, PIECES):
                    piece(i)
                sp_eng.wait_ge(mix_ready, RG_H)
                sp_eng.dma_start(w_out, ev_out).then_inc(w_out_loaded, 16)

            @block.scalar
            def _(act):
                steps = Steps(act, act_steps)

                def take_rows(i):
                    act.wait_ge(rows_out, i + 1)
                    act.activation(mod_rows[:, i % 2], rows_ps[i % 2], ACT.Copy).then_inc(rows_taken, 1)

                act.wait_ge(loaded, 16)
                act.activation(silu[:], col("cond"), ACT.Tanh, scale=0.5).then_inc(cond_tanh, 1)
                act.wait_ge(lam_abs, 1)
                act.activation(sp[:, 1], sp[:, 1], ACT.Exp, scale=-1.0).then_inc(lam_exp, 1)
                take_rows(0)
                take_rows(1)
                act.wait_ge(h_loaded, 16)
                mix0.act_squares(act)
                take_rows(2)
                take_rows(3)
                mix0.act_root(act)
                act.wait_ge(mod_ready, 1)
                mix0.act_affine(act, segs, lambda d, s: gain[:, 0, 0, d, s:s + 1],
                                lambda d, s: modc[:, 0, 0, d, s:s + 1])
                act.wait_ge(pads_set, 1)
                act.wait_ge(sp_ready, 1)
                next_piece = FIRST
                for n, (kind, i, *rest) in enumerate(UNITS0):
                    act.wait_ge(unit0_out, n + 1)
                    bank = ps[:, BANK[n % 4], :]
                    if kind == "proj" and i < RG_H:
                        act.activation(xpad[:, i, :, 2:2 + SEG], bank.rearrange("p (s t) -> p s t", s=2),
                                       ACT.Copy).then_inc(unit0_taken, 1)
                    elif kind == "proj" and i < 2 * RG_H:
                        act.activation(gate[:, i - RG_H], bank, ACT.Gelu_apprx_tanh).then_inc(unit0_taken, 1)
                    elif kind == "proj":
                        act.activation(xf[:, i - 2 * RG_H], bank, ACT.Copy).then_inc(unit0_taken, 1)
                    elif kind == "chan":
                        act.activation(xw[:, i % 4, i // 4], bank[:, 0:2 * P], ACT.Copy).then_inc(unit0_taken, 1)
                    elif kind == "time":
                        act.activation(mixT[:, RG_H + i // 2, segs[i % 2]], bank[:, 0:SEG], ACT.Identity,
                                       bias=col("fn_b")[:, i // 2:i // 2 + 1]).then_inc(unit0_taken, 1)
                    else:
                        d, (h, which) = i, rest
                        c = RG_H * d + h
                        if d == 1 and which == 0:
                            act.wait_ge(root_used, h // GROUP + 1)
                        if which == 0:
                            act.activation(root[:, h], bank, ACT.Tanh, scale=0.5,
                                           bias=half_b[:, 0, c:c + 1]).then_inc(unit0_taken, 1)
                            act.wait_ge(unit0_taken, n + 1)
                            to = decay_fwd if d == 0 else decay_back
                            steps(act.activation(to[:, h], root[:, h], ACT.Exp,
                                                 scale=sp[:, 6, c:c + 1], bias=sp[:, 6, c:c + 1]))
                            steps(act.activation(root[:, h], root[:, h], ACT.Tanh,
                                                 scale=sp[:, 7, c:c + 1], bias=sp[:, 7, c:c + 1]))
                        else:
                            act.activation((h_fwd if d == 0 else h_back)[:, h], bank, ACT.Tanh, scale=0.5,
                                           bias=half_b[:, 1, c:c + 1]).then_inc(unit0_taken, 1)
                            if h % GROUP == GROUP - 1:
                                hs = root[:, h + 1 - GROUP:h + 1]
                                act.activation(hs, hs, ACT.Sqrt, scale=0.25).then_inc(roots, 1)
                    for _ in range(AFTER.get(UNITS0[n], 0)):
                        take_rows(next_piece)
                        next_piece += 1
                for i in range(next_piece, PIECES):
                    take_rows(i)

            @block.vector
            def _(dve):
                steps = Steps(dve, dve_steps)
                dve.memset(ones[:], 1.0).then_inc(ones_set, 1)
                dve.wait_ge(cond_tanh, 1)
                steps(dve.scalar_tensor_tensor(out=silu[:], in0=silu[:], scalar=1.0, in1=col("cond"),
                                               op0=ALU.add, op1=ALU.mult))
                dve.tensor_scalar(silu[:], silu[:], 0.5, None, ALU.mult).then_inc(silu_ready, 1)
                lam = col("rg_lam").rearrange("p d h -> p (d h)")
                steps(dve.tensor_scalar(sp[:, 0], lam, -1.0, 0.0, ALU.mult, ALU.max))
                dve.scalar_tensor_tensor(out=sp[:, 1], in0=lam, scalar=-1.0, in1=lam, op0=ALU.mult,
                                         op1=ALU.max).then_inc(lam_abs, 1)
                for n, b in enumerate(("rg_ba", "rg_bx")):
                    steps(dve.tensor_scalar(half_b[:, n], col(b).rearrange("p d h -> p (d h)"), 0.5,
                                            None, ALU.mult))
                steps(dve.memset(xpad[:, :, :, 0:2], 0.0))
                steps(dve.memset(dft_w[:], 0.0))
                dve.memset(xpad[:, :, :, 2 + SEG:], 0.0).then_inc(pads_set, 1)
                dve.wait_ge(lam_exp, 1)
                softplus_tail(dve, steps, sp[:, 1], sp[:, 2], sp[:, 3], sp[:, 4])
                steps(dve.tensor_tensor(sp[:, 4], sp[:, 4], sp[:, 0], ALU.add))
                steps(dve.tensor_scalar(sp[:, 6], sp[:, 4], -4.0, None, ALU.mult))
                dve.tensor_scalar(sp[:, 7], sp[:, 4], 2.0, None, ALU.mult).then_inc(sp_ready, 1)
                mix0.dve_mean(dve)
                mix0.dve_scale(dve, steps)

                def take_modulation(layer, which, halves):
                    size = which.stop - which.start
                    at = (layer * N_MOD + which.start) * KT
                    steps(dve.tensor_tensor(
                        modc[:, layer, which].rearrange("p w k s -> p (w k) s"),
                        mod_ps.rearrange("p (a s) -> p a s", s=2)[:, at:at + size * KT],
                        col("mod_b")[:, layer, which.start * KT:which.stop * KT].unsqueeze(2).to_broadcast(
                            [P, size * KT, 2]), ALU.add))
                    for half in halves:
                        dve.scalar_tensor_tensor(
                            out=gain[:, layer, half], in0=modc[:, layer, 3 * half + 1], scalar=1.0,
                            in1=col("norm_g")[:, layer, half].unsqueeze(2).to_broadcast([P, KT, 2]),
                            op0=ALU.add, op1=ALU.mult).then_inc(mod_ready, 1)

                dve.wait_ge(mod_turned, FIRST)
                take_modulation(0, slice(0, 2), (0,))
                dve.wait_ge(pads_set, 1)
                w = col("rg_conv_w")
                for h in range(RG_H):
                    dve.wait_ge(unit0_taken, unit0["proj", h])
                    at = xc[:, h].rearrange("p (s t) -> p s t", s=2)
                    steps(dve.tensor_scalar(at, xpad[:, h, :, 0:SEG], w[:, h, 0:1],
                                            col("rg_conv_b")[:, h:h + 1], ALU.mult, ALU.add))
                    for i in range(1, CONV_W):
                        last = dve.scalar_tensor_tensor(out=at, in0=xpad[:, h, :, i:i + SEG],
                                                        scalar=w[:, h, i:i + 1], in1=at, op0=ALU.mult,
                                                        op1=ALU.add)
                        if i < CONV_W - 1:
                            steps(last)
                    last.then_inc(xc_ready, 1)
                dve.wait_ge(small_product, 1)
                small = ps[:, 0, 0:256].rearrange("p (j m e) -> p j m e", j=2, m=2)
                for g in range(2):
                    rows = slice(64 * g, 64 * g + 64)
                    dve.tensor_copy(dft_w[rows, :, :, 64 * g:64 * g + 64], small[rows]).then_inc(dft_w_ready, 1)

                def direction(d, group):
                    hs = slice(GROUP * group, GROUP * group + GROUP)
                    state, decay = (h_fwd, decay_fwd) if d == 0 else (h_back, decay_back)
                    dve.wait_ge(unit0_taken, unit0["gate", d, hs.stop - 1, 1])
                    steps(dve.scalar_tensor_tensor(out=state[:, hs], in0=state[:, hs], scalar=1.0,
                                                   in1=xc[:, hs], op0=ALU.add, op1=ALU.mult))
                    dve.wait_ge(roots, 2 * d + group + 1)
                    dve.tensor_tensor(state[:, hs], state[:, hs], root[:, hs], ALU.mult).then_inc(root_used, 1)
                    dve.wait_ge(root_used, 2 * d + group + 1)
                    steps(dve.scalar_tensor_tensor(out=state[:, hs], in0=decay[:, hs], scalar=1.0,
                                                   in1=state[:, hs], op0=ALU.add, op1=ALU.mult))
                    for h in range(hs.start, hs.stop):
                        if d == 0:
                            steps(dve.tensor_tensor_scan(out=state[:, h], data0=decay[:, h],
                                                         data1=state[:, h], initial=0.0,
                                                         op0=ALU.mult, op1=ALU.add))
                        else:
                            for s, first in ((0, 0.0), (1, state[:, h, 0:1])):
                                at = state[:, h, segs[s]][:, ::-1]
                                steps(dve.tensor_tensor_scan(
                                    out=at, data0=decay[:, h, segs[s]][:, ::-1], data1=at,
                                    initial=first, op0=ALU.mult, op1=ALU.add))

                for d in range(2):
                    for group in range(2):
                        direction(d, group)
                for h in range(RG_H):
                    steps(dve.tensor_tensor(h_back[:, h], h_back[:, h], h_fwd[:, h], ALU.add))
                    dve.tensor_tensor(mixT[:, h], h_back[:, h], gate[:, h], ALU.mult).then_inc(mix_ready, 1)
                dve.wait_ge(mod_turned, PIECES)
                take_modulation(0, slice(2, N_MOD), (1,))
                take_modulation(1, slice(0, N_MOD), (0, 1))
                for n in range(KT):
                    dve.wait_ge(even_out, n + 1)
                    for s in range(2):
                        last = dve.scalar_tensor_tensor(
                            out=hT[:, n, segs[s]], in0=ps[:, BANK[n % 4], segs[s]],
                            scalar=modc[:, 0, 2, n, s:s + 1], in1=hT[:, n, segs[s]], op0=ALU.mult,
                            op1=ALU.add)
                    last.then_inc(even_added, 1)

            @block.tensor
            def _(pe):
                def turn_rows(i):
                    pe.wait_ge(rows_taken, i + 1)
                    for jj in range(PIECE_J):
                        at = 2 * (PIECE_J * i + jj)
                        last = pe.transpose(mod_ps[:, at:at + 2], mod_rows[:, i % 2, jj * P:(jj + 1) * P],
                                            ident[0:2, 0:2])
                    last.then_inc(mod_turned, 1)

                def piece(i):
                    pe.wait_ge(piece_loaded[i % MOD_RING], 16 * (i // MOD_RING + 1))
                    if i >= 2:
                        pe.wait_ge(rows_taken, i - 1)
                    for k in range(KT):
                        last = pe.matmul(rows_ps[i % 2], silu[:, k], mod_ring[:, i % MOD_RING, k],
                                         start=(k == 0), stop=(k == KT - 1))
                    last.then_inc(rows_out, 1)
                    if i not in (0, FIRST):
                        turn_rows(i - 1)

                pe.wait_ge(silu_ready, 1)
                pe.wait_ge(consts_loaded, 16)
                for i in range(FIRST):
                    piece(i)
                    if i == 1:
                        pe.wait_ge(ones_set, 1)
                        mix0.pe_sums(pe, ones[:])
                turn_rows(FIRST - 1)
                pe.wait_ge(even_w_loaded, 16)
                pe.wait_ge(mix0.mean, 1)
                for j in range(2):
                    for m in range(2):
                        last = pe.matmul(ps[:, 0, (2 * j + m) * 64:(2 * j + m) * 64 + 64],
                                         const("chan_dft")[:, m], field(even_w, EVEN, "fn_w")[:, j],
                                         start=True, stop=True)
                last.then_inc(small_product, 1)
                rg_w = field(even_w, EVEN, "rg_w")
                next_piece = FIRST
                for n, (kind, i, *rest) in enumerate(UNITS0):
                    bank = ps[:, BANK[n % 4], :]
                    if n >= 4:
                        pe.wait_ge(unit0_taken, n - 3)
                    if kind == "proj":
                        if i % 2 == 0:
                            pe.wait_ge(w_in_loaded[i // 2], 16)
                        for k in range(KT):
                            if i == 0:
                                pe.wait_ge(mix0.ready, k + 1)
                            last = pe.matmul(bank, w_in[:, i // 2, k, i % 2 * P:i % 2 * P + P], uT[:, k],
                                             start=(k == 0), stop=(k == KT - 1))
                    elif kind == "gate":
                        h, which = rest
                        if (i, which) == (0, 0):
                            pe.wait_ge(xc_ready, h + 1)
                        last = pe.matmul(bank, rg_w[:, which, i, h], xc[:, h], start=True, stop=True)
                    elif kind == "chan":
                        if i == 0:
                            pe.wait_ge(dft_w_ready, 2)
                            pe.wait_ge(unit0_taken, unit0["proj", EV_J - 1])
                        j, tt = i // 4, i % 4
                        last = pe.matmul(bank[:, 0:2 * P], xf[:, j, tt * P:(tt + 1) * P],
                                         dft_w[:, j].rearrange("p m e -> p (m e)"), start=True, stop=True)
                    else:
                        if i == 0:
                            pe.wait_ge(unit0_taken, unit0["chan", 7])
                        j, s = i // 2, i % 2
                        for tl in range(2):
                            for m in range(2):
                                last = pe.matmul(bank[:, 0:SEG], xw[:, 2 * s + tl, j, m * P:(m + 1) * P],
                                                 const("time_dft")[:, m, tl], start=(tl + m == 0),
                                                 stop=(tl + m == 2))
                    last.then_inc(unit0_out, 1)
                    for _ in range(AFTER.get(UNITS0[n], 0)):
                        piece(next_piece)
                        next_piece += 1
                for i in range(next_piece, PIECES):
                    piece(i)
                turn_rows(PIECES - 1)
                pe.wait_ge(unit0_taken, len(UNITS0))
                pe.wait_ge(w_out_loaded, 16)
                pe.wait_ge(mix_ready, RG_H)
                for n in range(KT):
                    if n >= 4:
                        pe.wait_ge(even_added, n - 3)
                    for k in range(KT):
                        last = pe.matmul(ps[:, BANK[n % 4], :], w_out[:, k, n * P:(n + 1) * P], mixT[:, k],
                                         start=(k == 0), stop=(k == KT - 1))
                    last.then_inc(even_out, 1)
        even_stack.close()
        end_phase()

        def peer(layer, first_token, tiles):
            name = f"peer{layer}"
            stack = ExitStack()

            def psb(what, shape, dt=F32):
                return stack.enter_context(nc.sbuf_tensor(f"{name}_{what}", shape, dt))

            def psem(what):
                return sem(f"{name}_{what}")

            segments = segs if first_token == 0 else [slice(0, SEG)]
            seg_of = 0 if first_token == 0 else 1
            n_tokens = tiles * P
            w_q = psb("w_q", [P, 4, KT, 4 * P])
            keys = psb("keys", [P, PH, 2, NK])
            u_rows = psb("u_rows", [P, U_RING, D])
            v_rows = psb("v_rows", [P, V_RING, D])
            diag = psb("diag", [P, TOPK, P])
            xs = psb("xs", [P, KT, P])
            q_sb = psb("q", [P, 2, P])
            scores = psb("scores", [P, PH, 2, NK])
            vals = psb("vals", [P, 2, TOPK])
            ids = psb("ids", [P, 2, TOPK], U32)
            ids_f = psb("ids_f", [P, 2, TOPK])
            sums = psb("sums", [P, TOPK, TOPK])
            top = psb("top", [P, TOPK])
            pos = psb("pos", [P, TOPK], U32)
            pair = psb("pair", [P, 2, TOPK], U32)
            pair_f = psb("pair_f", [P, 2, TOPK])
            hot = psb("hot", [P, 2, TOPK, TOPK])
            picked = psb("picked", [P, 2, TOPK])
            expert = psb("expert", [P, PH, TOPK], I32)
            soft = psb("soft", [P, 2, TOPK + 4])
            g_half = psb("g_half", [P, TOPK])
            dot = psb("dot", [P, 2, TOPK])
            gelu_t = psb("gelu_t", [P, 2, TOPK])
            xg = psb("xg", [P, TOPK])
            weight = psb("weight", [P, PH, TOPK])

            w_q_loaded = [psem(f"w_q_loaded{c}") for c in range(4)]
            keys_loaded = psem("keys_loaded")
            u_landed = [psem(f"u_landed{r}") for r in range(U_RING)]
            v_landed = [psem(f"v_landed{r}") for r in range(V_RING)]
            turn = psem("turn")
            pause = psem("pause")
            own = psem("choice_steps")
            dve_steps = psem("dve_steps")
            staged = psem("staged")
            q_product, q_taken = psem("q_product"), psem("q_taken")
            s_product, s_taken = psem("s_product"), psem("s_taken")
            scores_used = psem("scores_used")
            soft_in, soft_out = psem("soft_in"), psem("soft_out")
            expert_ready = psem("expert_ready")
            dots_done = psem("dots_done")
            gelu_in, gelu_out = psem("gelu_in"), psem("gelu_out")
            weight_ready = psem("weight_ready")
            diag_ready = psem("diag_ready")
            v_added = psem("v_added")
            f_ready = psem("f_ready")
            sum_taken = psem("sum_taken")
            y_turned = psem("y_turned")
            y_added = psem("y_added")

            f_tok = ps[:, 0:2, :].rearrange("p a b -> p (a b)")
            acc = ps[:, 2:4, :]
            q_ps, s_ps = ps[:, 4, 0:2 * P], ps[:, 5, 0:2 * NK]
            norm = Norm(f"{name}_norm", sem, lambda d: hT[:, d, first_token:first_token + n_tokens],
                        squares, ps[:, 6, 0:n_tokens], rms[:, 0:n_tokens],
                        lambda d: uT[:, d, first_token:first_token + n_tokens], n_tokens, KT)

            def tokens_of(t):
                return bass.ds(t * P + first_token, P)

            with nc.Block() as block:
                @block.sync
                def _(sp_eng):
                    for c in range(4):
                        sp_eng.dma_start(w_q[:, c], peer_q[layer, c]).then_inc(w_q_loaded[c], 16)
                        if c == 0:
                            sp_eng.dma_start(keys[:], peer_keys[layer]).then_inc(keys_loaded, 16)

                @block.gpsimd
                def _(pool):
                    def gather_u(t, s):
                        if s % TOPK == 0:
                            pool.wait_ge(expert_ready, t * PH + (s // TOPK + 1))
                            pool.sem_inc(turn, 1)
                        pool.wait_ge(dots_done, t * SLOTS + (s + 1))
                        pool.sem_inc(turn, 1)
                        pool.indirect_dma_start(
                            out=u_rows[:, s % U_RING, :], out_offset=None, in_=peer_u[layer],
                            in_offset=bass.IndirectOffsetOnAxis(
                                ap=expert[:, s // TOPK, s % TOPK:s % TOPK + 1], axis=0)
                        ).then_inc(u_landed[s % U_RING], 16)

                    def gather_v(t, s):
                        pool.wait_ge(v_added, t * SLOTS + (s + 1 + SLOTS - V_RING))
                        pool.sem_inc(turn, 1)
                        pool.indirect_dma_start(
                            out=v_rows[:, s % V_RING, :], out_offset=None, in_=peer_v[layer],
                            in_offset=bass.IndirectOffsetOnAxis(
                                ap=expert[:, s // TOPK, s % TOPK:s % TOPK + 1], axis=0)
                        ).then_inc(v_landed[s % V_RING], 16)

                    def tile(t, more):
                        for s in range(SLOTS):
                            if s + LAG < SLOTS:
                                gather_u(t, s + LAG)
                            elif more:
                                gather_u(t + 1, s + LAG - SLOTS)
                            gather_v(t, s)

                    for s in range(LAG):
                        gather_u(0, s)
                    with pool.Fori(0, tiles - 1) as t:
                        tile(t, True)
                    tile(tiles - 1, False)

                @block.scalar
                def _(act):
                    norm.act_squares(act)
                    norm.act_root(act)
                    norm.act_affine(act, segments,
                                    lambda d, s: gain[:, layer, 1, d, s + seg_of:s + seg_of + 1],
                                    lambda d, s: modc[:, layer, 3, d, s + seg_of:s + seg_of + 1])

                    def stage(t):
                        act.activation(xs[:], uT[:, :, tokens_of(t)], ACT.Copy).then_inc(staged, 1)

                    def take_q(n):
                        act.wait_ge(q_product, n + 1)
                        act.activation(q_sb[:].rearrange("p a b -> p (a b)"), q_ps, ACT.Copy).then_inc(q_taken, 1)

                    def take_scores(n, h):
                        act.wait_ge(scores_used, n + 1)
                        act.wait_ge(s_product, n + 1)
                        act.activation(scores[:, h].rearrange("p a b -> p (a b)"), s_ps, ACT.Copy).then_inc(s_taken, 1)

                    def soften(n, i):
                        act.wait_ge(soft_in, n + 1)
                        act.activation(soft[:, i, 0:TOPK], top[:], ACT.Exp, bias=soft[:, i, TOPK:TOPK + 1],
                                       accum_out=soft[:, i, TOPK + 1:TOPK + 2]).then_inc(soft_out, 1)

                    def tile(t, more):
                        for j in range(PH):
                            if j == 4 and more:
                                act.wait_ge(q_product, t * PH + PH)
                                act.wait_ge(f_ready, t + 1)
                                stage(t + 1)
                            act.wait_ge(gelu_in, t * PH + (j + 1))
                            act.activation(gelu_t[:, 1], gelu_t[:, 0], ACT.Tanh, scale=GELU_S).then_inc(gelu_out, 1)
                            for k in range(TOPK):
                                s = j * TOPK + k
                                if k == 0:
                                    act.wait_ge(weight_ready, t * PH + (j + 1))
                                if k == 3 and (j < 4 or more):
                                    take_q(t * PH + (j + 4))
                                if k == 0 and (j < 6 or more):
                                    soften(t * PH + (j + 2), j % 2)
                                if k == 6 and (j < 4 or more):
                                    take_scores(t * PH + (j + 4), (j + 4) % PH)
                                act.wait_ge(v_added, t * SLOTS + (s + 1 + SLOTS - TOPK))
                                act.activation(diag[:, k], ident, ACT.Copy,
                                               scale=weight[:, j, k:k + 1]).then_inc(diag_ready, 1)
                        act.wait_ge(v_added, t * SLOTS + 2 * SLOTS)
                        at = uT[:, :, tokens_of(t)]
                        for half in range(2):
                            last = act.activation(at[:, 4 * half:4 * half + 4, :],
                                                  acc[:, half].rearrange("p (a b) -> p a b", a=4), ACT.Copy)
                        last.then_inc(sum_taken, 1)

                    act.wait_ge(norm.ready, KT)
                    stage(0)
                    for n in range(4):
                        take_q(n)
                        take_scores(n, n)
                        if n in (1, 2):
                            soften(n - 1, n - 1)
                    with act.Fori(0, tiles - 1) as t:
                        tile(t, True)
                    tile(tiles - 1, False)

                @block.vector
                def _(dve):
                    steps = Steps(dve, dve_steps)
                    dve.sem_inc(dots_done, U_RING)
                    dve.sem_inc(scores_used, PH)
                    norm.dve_mean(dve)
                    norm.dve_scale(dve, steps)

                    def choice(chain, k, n, h, behind=True):
                        halves = [(scores[:, h, i], vals[:, i], ids[:, i]) for i in range(2)]
                        grid = sums[:].rearrange("p a b -> p (a b)")
                        full = [P, 2, TOPK, TOPK]
                        if k == 0:
                            dve.wait_ge(s_taken, n + 1)
                            dve.wait_ge(v_added, n * TOPK + TOPK)
                            dve.sem_inc(pause, 1)
                            for src, values, _ in halves:
                                chain(dve.max(values[:, 0:8], src))
                        elif k == 1:
                            for src, values, places in halves:
                                chain(dve.max_index(places[:, 0:8], values[:, 0:8], src))
                        elif k == 2:
                            for src, values, _ in halves:
                                chain(dve.match_replace(src, values[:, 0:8], src, NEG))
                        elif k == 3:
                            for src, values, _ in halves:
                                chain(dve.max(values[:, 8:16], src))
                        elif k == 4:
                            chain(dve.max_index(ids[:, 0, 8:16], vals[:, 0, 8:16], scores[:, h, 0]))
                            dve.max_index(ids[:, 1, 8:16], vals[:, 1, 8:16],
                                          scores[:, h, 1]).then_inc(scores_used, 1)
                        elif k == 5:
                            dve.wait_ge(scores_used, n + (PH + 1))
                            if behind:
                                dve.wait_ge(soft_out, n)
                            chain(dve.tensor_tensor(
                                sums[:], vals[:, 0].unsqueeze(2).to_broadcast([P, TOPK, TOPK]),
                                vals[:, 1].unsqueeze(1).to_broadcast([P, TOPK, TOPK]), ALU.add))
                        elif k == 6:
                            chain(dve.max(top[:, 0:8], grid))
                        elif k == 7:
                            chain(dve.max_index(pos[:, 0:8], top[:, 0:8], grid))
                            chain(dve.tensor_scalar(soft[:, h % 2, TOPK:TOPK + 1], top[:, 0:1], -1.0,
                                                    None, ALU.mult))
                        elif k == 8:
                            chain(dve.match_replace(grid, top[:, 0:8], grid, NEG))
                        elif k == 9:
                            chain(dve.max(top[:, 8:16], grid))
                        elif k == 10:
                            dve.tensor_copy(ids_f[:], ids[:]).then_inc(soft_in, 1)
                            chain(dve.max_index(pos[:, 8:16], top[:, 8:16], grid))
                        elif k == 11:
                            chain(dve.tensor_single_scalar(pair[:, 0], pos[:], 4, ALU.logical_shift_right))
                            chain(dve.tensor_single_scalar(pair[:, 1], pos[:], TOPK - 1, ALU.bitwise_and))
                        elif k == 12:
                            chain(dve.tensor_copy(pair_f[:], pair[:]))
                        elif k == 13:
                            chain(dve.tensor_tensor(
                                hot[:], pair_f[:].unsqueeze(3).to_broadcast(full),
                                const("iota").unsqueeze(1).unsqueeze(1).to_broadcast(full), ALU.is_equal))
                        elif k == 14:
                            dve.wait_ge(soft_in, n + 1)
                            chain(dve.tensor_tensor(hot[:], hot[:], ids_f[:].unsqueeze(2).to_broadcast(full), ALU.mult))
                        else:
                            chain(dve.tensor_reduce(picked[:], hot[:], AX, ALU.add))
                            dve.scalar_tensor_tensor(out=expert[:, h], in0=picked[:, 0], scalar=float(NK),
                                                     in1=picked[:, 1], op0=ALU.mult,
                                                     op1=ALU.add).then_inc(expert_ready, 1)

                    def weigh(t, j):
                        dve.wait_ge(gelu_out, t * PH + (j + 1))
                        dve.scalar_tensor_tensor(out=weight[:, j], in0=gelu_t[:, 1], scalar=1.0, in1=xg[:],
                                                 op0=ALU.add, op1=ALU.mult).then_inc(weight_ready, 1)

                    def tile(chain, t, more):
                        for j in range(PH):
                            if j == 0:
                                dve.wait_ge(f_ready, t + 1)
                            for k in range(TOPK):
                                s = j * TOPK + k
                                r = s % U_RING
                                dve.wait_ge(u_landed[r], t * (16 * SLOTS // U_RING) + 16 * (s // U_RING + 1))
                                dve.tensor_tensor_reduce(
                                    out=u_rows[:, r], in0=u_rows[:, r], in1=f_tok, scale=1.0, scalar=0.0,
                                    op0=ALU.mult, op1=ALU.add,
                                    accum_out=dot[:, j % 2, k:k + 1]).then_inc(dots_done, 1)
                                if k == 1 and j > 0:
                                    weigh(t, j - 1)
                                if k == 12:
                                    dve.wait_ge(soft_out, t * PH + (j + 1))
                                    chain(dve.reciprocal(soft[:, j % 2, TOPK + 2:TOPK + 3],
                                                         soft[:, j % 2, TOPK + 1:TOPK + 2]))
                                if k == 13:
                                    chain(dve.tensor_scalar(g_half[:], soft[:, j % 2, 0:TOPK],
                                                            soft[:, j % 2, TOPK + 2:TOPK + 3], 0.5,
                                                            ALU.mult, ALU.mult))
                                if j < 6 or more:
                                    choice(chain, k, t * PH + (j + 2), (j + 2) % PH)
                            dve.wait_ge(dots_done, t * SLOTS + ((j + 1) * TOPK + U_RING))
                            d = dot[:, j % 2]
                            chain(dve.tensor_tensor(gelu_t[:, 0], d, d, ALU.mult))
                            chain(dve.tensor_scalar(gelu_t[:, 0], gelu_t[:, 0], GELU_C, 1.0, ALU.mult, ALU.add))
                            dve.tensor_tensor(gelu_t[:, 0], gelu_t[:, 0], d, ALU.mult).then_inc(gelu_in, 1)
                            chain(dve.tensor_tensor(xg[:], d, g_half[:], ALU.mult))
                            if j == PH - 1:
                                weigh(t, j)

                    chain = Steps(dve, own)
                    for n in range(2):
                        for k in range(TOPK):
                            choice(chain, k, n, n, behind=n > 0)
                    with dve.Fori(0, tiles - 1) as t:
                        dve.sem_clear(own)
                        tile(Steps(dve, own), t, True)
                    dve.sem_clear(own)
                    tile(Steps(dve, own), tiles - 1, False)
                    for t in range(tiles):
                        for d in range(KT):
                            dve.wait_ge(y_turned, t * 2 + d // 4 + 1)
                            at = hT[:, d, first_token + t * P:first_token + (t + 1) * P]
                            side = seg_of + t // 2
                            last = dve.scalar_tensor_tensor(
                                out=at, in0=ps[:, 4 + (2 * t + d // 4) % 4, d % 4 * P:d % 4 * P + P],
                                scalar=modc[:, layer, 5, d, side:side + 1], in1=at, op0=ALU.mult,
                                op1=ALU.add)
                            if d % 4 == 3:
                                last.then_inc(y_added, 1)

                @block.tensor
                def _(pe):
                    pe.sem_inc(v_added, SLOTS)
                    pe.sem_inc(sum_taken, 1)
                    norm.pe_sums(pe, ones[:])

                    def query(n, h, free):
                        if free is not None:
                            pe.wait_ge(q_taken, free)
                        for half in range(2):
                            hp = 2 * h + half
                            for k in range(KT):
                                last = pe.matmul(q_ps[:, half * P:half * P + P],
                                                 w_q[:, hp // 4, k, hp % 4 * P:hp % 4 * P + P], xs[:, k],
                                                 start=(k == 0), stop=(k == KT - 1))
                        last.then_inc(q_product, 1)

                    def score(n, h, free):
                        pe.wait_ge(q_taken, n + 1)
                        if free is not None:
                            pe.wait_ge(s_taken, free)
                        for half in range(2):
                            last = pe.matmul(s_ps[:, half * NK:half * NK + NK], q_sb[:, half], keys[:, h, half],
                                             start=True, stop=True)
                        last.then_inc(s_product, 1)

                    def by_token(t):
                        for d in range(KT):
                            last = pe.transpose(f_tok[:, d * P:(d + 1) * P], xs[:, d], ident)
                        last.then_inc(f_ready, 1)

                    def tile(t, more):
                        for j in range(PH):
                            for k in range(TOPK):
                                s = j * TOPK + k
                                r = s % V_RING
                                if s == 0:
                                    pe.wait_ge(sum_taken, t + 1)
                                pe.wait_ge(v_landed[r], t * (16 * SLOTS // V_RING) + 16 * (s // V_RING + 1))
                                pe.wait_ge(diag_ready, t * SLOTS + (s + 1))
                                for half in range(2):
                                    last = pe.matmul(acc[:, half], diag[:, k], v_rows[:, r, half * 512:half * 512 + 512],
                                                     start=(s == 0), stop=(s == SLOTS - 1))
                                last.then_inc(v_added, 1)
                                if k == 2 and (j < 4 or more):
                                    if j == 5:
                                        pe.wait_ge(staged, t + 2)
                                    query(t * PH + (j + 4), (j + 4) % PH, t * PH + (j + 4))
                                if k == 5 and (j < 4 or more):
                                    score(t * PH + (j + 4), (j + 4) % PH, t * PH + (j + 4))
                            if j == 6 and more:
                                pe.wait_ge(dots_done, t * SLOTS + (SLOTS + U_RING))
                                by_token(t + 1)

                    pe.wait_ge(staged, 1)
                    pe.wait_ge(keys_loaded, 16)
                    by_token(0)
                    for n in range(4):
                        pe.wait_ge(w_q_loaded[n // 2], 16)
                        query(n, n, n if n else None)
                        score(n, n, n if n else None)
                    for c in (2, 3):
                        pe.wait_ge(w_q_loaded[c], 16)
                    with pe.Fori(0, tiles - 1) as t:
                        tile(t, True)
                    tile(tiles - 1, False)
                    pe.wait_ge(sum_taken, tiles + 1)
                    for n in range(2 * tiles):
                        if n >= 4:
                            pe.wait_ge(y_added, n - 3)
                        t = n // 2
                        for i in range(4):
                            last = pe.transpose(
                                ps[:, 4 + n % 4, i * P:i * P + P],
                                uT[:, n % 2 * 4 + i, first_token + t * P:first_token + (t + 1) * P], ident)
                        last.then_inc(y_turned, 1)
                    pe.wait_ge(y_added, 2 * tiles)
            stack.close()
            end_phase()

        peer(0, 0, T // P)
        odd_stack = ExitStack()

        def osb(name, shape):
            return odd_stack.enter_context(nc.sbuf_tensor(name, shape, F32))

        N_LAT = SEG
        width = dict(ODD_PARTS)
        part_at, at = {}, 0
        for part, n in ODD_PARTS:
            part_at[part] = at
            at += KT * n
        od_w = osb("od_w", [P, at])
        uq_w = osb("uq_w", [P, Q_LORA // P, MLA_H * QD])
        uk_w = osb("uk_w", [P, KV_LORA // P, MLA_H, NOPE])
        uv_w = osb("uv_w", [P, KV_LORA // P, MLA_H * VD])
        work = osb("odd_work", [P, 10600])

        def od_part(part):
            at = part_at[part]
            return od_w[:, at:at + KT * width[part]].rearrange("p (k n) -> p k n", k=KT)

        at = 0
        PADDED = SEG + CONV_W - 1
        q_pad, at = view(work, at, ML_H, PADDED)
        k_pad, at = view(work, at, ML_H, 2, PADDED)
        after_pads = at
        v_tok, at = view(work, at, T // P, ML_H * P)
        o_tanh, at = view(work, at, ML_H, N_LAT)
        cq, at = view(work, at, Q_LORA // P, N_LAT)
        ckv, at = view(work, at, KV_LORA // P, T)
        k_rot, at = view(work, at, T)
        v_att, at = view(work, at, T // P, MLA_H * VD)
        g_in, g_forget = squares[:, 0], squares[:, 1]
        probs, at = view(work, 0, 2, T)
        h_sum, at = view(work, at, ML_H, N_LAT)
        cq_rms, at = view(work, at, N_LAT)
        den_abs, at = view(work, at, N_LAT)
        assert at <= after_pads
        base = part_at["v"]
        qs_ml, at = view(od_w, base, ML_H, N_LAT)
        ks_ml, at = view(od_w, at, ML_H, T)
        th, at = view(od_w, at, 2, T)
        chain_b, at = view(od_w, at, 8, T)
        assert at <= part_at["cq"]
        weights_ml, at = view(od_w, part_at["cq"], 2, T // P, N_LAT)
        k_att, at = view(od_w, at, 2, T)
        q_att, at = view(od_w, at, 2, N_LAT)
        q_raw, at = view(od_w, at, 2, N_LAT)
        q_sin, at = view(od_w, at, 2, N_LAT)
        c_col, at = view(od_w, at, T // P, HALF_ROWS)
        soft_a, at = view(od_w, at, 2, 4)
        h_rec, at = view(od_w, at, N_LAT)
        assert at <= part_at["gates"] + KT * width["gates"], at
        w_out2 = od_w[:, 0:KT * D].rearrange("p (k n) -> p k n", k=KT)
        uT_flat = uT[:].rearrange("p a b -> p (a b)")
        mix2, at = view(uT_flat, 0, KT, N_LAT)
        probs_t, at = view(uT_flat, at, 2, T // P, N_LAT)

        part_loaded = {part: sem(f"od_{part}_loaded") for part, _ in ODD_PARTS}
        mla_loaded = sem("mla_weights_loaded")
        w_out2_loaded = sem("od_out_loaded")
        mix1 = Norm("mix1", sem, lambda d: hT[:, d, :], squares, ps[:, 0, :], rms[:],
                    lambda d: uT[:, d, :], T, KT)
        kv_norm = Norm("kv_norm", sem, lambda d: ckv[:, d], squares, ps[:, 0, :], rms[:],
                       lambda d: ckv[:, d], T, KV_LORA // P)
        q_norm = Norm("q_norm", sem, lambda d: cq[:, d], squares, ps[:, 7, 0:N_LAT], cq_rms,
                      lambda d: cq[:, d], N_LAT, Q_LORA // P)
        UNITS = ([("gates", 0)] + [("k", i) for i in range(ML_H)] + [("q", i) for i in range(ML_H)]
                 + [("ckv", i) for i in range(2)] + [("krope", 0)] + [("cq", i) for i in range(3)]
                 + [("v", i) for i in range(T // P)] + [("o", i) for i in range(ML_H)])
        LAT_ONLY = ("q", "cq", "o")
        unit_done = {u: n + 1 for n, u in enumerate(UNITS)}
        unit_out, unit_taken = sem("od_unit_out"), sem("od_unit_taken")
        pads2 = sem("od_pads_set")
        forget_abs, forget_exp = sem("forget_abs"), sem("forget_exp")
        conv_done, conv_tanh, qk_ready = sem("ml_conv_done"), sem("ml_conv_tanh"), sem("ml_qk_ready")
        c_ready, c_turned, c_col_ready = sem("ml_c_ready"), sem("ml_c_turned"), sem("ml_c_col_ready")
        stab_in, stab_ready = sem("ml_stab_in"), sem("ml_stab_ready")
        key_swapped, key_ready = sem("key_swapped"), sem("key_ready")
        va_out, va_ready = sem("v_att_out"), sem("v_att_ready")
        ml_scores, ml_spread = sem("ml_scores"), sem("ml_spread")
        ml_arg, ml_exp, ml_weights = sem("ml_arg"), sem("ml_exp"), sem("ml_weights")
        ml_sums, ml_abs, ml_head = sem("ml_sums"), sem("ml_abs"), sem("ml_head")
        out_sq, out_ss, out_ms, out_root = (sem("ml_out_squares"), sem("ml_out_summed"),
                                            sem("ml_out_mean"), sem("ml_out_root"))
        ml_mixed = sem("ml_mixed")
        uq_out, q_raw_ready, q_swapped, q_ready = (sem("uq_out"), sem("q_raw_ready"),
                                                   sem("q_swapped"), sem("q_ready"))
        uk_out, k_nope_ready, k_rope_ready = sem("uk_out"), sem("k_nope_ready"), sem("k_rope_ready")
        att_scores, att_max, att_exp, att_probs = (sem("att_scores"), sem("att_max"), sem("att_exp"),
                                                   sem("att_probs"))
        att_turned, att_kept, att_out, att_mixed = (sem("att_turned"), sem("att_kept"),
                                                    sem("att_out"), sem("att_mixed"))
        odd_out, odd_added = sem("odd_out_product"), sem("odd_added")
        dve_steps, act_steps = sem("odd_dve_steps"), sem("odd_act_steps")
        LAT = slice(SEG, T)
        ML_SCALE = 0.25 * P ** -0.5
        ATT_SCALE = QD ** -0.5
        M_UNITS = 2 * ML_H

        with nc.Block() as block:
            @block.sync
            def _(sp_eng):
                for part in ("gates", "k", "q", "ckv", "krope", "cq", "v", "o"):
                    at = part_at[part]
                    sp_eng.dma_start(od_w[:, at:at + KT * width[part]],
                                     od[:, at:at + KT * width[part]]).then_inc(part_loaded[part], 16)
                sp_eng.dma_start(uv_w[:], w_uv.rearrange("p k h e -> p k (h e)")).then_inc(mla_loaded, 16)
                sp_eng.dma_start(uk_w[:], w_uk).then_inc(mla_loaded, 16)
                sp_eng.dma_start(uq_w[:], w_uq).then_inc(mla_loaded, 16)
                sp_eng.wait_ge(unit_out, unit_done["q", ML_H - 1])
                sp_eng.dma_start(w_out2, od_out).then_inc(w_out2_loaded, 16)

            @block.gpsimd
            def _(pool):
                for h in range(MLA_H):
                    if h == 0:
                        pool.wait_ge(key_ready, 1)
                    if h >= 2:
                        pool.wait_ge(att_scores, 2 * (h - 1))
                    pool.tensor_copy(k_att[NOPE:QD, h % 2], k_rot[NOPE:QD]).then_inc(k_rope_ready, 1)

            @block.scalar
            def _(act):
                steps = Steps(act, act_steps)
                mix1.act_squares(act)
                mix1.act_root(act)
                mix1.act_affine(act, segs, lambda d, s: gain[:, 1, 0, d, s:s + 1],
                                lambda d, s: modc[:, 1, 0, d, s:s + 1])
                act.wait_ge(pads2, 2)
                gate_b = col("ml_gate_b")
                for n, (part, i) in enumerate(UNITS):
                    act.wait_ge(unit_out, n + 1)
                    bank = ps[:, BANK[n % 4], :]
                    if part == "gates":
                        act.activation(g_in[0:HALF_ROWS], bank[0:HALF_ROWS], ACT.Identity,
                                       bias=gate_b[0:HALF_ROWS])
                        last = act.activation(g_forget[0:HALF_ROWS], bank[64:GATE_ROWS], ACT.Identity,
                                              bias=gate_b[64:GATE_ROWS])
                    elif part == "k":
                        last = act.activation(k_pad[:, i, :, 2:2 + SEG],
                                              bank.rearrange("p (s t) -> p s t", s=2), ACT.Copy)
                    elif part == "q":
                        last = act.activation(q_pad[:, i, 2:2 + SEG], bank[:, 0:N_LAT], ACT.Copy)
                    elif part == "ckv":
                        last = act.activation(ckv[:, i], bank, ACT.Copy)
                    elif part == "krope":
                        last = act.activation(k_rot[0:QD], bank[0:QD], ACT.Copy)
                    elif part == "cq":
                        last = act.activation(cq[:, i], bank[:, 0:N_LAT], ACT.Copy)
                    elif part == "v":
                        last = act.activation(v_tok[:, i], bank, ACT.Copy)
                    else:
                        last = act.activation(o_tanh[:, i], bank[:, 0:N_LAT], ACT.Tanh, scale=0.5)
                    last.then_inc(unit_taken, 1)
                act.wait_ge(forget_abs, 1)
                at = chain_b[0:HALF_ROWS, 0]
                act.activation(at, at, ACT.Exp, scale=-1.0).then_inc(forget_exp, 1)
                for n in range(2 * ML_H):
                    act.wait_ge(conv_done, n + 1)
                    if n >= 2:
                        act.wait_ge(qk_ready, n - 1)
                    size = T if n < ML_H else N_LAT
                    src = ks_ml[:, n] if n < ML_H else qs_ml[:, n - ML_H]
                    act.activation(th[:, n % 2, 0:size], src, ACT.Tanh, scale=0.5).then_inc(conv_tanh, 1)
                act.wait_ge(stab_in, 1)
                at = chain_b[0:HALF_ROWS, 7, N_LAT:T]
                act.activation(at, at, ACT.Exp).then_inc(stab_ready, 1)
                kv_norm.act_squares(act)
                kv_norm.act_root(act)
                kv_norm.act_affine(act, [slice(0, T)], lambda d, _: col("kv_norm_g")[:, d:d + 1], None)
                act.wait_ge(kv_norm.summed, KV_LORA // P)
                q_norm.act_squares(act)
                q_norm.act_root(act)
                q_norm.act_affine(act, [slice(0, N_LAT)], lambda d, _: col("q_norm_g")[:, d:d + 1], None)
                for tt in range(T // P):
                    act.wait_ge(va_out, tt + 1)
                    act.activation(v_att[:, tt], ps[:, BANK[tt], :], ACT.Copy).then_inc(va_ready, 1)

                def ml_e(m):
                    act.wait_ge(ml_arg, m + 1)
                    at = weights_ml[:, m % 2]
                    act.activation(at, at, ACT.Exp).then_inc(ml_exp, 1)

                ml_e(0)
                for m in range(M_UNITS):
                    if m + 1 < M_UNITS:
                        ml_e(m + 1)
                    act.wait_ge(ml_sums, m + 1)
                    if m >= 1:
                        act.wait_ge(ml_head, m)
                    act.activation(den_abs, ps[:, 3 + m % 2, N_LAT:T], ACT.Abs).then_inc(ml_abs, 1)
                act.wait_ge(ml_head, M_UNITS)
                act.activation(squares[:].rearrange("p a b -> p (a b)"),
                               h_sum.rearrange("p a b -> p (a b)"), ACT.Square).then_inc(out_sq, 1)
                act.wait_ge(out_ms, 2)
                for i in range(2):
                    act.activation(weights_ml[:, i, 0:2].rearrange("p a b -> p (a b)"),
                                   weights_ml[:, i, 0:2].rearrange("p a b -> p (a b)"),
                                   ACT.Sqrt).then_inc(out_root, 1)

                def prepare(h):
                    act.wait_ge(uq_out, h + 1)
                    if h >= 2:
                        act.wait_ge(q_ready, h - 1)
                    act.activation(q_raw[0:QD, h % 2], ps[0:QD, 1, 0:N_LAT], ACT.Copy).then_inc(q_raw_ready, 1)
                    act.wait_ge(uk_out, h + 1)
                    if h >= 2:
                        act.wait_ge(att_scores, 2 * (h - 1))
                    act.activation(k_att[0:NOPE, h % 2], ps[0:NOPE, 2, :], ACT.Copy).then_inc(k_nope_ready, 1)

                prepare(0)
                for h in range(MLA_H):
                    for qt in range(2):
                        n = 2 * h + qt
                        act.wait_ge(att_max, n + 1)
                        if n >= 2:
                            act.wait_ge(att_turned, n - 1)
                        act.activation(probs[:, qt], ps[:, 3 + qt, :], ACT.Exp, scale=ATT_SCALE,
                                       bias=soft_a[:, qt, 1:2], accum_out=soft_a[:, qt, 2:3]).then_inc(att_exp, 1)
                    if h + 1 < MLA_H:
                        prepare(h + 1)
                    for qt in range(2):
                        n = 2 * h + qt
                        act.wait_ge(att_turned, n + 1)
                        if h >= 2:
                            act.wait_ge(att_out, h - 1)
                        act.activation(probs_t[:, h % 2, :, qt * P:(qt + 1) * P],
                                       ps[:, 5 + qt, :].rearrange("p (a b) -> p a b", a=4),
                                       ACT.Copy).then_inc(att_kept, 1)
                    act.wait_ge(att_out, h + 1)
                    act.activation(mix2[VD * (h % 2):VD * (h % 2) + VD, ML_H + h // 2],
                                   ps[0:VD, 7, 0:N_LAT], ACT.Copy).then_inc(att_mixed, 1)

            @block.vector
            def _(dve):
                steps = Steps(dve, dve_steps)
                mix1.dve_mean(dve)
                mix1.dve_scale(dve, steps)
                q4, k4 = q_pad, k_pad
                steps(dve.memset(q4[:, :, 0:2], 0.0))
                steps(dve.memset(k4[:, :, :, 0:2], 0.0))
                dve.memset(q4[:, :, 2 + SEG:], 0.0).then_inc(pads2, 1)
                dve.memset(k4[:, :, :, 2 + SEG:], 0.0).then_inc(pads2, 1)
                rows = slice(0, HALF_ROWS)
                e, z, z2, lf, run, c, m_run, ns = (chain_b[rows, i] for i in range(8))
                dve.wait_ge(unit_taken, len(UNITS))
                gf, gi = g_forget[rows], g_in[rows]
                dve.scalar_tensor_tensor(out=e, in0=gf, scalar=-1.0, in1=gf, op0=ALU.mult,
                                         op1=ALU.max).then_inc(forget_abs, 1)
                dve.wait_ge(pads2, 2)
                for n in range(2 * ML_H):
                    i = n % ML_H
                    w = col("ml_conv_w")
                    blk = ML_H + i if n < ML_H else i
                    if n < ML_H:
                        to = ks_ml[:, i].rearrange("p (s t) -> p s t", s=2)
                        src = lambda a: k4[:, i, :, a:a + SEG]
                    else:
                        to = qs_ml[:, i]
                        src = lambda a: q4[:, i, a:a + SEG]
                    steps(dve.tensor_scalar(to, src(0), w[:, blk, 0:1], col("ml_conv_b")[:, blk:blk + 1],
                                            ALU.mult, ALU.add))
                    for a in range(1, CONV_W):
                        last = dve.scalar_tensor_tensor(out=to, in0=src(a), scalar=w[:, blk, a:a + 1],
                                                        in1=to, op0=ALU.mult, op1=ALU.add)
                        if a < CONV_W - 1:
                            steps(last)
                    last.then_inc(conv_done, 1)
                dve.wait_ge(forget_exp, 1)
                softplus_tail(dve, steps, e, z, z2, lf)
                steps(dve.scalar_tensor_tensor(out=lf, in0=gf, scalar=0.0, in1=lf, op0=ALU.min,
                                               op1=ALU.subtract))
                steps(dve.memset(e, 1.0))
                back = slice(32, HALF_ROWS)
                steps(dve.tensor_tensor_scan(out=run, data0=e, data1=lf, initial=0.0, op0=ALU.mult,
                                             op1=ALU.add))
                B = chain_b[:, 4]
                for s, first in ((0, 0.0), (1, B[back, 0:1])):
                    steps(dve.tensor_tensor_scan(
                        out=B[back, segs[s]][:, ::-1], data0=chain_b[back, 0, segs[s]][:, ::-1],
                        data1=chain_b[back, 3, segs[s]][:, ::-1], initial=first, op0=ALU.mult, op1=ALU.add))
                dve.tensor_tensor(c, gi, run, ALU.subtract).then_inc(c_ready, 1)
                dve.wait_ge(c_ready, 1)
                steps(dve.tensor_tensor_scan(out=m_run, data0=c, data1=c, initial=NEG, op0=ALU.max,
                                             op1=ALU.max))
                M, C = chain_b[:, 6], chain_b[:, 5]
                for s, first in ((0, NEG), (1, M[back, 0:1])):
                    steps(dve.tensor_tensor_scan(
                        out=M[back, segs[s]][:, ::-1], data0=C[back, segs[s]][:, ::-1],
                        data1=C[back, segs[s]][:, ::-1], initial=first, op0=ALU.max, op1=ALU.max))
                steps(dve.tensor_scalar(ns[:, 0:N_LAT], m_run[:, LAT], -1.0, None, ALU.mult))
                steps(dve.tensor_tensor(ns[:, LAT], ns[:, 0:N_LAT], run[:, LAT], ALU.subtract))
                dve.tensor_scalar(ns[:, LAT], ns[:, LAT], 80.0, None, ALU.min).then_inc(stab_in, 1)
                for n in range(2 * ML_H):
                    dve.wait_ge(conv_tanh, n + 1)
                    size = T if n < ML_H else N_LAT
                    at = ks_ml[:, n] if n < ML_H else qs_ml[:, n - ML_H]
                    dve.scalar_tensor_tensor(out=at, in0=th[:, n % 2, 0:size], scalar=1.0, in1=at,
                                             op0=ALU.add, op1=ALU.mult).then_inc(qk_ready, 1)
                dve.wait_ge(c_turned, 1)
                dve.tensor_copy(c_col, ps[:, 5, 0:4 * HALF_ROWS].rearrange("p (a b) -> p a b", a=4)
                                ).then_inc(c_col_ready, 1)
                dve.wait_ge(key_swapped, 1)
                steps(dve.tensor_tensor(q_sin[0:QD, 0], ps[0:QD, 6, 0:N_LAT], const("rope_sin")[0:QD], ALU.mult))
                steps(dve.tensor_tensor(k_rot[0:QD, LAT], k_rot[0:QD, LAT], const("rope_cos")[0:QD], ALU.mult))
                dve.tensor_tensor(k_rot[0:QD, LAT], k_rot[0:QD, LAT], q_sin[0:QD, 0],
                                  ALU.add).then_inc(key_ready, 1)
                dve.wait_ge(key_ready, 1)
                kv_norm.dve_mean(dve)
                kv_norm.dve_scale(dve, steps)
                q_norm.dve_mean(dve)
                q_norm.dve_scale(dve, steps)
                dve.wait_ge(c_col_ready, 1)

                def ml_d(m):
                    h, d = m // 2, m % 2
                    dve.wait_ge(ml_spread, m + 1)
                    if m >= 2:
                        dve.wait_ge(ml_sums, m - 1)
                    for kt in range(T // P):
                        row = 32 * d + h
                        last = dve.tensor_scalar(weights_ml[:, m % 2, kt], ps[:, 1 + m % 2, 0:N_LAT],
                                                 c_col[:, kt, row:row + 1], 0.0, ALU.add, ALU.min)
                    last.then_inc(ml_arg, 1)

                def ml_p(m):
                    h, d = m // 2, m % 2
                    dve.wait_ge(ml_exp, m + 1)
                    dve.wait_ge(ml_scores, h + 1)
                    at = weights_ml[:, m % 2].rearrange("p a b -> p (a b)")
                    steps(dve.scalar_tensor_tensor(
                        out=at, in0=ps[:, 6:8, :].rearrange("p a b -> p (a b)"), scalar=ML_SCALE, in1=at,
                        op0=ALU.mult, op1=ALU.mult))
                    late = weights_ml[:, m % 2, 2:4]
                    dve.tensor_tensor(late, late, const("causal")[:, d], ALU.mult).then_inc(ml_weights, 1)

                def ml_h(m):
                    h, d = m // 2, m % 2
                    dve.wait_ge(ml_abs, m + 1)
                    steps(dve.tensor_tensor(h_rec, den_abs, ps[:, 1 + m % 2, N_LAT:T], ALU.max))
                    steps(dve.reciprocal(h_rec, h_rec))
                    to = h_sum[:, h] if d == 0 else h_rec
                    if d == 0:
                        dve.tensor_tensor(to, ps[:, 3 + m % 2, 0:N_LAT], h_rec, ALU.mult).then_inc(ml_head, 1)
                    else:
                        steps(dve.tensor_tensor(to, ps[:, 3 + m % 2, 0:N_LAT], h_rec, ALU.mult))
                        dve.tensor_tensor(h_sum[:, h], h_sum[:, h], h_rec, ALU.add).then_inc(ml_head, 1)
                    dve.wait_ge(ml_head, m + 1)

                ml_d(0)
                for m in range(M_UNITS):
                    ml_p(m)
                    if m >= 1:
                        ml_h(m - 1)
                    if m + 1 < M_UNITS:
                        ml_d(m + 1)
                ml_h(M_UNITS - 1)
                dve.wait_ge(out_ss, 2)
                for i in range(2):
                    dve.tensor_scalar(weights_ml[:, i, 0:2].rearrange("p a b -> p (a b)"),
                                      ps[:, 5 if i == 0 else 0, :], 4.0 / P, 4.0 * EPS, ALU.mult,
                                      ALU.add).then_inc(out_ms, 1)
                dve.wait_ge(out_root, 2)
                for i in range(2):
                    at = weights_ml[:, i, 0:2]
                    steps(dve.reciprocal(at, at))
                    for j in range(2):
                        h = 2 * i + j
                        steps(dve.scalar_tensor_tensor(out=h_sum[:, h], in0=h_sum[:, h],
                                                       scalar=col("ml_head_g")[:, h:h + 1], in1=at[:, j],
                                                       op0=ALU.mult, op1=ALU.mult))
                        dve.scalar_tensor_tensor(out=mix2[:, h], in0=o_tanh[:, h], scalar=1.0,
                                                 in1=h_sum[:, h], op0=ALU.add,
                                                 op1=ALU.mult).then_inc(ml_mixed, 1)

                def rotate(h):
                    dve.wait_ge(q_swapped, h + 1)
                    if h >= 2:
                        dve.wait_ge(att_scores, 2 * (h - 1))
                    b = h % 2
                    steps(dve.tensor_tensor(q_sin[0:QD, b], ps[0:QD, 0, 0:N_LAT], const("rope_sin")[0:QD], ALU.mult))
                    steps(dve.tensor_tensor(q_att[0:QD, b], q_raw[0:QD, b], const("rope_cos")[0:QD], ALU.mult))
                    dve.tensor_tensor(q_att[0:QD, b], q_att[0:QD, b], q_sin[0:QD, b], ALU.add).then_inc(q_ready, 1)
                    dve.wait_ge(q_ready, h + 1)

                rotate(0)
                for h in range(MLA_H):
                    for qt in range(2):
                        n = 2 * h + qt
                        dve.wait_ge(att_scores, n + 1)
                        steps(dve.reduce_max(soft_a[:, qt, 0:1], ps[:, 3 + qt, :], AX))
                        dve.tensor_scalar(soft_a[:, qt, 1:2], soft_a[:, qt, 0:1], -ATT_SCALE, None,
                                          ALU.mult).then_inc(att_max, 1)
                    if h + 1 < MLA_H:
                        rotate(h + 1)
                    for qt in range(2):
                        n = 2 * h + qt
                        dve.wait_ge(att_exp, n + 1)
                        steps(dve.reciprocal(soft_a[:, qt, 3:4], soft_a[:, qt, 2:3]))
                        dve.tensor_scalar(probs[:, qt], probs[:, qt], soft_a[:, qt, 3:4], None,
                                          ALU.mult).then_inc(att_probs, 1)
                for n in range(KT):
                    dve.wait_ge(odd_out, n + 1)
                    dve.scalar_tensor_tensor(
                        out=hT[:, n, LAT], in0=ps[:, BANK[n % 4], 0:N_LAT],
                        scalar=modc[:, 1, 2, n, 1:2], in1=hT[:, n, LAT], op0=ALU.mult,
                        op1=ALU.add).then_inc(odd_added, 1)

            @block.tensor
            def _(pe):
                mix1.pe_sums(pe, ones[:])
                for n, (part, i) in enumerate(UNITS):
                    if i == 0:
                        pe.wait_ge(part_loaded[part], 16)
                    if n >= 4:
                        pe.wait_ge(unit_taken, n - 3)
                    w = od_part(part)
                    rows = min(P, width[part])
                    tokens = LAT if part in LAT_ONLY else slice(0, T)
                    for k in range(KT):
                        if n == 0:
                            pe.wait_ge(mix1.ready, k + 1)
                        if part == "v":
                            last = pe.matmul(ps[:, BANK[n % 4], :], uT[:, k, i * P:(i + 1) * P], w[:, k],
                                             start=(k == 0), stop=(k == KT - 1))
                        else:
                            size = tokens.stop - tokens.start
                            last = pe.matmul(ps[0:rows, BANK[n % 4], 0:size],
                                             w[:, k, i * P:i * P + rows], uT[:, k, tokens],
                                             start=(k == 0), stop=(k == KT - 1))
                    last.then_inc(unit_out, 1)
                pe.wait_ge(unit_taken, len(UNITS))
                pe.matmul(ps[0:QD, 6, 0:N_LAT], const("rope_swap")[0:QD], k_rot[0:QD, LAT], start=True,
                          stop=True).then_inc(key_swapped, 1)
                pe.wait_ge(c_ready, 1)
                for kt in range(T // P):
                    last = pe.transpose(ps[:, 5, kt * HALF_ROWS:(kt + 1) * HALF_ROWS],
                                        chain_b[0:HALF_ROWS, 5, kt * P:(kt + 1) * P],
                                        ident[0:HALF_ROWS, 0:HALF_ROWS])
                last.then_inc(c_turned, 1)
                kv_norm.pe_sums(pe, ones[:])
                q_norm.pe_sums(pe, ones[:])
                pe.wait_ge(mla_loaded, 48)
                pe.wait_ge(kv_norm.ready, KV_LORA // P)
                for tt in range(T // P):
                    for k in range(KV_LORA // P):
                        last = pe.matmul(ps[:, BANK[tt], :], ckv[:, k, tt * P:(tt + 1) * P], uv_w[:, k],
                                         start=(k == 0), stop=(k == KV_LORA // P - 1))
                    last.then_inc(va_out, 1)

                def spread(m):
                    if m >= 2:
                        pe.wait_ge(ml_head, m - 1)
                    i = ML_H * (m % 2) + m // 2
                    pe.matmul(ps[:, 1 + m % 2, :], const("pick")[0:HALF_ROWS, i], chain_b[0:HALF_ROWS, 7],
                              start=True, stop=True).then_inc(ml_spread, 1)

                def ml_score(h):
                    if h >= 1:
                        pe.wait_ge(ml_weights, 2 * h)
                    for kt in range(T // P):
                        last = pe.matmul(ps[:, 6 + kt // 2, kt % 2 * N_LAT:kt % 2 * N_LAT + N_LAT],
                                         ks_ml[:, h, kt * P:(kt + 1) * P], qs_ml[:, h], start=True, stop=True)
                    last.then_inc(ml_scores, 1)

                pe.wait_ge(va_ready, T // P)
                pe.wait_ge(stab_ready, 1)
                pe.wait_ge(qk_ready, 2 * ML_H)
                pe.wait_ge(key_ready, 1)
                pe.wait_ge(q_norm.ready, Q_LORA // P)
                spread(0)
                ml_score(0)
                spread(1)
                for m in range(M_UNITS):
                    h = m // 2
                    pe.wait_ge(ml_weights, m + 1)
                    if m >= 2:
                        pe.wait_ge(ml_head, m - 1)
                    for to, lhs in ((slice(0, N_LAT), None), (LAT, ones[:])):
                        for kt in range(T // P):
                            last = pe.matmul(ps[:, 3 + m % 2, to],
                                             v_tok[:, kt, h * P:(h + 1) * P] if lhs is None else lhs,
                                             weights_ml[:, m % 2, kt], start=(kt == 0), stop=(kt == T // P - 1))
                    last.then_inc(ml_sums, 1)
                    if m % 2 == 1 and h + 1 < ML_H:
                        ml_score(h + 1)
                    if m + 2 < M_UNITS:
                        spread(m + 2)
                pe.wait_ge(out_sq, 1)
                for i in range(2):
                    pe.matmul(ps[:, 5 if i == 0 else 0, :], ones[:], squares[:, i], start=True,
                              stop=True).then_inc(out_ss, 1)

                def prepare_q(h):
                    if h >= 1:
                        pe.wait_ge(q_raw_ready, h)
                    for k in range(Q_LORA // P):
                        last = pe.matmul(ps[0:QD, 1, 0:N_LAT], uq_w[:, k, h * QD:(h + 1) * QD], cq[:, k],
                                         start=(k == 0), stop=(k == Q_LORA // P - 1))
                    last.then_inc(uq_out, 1)
                    if h >= 1:
                        pe.wait_ge(k_nope_ready, h)
                    for k in range(KV_LORA // P):
                        last = pe.matmul(ps[0:NOPE, 2, :], uk_w[:, k, h], ckv[:, k],
                                         start=(k == 0), stop=(k == KV_LORA // P - 1))
                    last.then_inc(uk_out, 1)

                def swap_q(h):
                    pe.wait_ge(q_raw_ready, h + 1)
                    if h >= 1:
                        pe.wait_ge(q_ready, h)
                    pe.matmul(ps[0:QD, 0, 0:N_LAT], const("rope_swap")[0:QD], q_raw[0:QD, h % 2],
                              start=True, stop=True).then_inc(q_swapped, 1)

                pe.wait_ge(out_ms, 2)
                pe.wait_ge(ml_head, M_UNITS)
                prepare_q(0)
                swap_q(0)
                for h in range(MLA_H):
                    pe.wait_ge(q_ready, h + 1)
                    pe.wait_ge(k_nope_ready, h + 1)
                    pe.wait_ge(k_rope_ready, h + 1)
                    for qt in range(2):
                        if h >= 1:
                            pe.wait_ge(att_exp, 2 * (h - 1) + qt + 1)
                        pe.matmul(ps[:, 3 + qt, :], q_att[0:QD, h % 2, qt * P:(qt + 1) * P],
                                  k_att[0:QD, h % 2], start=True, stop=True).then_inc(att_scores, 1)
                    if h + 1 < MLA_H:
                        prepare_q(h + 1)
                        swap_q(h + 1)
                    for qt in range(2):
                        n = 2 * h + qt
                        pe.wait_ge(att_probs, n + 1)
                        if h >= 1:
                            pe.wait_ge(att_kept, n - 1)
                        for kt in range(T // P):
                            last = pe.transpose(ps[:, 5 + qt, kt * P:(kt + 1) * P],
                                                probs[:, qt, kt * P:(kt + 1) * P], ident)
                        last.then_inc(att_turned, 1)
                    pe.wait_ge(att_kept, 2 * h + 2)
                    if h >= 1:
                        pe.wait_ge(att_mixed, h)
                    for kt in range(T // P):
                        last = pe.matmul(ps[0:VD, 7, 0:N_LAT], v_att[:, kt, h * VD:(h + 1) * VD],
                                         probs_t[:, h % 2, kt], start=(kt == 0), stop=(kt == T // P - 1))
                    last.then_inc(att_out, 1)
                pe.wait_ge(w_out2_loaded, 16)
                pe.wait_ge(ml_mixed, ML_H)
                pe.wait_ge(att_mixed, MLA_H)
                pe.wait_ge(att_exp, 2 * MLA_H)
                for n in range(KT):
                    if n >= 4:
                        pe.wait_ge(odd_added, n - 3)
                    for k in range(KT):
                        last = pe.matmul(ps[:, BANK[n % 4], 0:N_LAT], w_out2[:, k, n * P:(n + 1) * P],
                                         mix2[:, k], start=(k == 0), stop=(k == KT - 1))
                    last.then_inc(odd_out, 1)
        odd_stack.close()
        end_phase()

        peer(1, SEG, SEG // P)

        last_norm = Norm("last", sem, lambda d: hT[:, d, LAT], squares, ps[:, 0, 0:N_LAT],
                         rms[:, 0:N_LAT], lambda d: uT[:, d, LAT], N_LAT, KT)
        stored = sem("stored")
        dve_steps = sem("last_dve_steps")
        with nc.Block() as block:
            @block.scalar
            def _(act):
                last_norm.act_squares(act)
                last_norm.act_root(act)
                last_norm.act_affine(act, [slice(0, N_LAT)], lambda d, _: col("final_g")[:, d:d + 1], None)

            @block.vector
            def _(dve):
                steps = Steps(dve, dve_steps)
                last_norm.dve_mean(dve)
                last_norm.dve_scale(dve, steps)

            @block.tensor
            def _(pe):
                last_norm.pe_sums(pe, ones[:])

            @block.sync
            def _(sp_eng):
                for half in range(2):
                    blocks = slice(4 * half, 4 * half + 4)
                    sp_eng.wait_ge(last_norm.ready, 4 * half + 4)
                    sp_eng.dma_start(out[:, blocks], uT[:, blocks, LAT]).then_inc(stored, 16)
                sp_eng.wait_ge(stored, 32)


def blocks_of(v):
    return v.reshape(-1, P).T


def rows_of(w):
    return np.ascontiguousarray(w.reshape(-1, P, w.shape[-1]).transpose(1, 0, 2))


def constants():
    c = np.zeros((P, N_CONSTS), np.float32)

    def put(name, value):
        at, shape = CONSTS[name]
        value = np.asarray(value, np.float64)
        value = value.reshape(value.shape[0], -1)
        c[:value.shape[0], at:at + value.shape[1]] = value

    put("ident", np.eye(P))
    a = 2 * np.pi * (np.outer(np.arange(64), np.arange(64)) % 64) / 64
    put("chan_dft", np.concatenate([np.kron(np.eye(2), np.cos(a)), np.kron(np.eye(2), np.sin(a))], 1))
    a = 2 * np.pi * (np.outer(np.arange(SEG), np.arange(SEG)) % SEG) / SEG
    both = np.stack([np.cos(a), -np.sin(a)]) / 128.0
    put("time_dft", both.reshape(2, 2, P, SEG).transpose(2, 0, 1, 3))
    half = ROPE // 2
    inv = (np.float32(10000.0) ** (-np.arange(0, half, 2, dtype=np.float32) / np.float32(half))).astype(np.float32)
    row = np.repeat(np.arange(SEG // 64, dtype=np.float32), 64)
    colu = np.tile(np.arange(64, dtype=np.float32), SEG // 64)
    ang = np.concatenate([row[:, None] * inv, colu[:, None] * inv], axis=-1).astype(np.float32)
    cos, sin = np.ones((QD, SEG)), np.zeros((QD, SEG))
    cos[NOPE:] = np.repeat(np.cos(ang.astype(np.float64)).T, 2, axis=0)
    sin[NOPE:] = np.repeat(np.sin(ang.astype(np.float64)).T, 2, axis=0)
    put("rope_cos", cos)
    put("rope_sin", sin)
    swap = np.zeros((QD, QD))
    for i in range(NOPE, QD, 2):
        swap[i + 1, i] = -1.0
        swap[i, i + 1] = 1.0
    put("rope_swap", swap)
    s, t = np.arange(SEG)[:, None], np.arange(SEG)[None, :]
    masks = np.stack([s <= t, s >= t]).astype(np.float64)
    put("causal", masks.reshape(2, 2, P, SEG).transpose(2, 0, 1, 3))
    pick = np.zeros((P, 2 * ML_H, P))
    for i in range(2 * ML_H):
        pick[32 * (i // ML_H) + i % ML_H, i] = 1.0
    put("pick", pick)
    put("iota", np.broadcast_to(np.arange(TOPK), (P, TOPK)))
    return c


def lay_out(x, c, ctx, c_ctx, mod_w, mod_b, norm_mix_g, norm_ffn_g, ev_w_in, ev_w_out, rg_conv_w,
            rg_conv_b, rg_wa, rg_ba, rg_wx, rg_bx, rg_lam, fn_w, fn_b, od_w_in, od_w_out,
            ml_conv_w, ml_conv_b, ml_gate_b, ml_head_g, mla_q_norm_g, mla_w_uq, mla_kv_norm_g,
            mla_w_ukv, peer_w_q, peer_keys, peer_u, peer_v, final_g):
    cols = np.zeros((P, N_COLS), np.float32)

    def put(name, value):
        at, shape = COLS[name]
        value = value.reshape(value.shape[0], -1)
        cols[:value.shape[0], at:at + value.shape[1]] = value

    put("cond", np.stack([blocks_of(c_ctx), blocks_of(c[0])], 2))
    put("mod_b", blocks_of(mod_b))
    put("norm_g", np.stack([norm_mix_g, norm_ffn_g], 1).reshape(-1, P).T)
    put("final_g", blocks_of(final_g))
    put("rg_conv_w", rg_conv_w[0].reshape(CONV_W, RG_H, P).transpose(2, 1, 0))
    put("rg_conv_b", blocks_of(rg_conv_b))
    put("rg_ba", blocks_of(rg_ba))
    put("rg_bx", blocks_of(rg_bx))
    put("rg_lam", blocks_of(rg_lam))
    put("fn_b", blocks_of(fn_b))
    put("ml_conv_w", ml_conv_w[0].reshape(CONV_W, 8, P).transpose(2, 1, 0))
    put("ml_conv_b", blocks_of(ml_conv_b))
    put("ml_head_g", blocks_of(ml_head_g))
    put("q_norm_g", blocks_of(mla_q_norm_g))
    put("kv_norm_g", blocks_of(mla_kv_norm_g))
    gb = np.zeros((GATE_ROWS, 1), np.float32)
    b = ml_gate_b.reshape(2, 2, ML_H)
    for d in range(2):
        for kind in range(2):
            at = 64 * kind + 32 * d
            gb[at:at + ML_H, 0] = b[d, kind]
    put("ml_gate_b", gb)

    even = np.zeros((P, N_EVEN), np.float32)
    at, _ = EVEN["fn_w"]
    even[:, :at] = np.stack([rg_wa[0], rg_wx[0]]).transpose(3, 0, 1, 2, 4).reshape(P, -1)
    even[:, at:] = fn_w[0].reshape(2, P, 64).transpose(1, 0, 2).reshape(P, -1)

    w = od_w_in[0]
    parts, at = {}, 0
    for name, n in ODD_PARTS[:4]:
        parts[name] = w[:, at:at + n]
        at += n
    gates = w[:, at:at + 16].reshape(D, 2, 2, ML_H)
    at += 16
    for name, n in ODD_PARTS[4:6]:
        parts[name] = w[:, at:at + n]
        at += n
    krope = np.zeros((D, QD), np.float32)
    krope[:, NOPE:] = w[:, at:]
    parts["krope"] = krope
    g = np.zeros((D, GATE_ROWS), np.float32)
    for kind in range(2):
        for d in range(2):
            g[:, 64 * kind + 32 * d:64 * kind + 32 * d + ML_H] = gates[:, d, kind]
    parts["gates"] = g
    od = np.concatenate([rows_of(parts[name]).reshape(P, -1) for name, _ in ODD_PARTS], 1)

    tokens = np.concatenate([ctx[0], x[0]], 0)
    ukv = rows_of(mla_w_ukv[0]).reshape(P, KV_LORA // P, MLA_H, NOPE + VD)
    return {
        "hT0": rows_of(np.ascontiguousarray(tokens.T)),
        "cols_in": cols,
        "consts_in": constants(),
        "mod_w": np.ascontiguousarray(
            mod_w.reshape(2, KT, P, N_MOD * KT // PIECE_J, PIECE_J * P).transpose(0, 3, 2, 1, 4)
        ).reshape(PIECES, P, KT, PIECE_J * P),
        "ev_in": np.ascontiguousarray(ev_w_in[0].reshape(KT, P, 7, 2 * P).transpose(2, 1, 0, 3)),
        "ev_out": rows_of(ev_w_out[0]),
        "even_in": even,
        "od": np.ascontiguousarray(od),
        "w_uq": rows_of(mla_w_uq[0]),
        "w_uk": np.ascontiguousarray(ukv[..., :NOPE]),
        "w_uv": np.ascontiguousarray(ukv[..., NOPE:]),
        "od_out": rows_of(od_w_out[0]),
        "peer_q": np.ascontiguousarray(
            peer_w_q.reshape(2, KT, P, 4, 4 * P).transpose(0, 3, 2, 1, 4)),
        "peer_keys": np.ascontiguousarray(peer_keys.transpose(0, 4, 2, 1, 3)),
        "peer_u0": peer_u[0], "peer_u1": peer_u[1], "peer_v0": peer_v[0], "peer_v1": peer_v[1],
    }


def kernel(**inputs):
    import concourse.bacc as _bacc
    from concourse import mybir as _mybir
    from concourse.bass_utils import run_bass_kernel_spmd as _run
    nc = _bacc.Bacc("TRN2", target_bir_lowering=False, num_devices=1)
    data = lay_out(**{name: np.asarray(value) for name, value in inputs.items()})
    args, arrays = {}, {}
    for name, value in data.items():
        arrays[f"in_{name}_dram"] = value
        args[name] = nc.dram_tensor(f"in_{name}_dram", value.shape, _mybir.dt.from_np(value.dtype),
                                    kind="ExternalInput").ap()
    out = nc.dram_tensor("out_0_dram", (P, KT, SEG), F32, kind="ExternalOutput").ap()
    args["peer_u"] = [args.pop("peer_u0"), args.pop("peer_u1")]
    args["peer_v"] = [args.pop("peer_v0"), args.pop("peer_v1")]
    backbone(nc, out=out, **args)
    got = _run(nc, [arrays], core_ids=[0]).results[0]["out_0_dram"]
    return np.ascontiguousarray(got.transpose(1, 0, 2).reshape(D, SEG).T).reshape(1, SEG, D)
```

```python
import math
from contextlib import ExitStack

import concourse.bass as bass
import numpy as np
from concourse import mybir

ALU = mybir.AluOpType
ACT = mybir.ActivationFunctionType
F32 = mybir.dt.float32
I32 = mybir.dt.int32
U32 = mybir.dt.uint32
AX = mybir.AxisListType.X

P = 128
D = 1024
KT = D // P
SEG = 256
T = 2 * SEG
EPS = 1e-6
N_MOD = 6
CONV_W = 4
RG_H = 6
EV_J = 14
ML_H = 4
MLA_H = 8
NOPE, ROPE, VD = 64, 32, 64
QD = NOPE + ROPE
Q_LORA, KV_LORA = 384, 256
PH = 8
NK = 128
TOPK = 16
SLOTS = PH * TOPK
PIECE_J = 4
PIECES = 2 * N_MOD * KT // PIECE_J
MOD_RING = 2
U_RING, V_RING = 8, 4
LAG = 20
NEG = -3.0e38
GATE_ROWS = 100
HALF_ROWS = 36
GELU_C = 0.044715
GELU_S = math.sqrt(2.0 / math.pi)


def offsets(spec):
    out, at = {}, 0
    for name, *shape in spec:
        out[name] = (at, shape)
        at += math.prod(shape)
    return out, at


COLS, N_COLS = offsets([
    ("cond", KT, 2), ("mod_b", 2, N_MOD * KT), ("norm_g", 2, 2, KT), ("final_g", KT),
    ("rg_conv_w", RG_H, CONV_W), ("rg_conv_b", RG_H), ("rg_ba", 2, RG_H), ("rg_bx", 2, RG_H),
    ("rg_lam", 2, RG_H), ("fn_b", 2), ("ml_conv_w", 8, CONV_W), ("ml_conv_b", 8),
    ("ident", P), ("ml_gate_b", 1), ("ml_head_g", ML_H), ("q_norm_g", Q_LORA // P), ("kv_norm_g", KV_LORA // P)])
CONSTS, N_CONSTS = offsets([
    ("chan_dft", 2, P), ("time_dft", 2, 2, SEG), ("rope_cos", SEG),
    ("rope_sin", SEG), ("rope_swap", QD), ("causal", 2, 2, SEG), ("pick", 2 * ML_H, P),
    ("iota", TOPK)])
EVEN, N_EVEN = offsets([("rg_w", 2, 2, RG_H, P), ("fn_w", 2, 64)])
ODD_PARTS = [("q", 512), ("k", 512), ("v", 512), ("o", 512), ("cq", Q_LORA), ("ckv", KV_LORA),
             ("krope", QD), ("gates", GATE_ROWS)]


def field(tensor, table, name):
    at, shape = table[name]
    ap = tensor[:, at:at + math.prod(shape)]
    if len(shape) > 1:
        names = "abcd"[:len(shape)]
        ap = ap.rearrange(f"p ({' '.join(names)}) -> p {' '.join(names)}",
                          **{n: s for n, s in zip(names, shape)})
    return ap


class Steps:

    def __init__(self, engine, semaphore):
        self.engine, self.semaphore, self.n = engine, semaphore, 0

    def __call__(self, instruction):
        self.n += 1
        instruction.then_inc(self.semaphore, 1)
        self.engine.wait_ge(self.semaphore, self.n)


class Norm:

    def __init__(self, name, sem, src, squares, bank, work, out, tokens, blocks, eps_of=None):
        self.src, self.squares, self.bank, self.work, self.out = src, squares, bank, work, out
        self.tokens, self.blocks = tokens, blocks
        self.squared = sem(f"{name}_squared")
        self.summed = sem(f"{name}_summed")
        self.mean = sem(f"{name}_mean")
        self.root = sem(f"{name}_root")
        self.scaled = sem(f"{name}_scaled")
        self.ready = sem(f"{name}_ready")

    def act_squares(self, act, after=None):
        for d in range(self.blocks):
            if after is not None:
                act.wait_ge(after[0], after[1] + d + 1)
            if d >= 2:
                act.wait_ge(self.summed, d - 1)
            act.activation(self.squares[:, d % 2, 0:self.tokens], self.src(d),
                           ACT.Square).then_inc(self.squared, 1)

    def pe_sums(self, pe, ones):
        for d in range(self.blocks):
            pe.wait_ge(self.squared, d + 1)
            pe.matmul(self.bank, ones, self.squares[:, d % 2, 0:self.tokens], start=(d == 0),
                      stop=(d == self.blocks - 1)).then_inc(self.summed, 1)

    def dve_mean(self, dve):
        dve.wait_ge(self.summed, self.blocks)
        dve.tensor_scalar(self.work, self.bank, 1.0 / (self.blocks * P), EPS, ALU.mult,
                          ALU.add).then_inc(self.mean, 1)

    def act_root(self, act):
        act.wait_ge(self.mean, 1)
        act.activation(self.work, self.work, ACT.Sqrt).then_inc(self.root, 1)

    def dve_scale(self, dve, steps):
        dve.wait_ge(self.root, 1)
        steps(dve.reciprocal(self.work, self.work))
        for d in range(self.blocks):
            dve.tensor_tensor(self.out(d), self.src(d), self.work, ALU.mult).then_inc(self.scaled, 1)

    def act_affine(self, act, parts, scale, shift):
        for d in range(self.blocks):
            act.wait_ge(self.scaled, d + 1)
            for n, part in enumerate(parts):
                at = self.out(d)[:, part]
                if shift is None:
                    last = act.activation(at, at, ACT.Copy, scale=scale(d, n))
                else:
                    last = act.activation(at, at, ACT.Identity, scale=scale(d, n), bias=shift(d, n))
            last.then_inc(self.ready, 1)


def softplus_tail(dve, steps, e, z, z2, p):
    steps(dve.tensor_scalar(z, e, 2.0, None, ALU.add))
    steps(dve.reciprocal(z, z))
    steps(dve.tensor_tensor(z, z, e, ALU.mult))
    steps(dve.tensor_tensor(z2, z, z, ALU.mult))
    steps(dve.tensor_scalar(p, z2, 1.0 / 17.0, None, ALU.mult))
    for k in (15, 13, 11, 9, 7, 5, 3):
        steps(dve.scalar_tensor_tensor(out=p, in0=p, scalar=1.0 / k, in1=z2, op0=ALU.add, op1=ALU.mult))
    steps(dve.scalar_tensor_tensor(out=p, in0=p, scalar=1.0, in1=z, op0=ALU.add, op1=ALU.mult))
    steps(dve.tensor_scalar(p, p, 2.0, None, ALU.mult))


def backbone(nc, hT0, cols_in, consts_in, mod_w, ev_in, ev_out, even_in, od, w_uq,
             w_uk, w_uv, od_out, peer_q, peer_keys, peer_u, peer_v, out):
    with ExitStack() as ctx:
        def sb(name, shape, dt=F32):
            return ctx.enter_context(nc.sbuf_tensor(name, shape, dt))

        phase_sems = []

        def sem(name):
            phase_sems.append(nc.alloc_semaphore(name=name))
            return phase_sems[-1]

        def end_phase():
            nc.clear_and_free_semaphores(phase_sems)
            nc.all_engine_barrier()
            phase_sems.clear()

        ps = ctx.enter_context(nc.psum_tensor("banks", [P, 8, 512], F32))

        hT = sb("hT", [P, KT, T])
        uT = sb("uT", [P, KT, T])
        cols = sb("cols", [P, N_COLS])
        consts = sb("consts", [P, N_CONSTS])
        ones = sb("ones", [P, P])
        modc = sb("modc", [P, 2, N_MOD, KT, 2])
        gain = sb("gain", [P, 2, 2, KT, 2])
        squares = sb("squares", [P, 2, T])
        rms = sb("rms", [P, T])
        weights = sb("weights", [P, KT * sum(n for _, n in ODD_PARTS)])

        def col(name):
            return field(cols, COLS, name)

        def const(name):
            return field(consts, CONSTS, name)

        def view(base, at, *shape):
            n = math.prod(shape)
            names = "abcd"[:len(shape)]
            return base[:, at:at + n].rearrange(
                f"p ({' '.join(names)}) -> p {' '.join(names)}",
                **{x: s for x, s in zip(names, shape)}), at + n

        CHUNK = KT * 4 * P
        w_q = [view(weights, (c + 2) % 4 * CHUNK, KT, 4 * P)[0] for c in range(4)]
        keys, peer_free = view(weights, 4 * CHUNK, PH, 2, NK)
        EARLY = 3

        def load_early(sp_eng, layer, arrived):
            for c in (0, 1):
                sp_eng.dma_start(w_q[c], peer_q[layer, c]).then_inc(arrived, 16)
            sp_eng.dma_start(keys, peer_keys[layer]).then_inc(arrived, 16)

        def peer_norm(layer, part, bank):
            n = part.stop - part.start
            return Norm(f"peer{layer}_norm{part.start}", sem, lambda d: hT[:, d, part], squares,
                        ps[:, bank, 0:n], rms[:, part], lambda d: uT[:, d, part], n, KT)

        def mix1_norm(side, bank):
            part = slice(side * SEG, (side + 1) * SEG)
            return Norm(f"mix1_norm{side}", sem, lambda d: hT[:, d, part], squares,
                        ps[:, bank, 0:SEG], rms[:, part], lambda d: uT[:, d, part], SEG, KT)

        ident = col("ident")
        loaded = sem("tables_loaded")
        ones_set = sem("ones_set")
        dve_steps = sem("even_dve_steps")
        act_steps = sem("even_act_steps")

        even_stack = ExitStack()

        def esb(name, shape):
            return even_stack.enter_context(nc.sbuf_tensor(name, shape, F32))

        even_w = esb("even_w", [P, N_EVEN])
        silu = esb("silu", [P, KT, 2])
        mod_ring, at = view(weights, 0, MOD_RING, KT, PIECE_J * P)
        w_in_at = at
        w_in, at = view(weights, at, 7, KT, 2 * P)
        mod_rows = esb("mod_rows", [2, 2, PIECE_J * P])
        select = esb("select", [P, 2, 2])
        row_parts = squares
        mixer = esb("even_mixer", [P, 10908])

        at = 0
        xpad, at = view(mixer, at, RG_H, 2, SEG + CONV_W - 1)
        decay_fwd, _ = view(mixer, 0, RG_H, T)
        xc, at = view(mixer, at, RG_H, T)
        gate, at = view(mixer, at, RG_H, T)
        w_out, _ = view(mixer, 0, KT, D)
        xf, at = view(mixer, at, 2, T)
        dft_w, at = view(mixer, at, 2, 2, P)
        sp, at = view(mixer, at, 8, 2 * RG_H)
        half_b, at = view(mixer, at, 2, 2 * RG_H)
        assert at <= 10908 and KT * D <= RG_H * (2 * (SEG + CONV_W - 1) + 2 * T)
        root, at = view(weights, w_in_at, RG_H, T)
        h_fwd, at = view(weights, at, RG_H, T)
        assert at <= w_in_at + (RG_H // 2) * KT * 2 * P
        h_back, at = view(weights, at, RG_H, T)
        decay_back, at = view(weights, at, RG_H, T)
        xw, at = view(weights, at, 4, 2, 2 * P)
        mixT = uT
        segs = [slice(0, SEG), slice(SEG, T)]
        BANK = [1, 2, 3, 4]
        ON_VECTOR = (5, 7, 10, 13)
        FIRST = 2 * 2
        UNITS0 = [("proj", j) for j in range(RG_H + 1)]
        for h in range(RG_H):
            UNITS0 += [("gate", 0, h, 0), ("gate", 0, h, 1), ("proj", RG_H + 1 + h)]
        UNITS0 += [("proj", EV_J - 1)] + [("chan", n) for n in range(8)] + [("time", n) for n in range(4)]
        UNITS0 += [("gate", 1, h, kind) for h in range(RG_H) for kind in range(2)]
        unit0 = {u: n + 1 for n, u in enumerate(UNITS0)}
        AFTER = {("proj", 6): 2, ("proj", 7): 1, ("proj", 8): 1, ("proj", 9): 1, ("proj", 13): 1,
                 ("chan", 7): 2, ("time", 3): 1, ("gate", 1, 2, 1): 2, ("gate", 1, RG_H - 1, 1): 6}
        OUT_AT = FIRST + sum(AFTER.values())
        assert OUT_AT >= N_MOD * KT // PIECE_J

        part0, part1 = sem("mod_part0"), sem("mod_part1")
        parts_made, select_set = sem("mod_parts_made"), sem("select_set")
        piece_loaded = [sem(f"mod_piece_loaded{r}") for r in range(MOD_RING)]
        rows_out, rows_taken, mod_turned = sem("mod_rows_out"), sem("mod_rows_taken"), sem("mod_turned")
        w_in_loaded = [sem(f"ev_w_in_loaded{c}") for c in range(7)]
        w_out_loaded = sem("ev_w_out_loaded")
        h_loaded, even_w_loaded = sem("hT_loaded"), sem("even_w_loaded")
        consts_loaded = sem("consts_loaded")
        cond_tanh, silu_ready, mod_ready = sem("cond_tanh"), sem("silu_ready"), sem("mod_ready")
        mix0 = Norm("mix0", sem, lambda d: hT[:, d, :], squares, ps[:, 0, :], rms[:],
                    lambda d: uT[:, d, :], T, KT)
        unit0_out, unit0_taken = sem("even_unit_out"), sem("even_unit_taken")
        pads_set = sem("even_pads_set")
        xc_ready = sem("xc_ready")
        lam_exp, lam_abs, sp_ready = sem("lam_exp"), sem("lam_abs"), sem("softplus_ready")
        roots, root_used = sem("rg_roots"), sem("rg_root_used")
        small_product, dft_w_ready = sem("dft_w_product"), sem("dft_w_ready")
        mix_ready = sem("rg_mix_ready")
        even_out, even_added = sem("even_out_product"), sem("even_added")
        early0 = sem("peer0_weights_arrived")
        norms0 = [peer_norm(0, segs[side], 0) for side in range(2)]

        mod_ps = ps[:, 7, 0:2 * N_MOD * KT * 2]
        rows_ps = [ps[0:2, 5, :], ps[0:2, 6, :]]
        GROUP = RG_H // 2

        with nc.Block() as block:
            @block.sync
            def _(sp_eng):
                def piece(i):
                    before = i - MOD_RING
                    if before in ON_VECTOR:
                        sp_eng.wait_ge(parts_made, ON_VECTOR.index(before) + 1)
                    elif before >= 0:
                        sp_eng.wait_ge(rows_out, before + 1)
                    sp_eng.dma_start(mod_ring[:, i % MOD_RING], mod_w[i]).then_inc(
                        piece_loaded[i % MOD_RING], 16)

                sp_eng.dma_start(cols[:], cols_in).then_inc(loaded, 16)
                piece(0)
                piece(1)
                sp_eng.dma_start(hT[:], hT0).then_inc(h_loaded, 16)
                piece(2)
                piece(3)
                for c in range(7):
                    sp_eng.dma_start(w_in[:, c], ev_in[c]).then_inc(w_in_loaded[c], 16)
                    if c == 2:
                        sp_eng.dma_start(even_w[:], even_in).then_inc(even_w_loaded, 16)
                    if c == 3:
                        sp_eng.dma_start(consts[:], consts_in).then_inc(consts_loaded, 16)
                for i in range(FIRST, OUT_AT):
                    piece(i)
                sp_eng.wait_ge(mix_ready, RG_H)
                sp_eng.dma_start(w_out, ev_out).then_inc(w_out_loaded, 16)
                sp_eng.wait_ge(unit0_out, unit0["time", 3])
                load_early(sp_eng, 0, early0)
                for i in range(OUT_AT, PIECES):
                    piece(i)
                sp_eng.wait_ge(early0, 16 * EARLY)

            @block.scalar
            def _(act):
                steps = Steps(act, act_steps)

                def take_rows(i):
                    act.wait_ge(rows_out, i + 1)
                    act.activation(mod_rows[:, i % 2], rows_ps[i % 2], ACT.Copy).then_inc(rows_taken, 1)

                act.wait_ge(loaded, 16)
                act.activation(silu[:], col("cond"), ACT.Tanh, scale=0.5).then_inc(cond_tanh, 1)
                act.wait_ge(lam_abs, 1)
                act.activation(sp[:, 1], sp[:, 1], ACT.Exp, scale=-1.0).then_inc(lam_exp, 1)
                take_rows(0)
                take_rows(1)
                act.wait_ge(h_loaded, 16)
                mix0.act_squares(act)
                mix0.act_root(act)
                take_rows(2)
                take_rows(3)
                act.wait_ge(mod_ready, 1)
                mix0.act_affine(act, segs, lambda d, s: gain[:, 0, 0, d, s:s + 1],
                                lambda d, s: modc[:, 0, 0, d, s:s + 1])
                act.wait_ge(pads_set, 1)
                act.wait_ge(sp_ready, 1)
                next_piece = FIRST
                for n, (kind, i, *rest) in enumerate(UNITS0):
                    act.wait_ge(unit0_out, n + 1)
                    bank = ps[:, BANK[n % 4], :]
                    if kind == "proj" and i < RG_H:
                        act.activation(xpad[:, i, :, 2:2 + SEG], bank.rearrange("p (s t) -> p s t", s=2),
                                       ACT.Copy).then_inc(unit0_taken, 1)
                    elif kind == "proj" and i < 2 * RG_H:
                        act.activation(gate[:, i - RG_H], bank, ACT.Gelu_apprx_tanh).then_inc(unit0_taken, 1)
                    elif kind == "proj":
                        act.activation(xf[:, i - 2 * RG_H], bank, ACT.Copy).then_inc(unit0_taken, 1)
                    elif kind == "chan":
                        act.activation(xw[:, i % 4, i // 4], bank[:, 0:2 * P], ACT.Copy).then_inc(unit0_taken, 1)
                    elif kind == "time":
                        act.activation(mixT[:, RG_H + i // 2, segs[i % 2]], bank[:, 0:SEG], ACT.Identity,
                                       bias=col("fn_b")[:, i // 2:i // 2 + 1]).then_inc(unit0_taken, 1)
                    else:
                        d, (h, which) = i, rest
                        c = RG_H * d + h
                        if d == 1 and which == 0:
                            act.wait_ge(root_used, h // GROUP + 1)
                        if which == 0:
                            act.activation(root[:, h], bank, ACT.Tanh, scale=0.5,
                                           bias=half_b[:, 0, c:c + 1]).then_inc(unit0_taken, 1)
                            act.wait_ge(unit0_taken, n + 1)
                            to = decay_fwd if d == 0 else decay_back
                            steps(act.activation(to[:, h], root[:, h], ACT.Exp,
                                                 scale=sp[:, 6, c:c + 1], bias=sp[:, 6, c:c + 1]))
                            steps(act.activation(root[:, h], root[:, h], ACT.Tanh,
                                                 scale=sp[:, 7, c:c + 1], bias=sp[:, 7, c:c + 1]))
                        else:
                            act.activation((h_fwd if d == 0 else h_back)[:, h], bank, ACT.Tanh, scale=0.5,
                                           bias=half_b[:, 1, c:c + 1]).then_inc(unit0_taken, 1)
                            if h % GROUP == GROUP - 1:
                                hs = root[:, h + 1 - GROUP:h + 1]
                                act.activation(hs, hs, ACT.Sqrt, scale=0.25).then_inc(roots, 1)
                    for _ in range(AFTER.get(UNITS0[n], 0)):
                        take_rows(next_piece)
                        next_piece += 1
                for side, norm in enumerate(norms0):
                    if side == 1:
                        act.wait_ge(norms0[0].summed, KT)
                    if side == 0:
                        act.wait_ge(rows_out, OUT_AT)
                    norm.act_squares(act, after=(even_added, KT * side))
                    if side == 1:
                        take_rows(OUT_AT)
                    norm.act_root(act)
                    norm.act_affine(act, [slice(0, SEG)],
                                    lambda d, _: gain[:, 0, 1, d, side:side + 1],
                                    lambda d, _: modc[:, 0, 3, d, side:side + 1])
                for i in range(OUT_AT + 1, PIECES):
                    take_rows(i)

            @block.vector
            def _(dve):
                steps = Steps(dve, dve_steps)
                dve.memset(ones[:], 1.0).then_inc(ones_set, 1)
                steps(dve.memset(select[:], 0.0))
                for c in range(2):
                    dve.memset(select[:, c, c:c + 1], 1.0).then_inc(select_set, 1)
                dve.wait_ge(cond_tanh, 1)
                steps(dve.scalar_tensor_tensor(out=silu[:], in0=silu[:], scalar=1.0, in1=col("cond"),
                                               op0=ALU.add, op1=ALU.mult))
                dve.tensor_scalar(silu[:], silu[:], 0.5, None, ALU.mult).then_inc(silu_ready, 1)
                lam = col("rg_lam").rearrange("p d h -> p (d h)")
                steps(dve.tensor_scalar(sp[:, 0], lam, -1.0, 0.0, ALU.mult, ALU.max))
                dve.scalar_tensor_tensor(out=sp[:, 1], in0=lam, scalar=-1.0, in1=lam, op0=ALU.mult,
                                         op1=ALU.max).then_inc(lam_abs, 1)
                for n, b in enumerate(("rg_ba", "rg_bx")):
                    steps(dve.tensor_scalar(half_b[:, n], col(b).rearrange("p d h -> p (d h)"), 0.5,
                                            None, ALU.mult))
                steps(dve.memset(xpad[:, :, :, 0:2], 0.0))
                steps(dve.memset(dft_w[:], 0.0))
                dve.memset(xpad[:, :, :, 2 + SEG:], 0.0).then_inc(pads_set, 1)
                dve.wait_ge(lam_exp, 1)
                softplus_tail(dve, steps, sp[:, 1], sp[:, 2], sp[:, 3], sp[:, 4])
                steps(dve.tensor_tensor(sp[:, 4], sp[:, 4], sp[:, 0], ALU.add))
                steps(dve.tensor_scalar(sp[:, 6], sp[:, 4], -4.0, None, ALU.mult))
                dve.tensor_scalar(sp[:, 7], sp[:, 4], 2.0, None, ALU.mult).then_inc(sp_ready, 1)
                mix0.dve_mean(dve)
                mix0.dve_scale(dve, steps)

                def take_modulation(layer, which, halves):
                    size = which.stop - which.start
                    at = (layer * N_MOD + which.start) * KT
                    steps(dve.tensor_tensor(
                        modc[:, layer, which].rearrange("p w k s -> p (w k) s"),
                        mod_ps.rearrange("p (a s) -> p a s", s=2)[:, at:at + size * KT],
                        col("mod_b")[:, layer, which.start * KT:which.stop * KT].unsqueeze(2).to_broadcast(
                            [P, size * KT, 2]), ALU.add))
                    for half in halves:
                        dve.scalar_tensor_tensor(
                            out=gain[:, layer, half], in0=modc[:, layer, 3 * half + 1], scalar=1.0,
                            in1=col("norm_g")[:, layer, half].unsqueeze(2).to_broadcast([P, KT, 2]),
                            op0=ALU.add, op1=ALU.mult).then_inc(mod_ready, 1)

                dve.wait_ge(mod_turned, FIRST)
                take_modulation(0, slice(0, 2), (0,))

                def multiply(i, ks):
                    if ks.start == 0:
                        dve.wait_ge(piece_loaded[i % MOD_RING], 16 * (i // MOD_RING + 1))
                        if i == ON_VECTOR[0]:
                            dve.wait_ge(mix0.summed, KT)
                        else:
                            dve.wait_ge(rows_out, ON_VECTOR[ON_VECTOR.index(i) - 1] + 1)
                    for k in ks:
                        for c in range(2):
                            if k == 0:
                                last = dve.tensor_scalar(row_parts[:, c], mod_ring[:, i % MOD_RING, k],
                                                         silu[:, k, c:c + 1], None, ALU.mult)
                            else:
                                last = dve.scalar_tensor_tensor(
                                    out=row_parts[:, c], in0=mod_ring[:, i % MOD_RING, k],
                                    scalar=silu[:, k, c:c + 1], in1=row_parts[:, c], op0=ALU.mult,
                                    op1=ALU.add)
                            if c == 0:
                                last.then_inc(part0, 1)
                            elif k < KT - 1:
                                last.then_inc(part1, 1)
                        if k < KT - 1:
                            count = ON_VECTOR.index(i)
                            dve.wait_ge(part0, count * KT + k + 1)
                            dve.wait_ge(part1, count * (KT - 1) + k + 1)
                    if ks.stop == KT:
                        last.then_inc(parts_made, 1)

                dve.wait_ge(pads_set, 1)
                w = col("rg_conv_w")
                for h in range(RG_H):
                    dve.wait_ge(unit0_taken, unit0["proj", h])
                    at = xc[:, h].rearrange("p (s t) -> p s t", s=2)
                    steps(dve.tensor_scalar(at, xpad[:, h, :, 0:SEG], w[:, h, 0:1],
                                            col("rg_conv_b")[:, h:h + 1], ALU.mult, ALU.add))
                    for i in range(1, CONV_W):
                        last = dve.scalar_tensor_tensor(out=at, in0=xpad[:, h, :, i:i + SEG],
                                                        scalar=w[:, h, i:i + 1], in1=at, op0=ALU.mult,
                                                        op1=ALU.add)
                        if i < CONV_W - 1:
                            steps(last)
                    last.then_inc(xc_ready, 1)
                    if 1 <= h < 5:
                        multiply(ON_VECTOR[0], range(2 * h - 2, 2 * h))
                multiply(ON_VECTOR[1], range(KT))
                dve.wait_ge(small_product, 1)
                small = ps[:, 0, 0:256].rearrange("p (j m e) -> p j m e", j=2, m=2)
                for g in range(2):
                    rows = slice(64 * g, 64 * g + 64)
                    dve.tensor_copy(dft_w[rows, :, :, 64 * g:64 * g + 64], small[rows]).then_inc(dft_w_ready, 1)

                def direction(d, group):
                    hs = slice(GROUP * group, GROUP * group + GROUP)
                    state, decay = (h_fwd, decay_fwd) if d == 0 else (h_back, decay_back)
                    dve.wait_ge(unit0_taken, unit0["gate", d, hs.stop - 1, 1])
                    steps(dve.scalar_tensor_tensor(out=state[:, hs], in0=state[:, hs], scalar=1.0,
                                                   in1=xc[:, hs], op0=ALU.add, op1=ALU.mult))
                    dve.wait_ge(roots, 2 * d + group + 1)
                    dve.tensor_tensor(state[:, hs], state[:, hs], root[:, hs], ALU.mult).then_inc(root_used, 1)
                    dve.wait_ge(root_used, 2 * d + group + 1)
                    steps(dve.scalar_tensor_tensor(out=state[:, hs], in0=decay[:, hs], scalar=1.0,
                                                   in1=state[:, hs], op0=ALU.add, op1=ALU.mult))
                    for h in range(hs.start, hs.stop):
                        if d == 0:
                            steps(dve.tensor_tensor_scan(out=state[:, h], data0=decay[:, h],
                                                         data1=state[:, h], initial=0.0,
                                                         op0=ALU.mult, op1=ALU.add))
                        else:
                            for s, first in ((0, 0.0), (1, state[:, h, 0:1])):
                                at = state[:, h, segs[s]][:, ::-1]
                                steps(dve.tensor_tensor_scan(
                                    out=at, data0=decay[:, h, segs[s]][:, ::-1], data1=at,
                                    initial=first, op0=ALU.mult, op1=ALU.add))

                for d in range(2):
                    for group in range(2):
                        direction(d, group)
                    if d == 0:
                        for i in ON_VECTOR[2:]:
                            multiply(i, range(KT))
                for h in range(RG_H):
                    steps(dve.tensor_tensor(h_back[:, h], h_back[:, h], h_fwd[:, h], ALU.add))
                    dve.tensor_tensor(mixT[:, h], h_back[:, h], gate[:, h], ALU.mult).then_inc(mix_ready, 1)
                dve.wait_ge(mod_turned, OUT_AT)
                take_modulation(0, slice(2, N_MOD), (1,))
                dve.wait_ge(mod_ready, 2)
                for side in range(2):
                    for n in range(KT):
                        unit = KT * side + n
                        dve.wait_ge(even_out, unit + 1)
                        dve.scalar_tensor_tensor(
                            out=hT[:, n, segs[side]], in0=ps[:, BANK[unit % 4], 0:SEG],
                            scalar=modc[:, 0, 2, n, side:side + 1], in1=hT[:, n, segs[side]],
                            op0=ALU.mult, op1=ALU.add).then_inc(even_added, 1)
                        if (side, n) == (1, 1):
                            norms0[0].dve_mean(dve)
                        if (side, n) == (1, 3):
                            norms0[0].dve_scale(dve, steps)
                norms0[1].dve_mean(dve)
                norms0[1].dve_scale(dve, steps)
                dve.wait_ge(mod_turned, PIECES)
                take_modulation(1, slice(0, N_MOD), (0, 1))

            @block.tensor
            def _(pe):
                def turn_rows(i):
                    pe.wait_ge(rows_taken, i + 1)
                    for jj in range(PIECE_J):
                        at = 2 * (PIECE_J * i + jj)
                        last = pe.transpose(mod_ps[:, at:at + 2], mod_rows[:, i % 2, jj * P:(jj + 1) * P],
                                            ident[0:2, 0:2])
                    last.then_inc(mod_turned, 1)

                def piece(i):
                    if i >= 2:
                        pe.wait_ge(rows_taken, i - 1)
                    if i in ON_VECTOR:
                        pe.wait_ge(parts_made, ON_VECTOR.index(i) + 1)
                        for c in range(2):
                            last = pe.matmul(rows_ps[i % 2], select[:, c], row_parts[:, c],
                                             start=(c == 0), stop=(c == 1))
                    else:
                        pe.wait_ge(piece_loaded[i % MOD_RING], 16 * (i // MOD_RING + 1))
                        for k in range(KT):
                            last = pe.matmul(rows_ps[i % 2], silu[:, k], mod_ring[:, i % MOD_RING, k],
                                             start=(k == 0), stop=(k == KT - 1))
                    last.then_inc(rows_out, 1)
                    if i not in (0, FIRST, OUT_AT):
                        turn_rows(i - 1)

                pe.wait_ge(silu_ready, 1)
                pe.wait_ge(select_set, 2)
                for i in range(FIRST):
                    piece(i)
                    if i == 1:
                        pe.wait_ge(ones_set, 1)
                        mix0.pe_sums(pe, ones[:])
                turn_rows(FIRST - 1)
                rg_w = field(even_w, EVEN, "rg_w")
                next_piece = FIRST
                for n, (kind, i, *rest) in enumerate(UNITS0):
                    bank = ps[:, BANK[n % 4], :]
                    if n >= 4:
                        pe.wait_ge(unit0_taken, n - 3)
                    if kind == "proj":
                        if i % 2 == 0:
                            pe.wait_ge(w_in_loaded[i // 2], 16)
                        for k in range(KT):
                            if i == 0:
                                pe.wait_ge(mix0.ready, k + 1)
                            last = pe.matmul(bank, w_in[:, i // 2, k, i % 2 * P:i % 2 * P + P], uT[:, k],
                                             start=(k == 0), stop=(k == KT - 1))
                    elif kind == "gate":
                        h, which = rest
                        if (i, which) == (0, 0):
                            pe.wait_ge(xc_ready, h + 1)
                            pe.wait_ge(even_w_loaded, 16)
                        last = pe.matmul(bank, rg_w[:, which, i, h], xc[:, h], start=True, stop=True)
                    elif kind == "chan":
                        if i == 0:
                            pe.wait_ge(dft_w_ready, 2)
                            pe.wait_ge(unit0_taken, unit0["proj", EV_J - 1])
                        j, tt = i // 4, i % 4
                        last = pe.matmul(bank[:, 0:2 * P], xf[:, j, tt * P:(tt + 1) * P],
                                         dft_w[:, j].rearrange("p m e -> p (m e)"), start=True, stop=True)
                    else:
                        if i == 0:
                            pe.wait_ge(unit0_taken, unit0["chan", 7])
                        j, s = i // 2, i % 2
                        for tl in range(2):
                            for m in range(2):
                                last = pe.matmul(bank[:, 0:SEG], xw[:, 2 * s + tl, j, m * P:(m + 1) * P],
                                                 const("time_dft")[:, m, tl], start=(tl + m == 0),
                                                 stop=(tl + m == 2))
                    last.then_inc(unit0_out, 1)
                    if (kind, i) == ("proj", RG_H + 2):
                        pe.wait_ge(consts_loaded, 16)
                        pe.wait_ge(mix0.mean, 1)
                        for j in range(2):
                            for m in range(2):
                                last = pe.matmul(ps[:, 0, (2 * j + m) * 64:(2 * j + m) * 64 + 64],
                                                 const("chan_dft")[:, m], field(even_w, EVEN, "fn_w")[:, j],
                                                 start=True, stop=True)
                        last.then_inc(small_product, 1)
                    for _ in range(AFTER.get(UNITS0[n], 0)):
                        piece(next_piece)
                        next_piece += 1
                turn_rows(OUT_AT - 1)
                pe.wait_ge(unit0_taken, len(UNITS0))
                pe.wait_ge(w_out_loaded, 16)
                pe.wait_ge(mix_ready, RG_H)
                for side in range(2):
                    for n in range(KT):
                        unit = KT * side + n
                        if unit >= 4:
                            pe.wait_ge(even_added, unit - 3)
                        for k in range(KT):
                            last = pe.matmul(ps[:, BANK[unit % 4], 0:SEG], w_out[:, k, n * P:(n + 1) * P],
                                             mixT[:, k, segs[side]], start=(k == 0), stop=(k == KT - 1))
                        last.then_inc(even_out, 1)
                        if (side, n) == (1, 1):
                            norms0[0].pe_sums(pe, ones[:])
                pe.wait_ge(mod_ready, 2)
                for i in range(OUT_AT, PIECES):
                    piece(i)
                    if i == OUT_AT:
                        pe.wait_ge(norms0[0].mean, 1)
                        norms0[1].pe_sums(pe, ones[:])
                turn_rows(PIECES - 1)
        even_stack.close()
        end_phase()

        def peer(layer, first_token, tiles, late=None, ahead=None):
            name = f"peer{layer}"
            stack = ExitStack()

            def psb(what, shape, dt=F32):
                return stack.enter_context(nc.sbuf_tensor(f"{name}_{what}", shape, dt))

            def psem(what):
                return sem(f"{name}_{what}")

            seg_of = 0 if first_token == 0 else 1
            u_rows = psb("u_rows", [P, U_RING, D])
            v_rows, _ = view(weights, peer_free, V_RING, D)
            diag = psb("diag", [P, TOPK, P])
            xs = psb("xs", [P, KT, P])
            q_sb = psb("q", [P, 2, P])
            scores = psb("scores", [P, PH, 2, NK])
            vals = psb("vals", [P, 2, TOPK])
            ids = psb("ids", [P, 2, TOPK], U32)
            ids_f = psb("ids_f", [P, 2, TOPK])
            sums = psb("sums", [P, TOPK, TOPK])
            top = psb("top", [P, TOPK])
            pos = psb("pos", [P, TOPK], U32)
            pair = psb("pair", [P, 2, TOPK], U32)
            pair_f = psb("pair_f", [P, 2, TOPK])
            hot = psb("hot", [P, 2, TOPK, TOPK])
            picked = psb("picked", [P, 2, TOPK])
            expert = psb("expert", [P, PH, TOPK], I32)
            soft = psb("soft", [P, 2, TOPK + 4])
            g_half = psb("g_half", [P, TOPK])
            dot = psb("dot", [P, 2, TOPK])
            gelu_t = psb("gelu_t", [P, 2, TOPK])
            xg = psb("xg", [P, TOPK])
            weight = psb("weight", [P, PH, TOPK])

            w_q_loaded = [psem(f"w_q_loaded{c}") for c in (2, 3)]
            u_landed = [psem(f"u_landed{r}") for r in range(U_RING)]
            v_landed = [psem(f"v_landed{r}") for r in range(V_RING)]
            turn = psem("turn")
            pause = psem("pause")
            own = psem("choice_steps")
            staged = psem("staged")
            q_product, q_taken = psem("q_product"), psem("q_taken")
            s_product, s_taken = psem("s_product"), psem("s_taken")
            scores_used = psem("scores_used")
            soft_in, soft_out = psem("soft_in"), psem("soft_out")
            expert_ready = psem("expert_ready")
            dots_done = psem("dots_done")
            gelu_in, gelu_out = psem("gelu_in"), psem("gelu_out")
            weight_ready = psem("weight_ready")
            diag_ready = psem("diag_ready")
            v_added = psem("v_added")
            f_ready = psem("f_ready")
            sum_taken = psem("sum_taken")
            y_turned = psem("y_turned")
            y_added = psem("y_added")

            f_tok = ps[:, 0:2, :].rearrange("p a b -> p (a b)")
            acc = ps[:, 2:4, :]
            q_ps, s_ps = ps[:, 4, 0:2 * P], ps[:, 5, 0:2 * NK]
            dve_steps = psem("dve_steps")
            norm = late and peer_norm(layer, late, 6)
            next_norm = ahead and ahead(4)

            def tokens_of(t):
                return bass.ds(t * P + first_token, P)

            with nc.Block() as block:
                @block.sync
                def _(sp_eng):
                    for c in (2, 3):
                        sp_eng.dma_start(w_q[c], peer_q[layer, c]).then_inc(w_q_loaded[c - 2], 16)

                @block.gpsimd
                def _(pool):
                    def gather_u(t, s):
                        if s % TOPK == 0:
                            pool.wait_ge(expert_ready, t * PH + (s // TOPK + 1))
                            pool.sem_inc(turn, 1)
                        pool.wait_ge(dots_done, t * SLOTS + (s + 1))
                        pool.sem_inc(turn, 1)
                        pool.indirect_dma_start(
                            out=u_rows[:, s % U_RING, :], out_offset=None, in_=peer_u[layer],
                            in_offset=bass.IndirectOffsetOnAxis(
                                ap=expert[:, s // TOPK, s % TOPK:s % TOPK + 1], axis=0)
                        ).then_inc(u_landed[s % U_RING], 16)

                    def gather_v(t, s):
                        pool.wait_ge(v_added, t * SLOTS + (s + 1 + SLOTS - V_RING))
                        pool.sem_inc(turn, 1)
                        pool.indirect_dma_start(
                            out=v_rows[:, s % V_RING, :], out_offset=None, in_=peer_v[layer],
                            in_offset=bass.IndirectOffsetOnAxis(
                                ap=expert[:, s // TOPK, s % TOPK:s % TOPK + 1], axis=0)
                        ).then_inc(v_landed[s % V_RING], 16)

                    def tile(t, more):
                        for s in range(SLOTS):
                            if s + LAG < SLOTS:
                                gather_u(t, s + LAG)
                            elif more:
                                gather_u(t + 1, s + LAG - SLOTS)
                            gather_v(t, s)

                    for s in range(LAG):
                        gather_u(0, s)
                    with pool.Fori(0, tiles - 1) as t:
                        tile(t, True)
                    tile(tiles - 1, False)

                @block.scalar
                def _(act):
                    def stage(t):
                        act.activation(xs[:], uT[:, :, tokens_of(t)], ACT.Copy).then_inc(staged, 1)

                    def take_q(n):
                        act.wait_ge(q_product, n + 1)
                        act.activation(q_sb[:].rearrange("p a b -> p (a b)"), q_ps, ACT.Copy).then_inc(q_taken, 1)

                    def take_scores(n, h):
                        act.wait_ge(scores_used, n + 1)
                        act.wait_ge(s_product, n + 1)
                        act.activation(scores[:, h].rearrange("p a b -> p (a b)"), s_ps, ACT.Copy).then_inc(s_taken, 1)

                    def soften(n, i):
                        act.wait_ge(soft_in, n + 1)
                        act.activation(soft[:, i, 0:TOPK], top[:], ACT.Exp, bias=soft[:, i, TOPK:TOPK + 1],
                                       accum_out=soft[:, i, TOPK + 1:TOPK + 2]).then_inc(soft_out, 1)

                    def tile(t, more):
                        for j in range(PH):
                            if j == 4 and more:
                                act.wait_ge(q_product, t * PH + PH)
                                act.wait_ge(f_ready, t + 1)
                                stage(t + 1)
                            act.wait_ge(gelu_in, t * PH + (j + 1))
                            act.activation(gelu_t[:, 1], gelu_t[:, 0], ACT.Tanh, scale=GELU_S).then_inc(gelu_out, 1)
                            for k in range(TOPK):
                                s = j * TOPK + k
                                if k == 0:
                                    act.wait_ge(weight_ready, t * PH + (j + 1))
                                if k == 3 and (j < 4 or more):
                                    take_q(t * PH + (j + 4))
                                if k == 0 and (j < 6 or more):
                                    soften(t * PH + (j + 2), j % 2)
                                if k == 6 and (j < 4 or more):
                                    take_scores(t * PH + (j + 4), (j + 4) % PH)
                                if next_norm and not more and (j, k) == (6, 0):
                                    act.wait_ge(y_added, 2 * next_norm.tokens // P)
                                    next_norm.act_squares(act)
                                if next_norm and not more and (j, k) == (7, 8):
                                    next_norm.act_root(act)
                                act.wait_ge(v_added, t * SLOTS + (s + 1 + SLOTS - TOPK))
                                act.activation(diag[:, k], ident, ACT.Copy,
                                               scale=weight[:, j, k:k + 1]).then_inc(diag_ready, 1)
                        if next_norm and not more:
                            if layer == 0:
                                next_norm.act_affine(act, [slice(0, SEG)],
                                                     lambda d, _: gain[:, 1, 0, d, 0:1],
                                                     lambda d, _: modc[:, 1, 0, d, 0:1])
                            else:
                                next_norm.act_affine(act, [slice(0, P)],
                                                     lambda d, _: col("final_g")[:, d:d + 1], None)
                        act.wait_ge(v_added, t * SLOTS + 2 * SLOTS)
                        at = uT[:, :, tokens_of(t)]
                        for half in range(2):
                            last = act.activation(at[:, 4 * half:4 * half + 4, :],
                                                  acc[:, half].rearrange("p (a b) -> p a b", a=4), ACT.Copy)
                        last.then_inc(sum_taken, 1)

                    stage(0)
                    for n in range(4):
                        take_q(n)
                        take_scores(n, n)
                        if n in (1, 2):
                            soften(n - 1, n - 1)
                        if n == 1 and norm:
                            norm.act_squares(act)
                            norm.act_root(act)
                    if norm:
                        norm.act_affine(act, [slice(0, norm.tokens)], lambda d, _: gain[:, layer, 1, d, 1:2],
                                        lambda d, _: modc[:, layer, 3, d, 1:2])
                    with act.Fori(0, tiles - 1) as t:
                        tile(t, True)
                    tile(tiles - 1, False)

                @block.vector
                def _(dve):
                    dve.sem_inc(dots_done, U_RING)
                    dve.sem_inc(scores_used, PH)
                    def choice(chain, k, n, h, behind=True):
                        halves = [(scores[:, h, i], vals[:, i], ids[:, i]) for i in range(2)]
                        grid = sums[:].rearrange("p a b -> p (a b)")
                        full = [P, 2, TOPK, TOPK]
                        if k == 0:
                            dve.wait_ge(s_taken, n + 1)
                            dve.wait_ge(v_added, n * TOPK + TOPK)
                            dve.sem_inc(pause, 1)
                            for src, values, _ in halves:
                                chain(dve.max(values[:, 0:8], src))
                        elif k == 1:
                            for src, values, places in halves:
                                chain(dve.max_index(places[:, 0:8], values[:, 0:8], src))
                        elif k == 2:
                            for src, values, _ in halves:
                                chain(dve.match_replace(src, values[:, 0:8], src, NEG))
                        elif k == 3:
                            for src, values, _ in halves:
                                chain(dve.max(values[:, 8:16], src))
                        elif k == 4:
                            chain(dve.max_index(ids[:, 0, 8:16], vals[:, 0, 8:16], scores[:, h, 0]))
                            dve.max_index(ids[:, 1, 8:16], vals[:, 1, 8:16],
                                          scores[:, h, 1]).then_inc(scores_used, 1)
                        elif k == 5:
                            dve.wait_ge(scores_used, n + (PH + 1))
                            if behind:
                                dve.wait_ge(soft_out, n)
                            chain(dve.tensor_tensor(
                                sums[:], vals[:, 0].unsqueeze(2).to_broadcast([P, TOPK, TOPK]),
                                vals[:, 1].unsqueeze(1).to_broadcast([P, TOPK, TOPK]), ALU.add))
                        elif k == 6:
                            chain(dve.max(top[:, 0:8], grid))
                        elif k == 7:
                            chain(dve.max_index(pos[:, 0:8], top[:, 0:8], grid))
                            chain(dve.tensor_scalar(soft[:, h % 2, TOPK:TOPK + 1], top[:, 0:1], -1.0,
                                                    None, ALU.mult))
                        elif k == 8:
                            chain(dve.match_replace(grid, top[:, 0:8], grid, NEG))
                        elif k == 9:
                            chain(dve.max(top[:, 8:16], grid))
                        elif k == 10:
                            dve.tensor_copy(ids_f[:], ids[:]).then_inc(soft_in, 1)
                            chain(dve.max_index(pos[:, 8:16], top[:, 8:16], grid))
                        elif k == 11:
                            chain(dve.tensor_single_scalar(pair[:, 0], pos[:], 4, ALU.logical_shift_right))
                            chain(dve.tensor_single_scalar(pair[:, 1], pos[:], TOPK - 1, ALU.bitwise_and))
                        elif k == 12:
                            chain(dve.tensor_copy(pair_f[:], pair[:]))
                        elif k == 13:
                            chain(dve.tensor_tensor(
                                hot[:], pair_f[:].unsqueeze(3).to_broadcast(full),
                                const("iota").unsqueeze(1).unsqueeze(1).to_broadcast(full), ALU.is_equal))
                        elif k == 14:
                            dve.wait_ge(soft_in, n + 1)
                            chain(dve.tensor_tensor(hot[:], hot[:], ids_f[:].unsqueeze(2).to_broadcast(full), ALU.mult))
                        else:
                            chain(dve.tensor_reduce(picked[:], hot[:], AX, ALU.add))
                            dve.scalar_tensor_tensor(out=expert[:, h], in0=picked[:, 0], scalar=float(NK),
                                                     in1=picked[:, 1], op0=ALU.mult,
                                                     op1=ALU.add).then_inc(expert_ready, 1)

                    def weigh(t, j):
                        dve.wait_ge(gelu_out, t * PH + (j + 1))
                        dve.scalar_tensor_tensor(out=weight[:, j], in0=gelu_t[:, 1], scalar=1.0, in1=xg[:],
                                                 op0=ALU.add, op1=ALU.mult).then_inc(weight_ready, 1)

                    def fold(n):
                        t = n // 2
                        dve.wait_ge(y_turned, n + 1)
                        for i in range(4):
                            d = n % 2 * 4 + i
                            at = hT[:, d, first_token + t * P:first_token + (t + 1) * P]
                            side = seg_of + t // 2
                            last = dve.scalar_tensor_tensor(
                                out=at, in0=ps[:, 6 + n % 2, i * P:i * P + P],
                                scalar=modc[:, layer, 5, d, side:side + 1], in1=at, op0=ALU.mult,
                                op1=ALU.add)
                        last.then_inc(y_added, 1)

                    def tile(chain, t, more):
                        for j in range(PH):
                            if j == 0:
                                dve.wait_ge(f_ready, t + 1)
                            for k in range(TOPK):
                                s = j * TOPK + k
                                r = s % U_RING
                                dve.wait_ge(u_landed[r], t * (16 * SLOTS // U_RING) + 16 * (s // U_RING + 1))
                                dve.tensor_tensor_reduce(
                                    out=u_rows[:, r], in0=u_rows[:, r], in1=f_tok, scale=1.0, scalar=0.0,
                                    op0=ALU.mult, op1=ALU.add,
                                    accum_out=dot[:, j % 2, k:k + 1]).then_inc(dots_done, 1)
                                if k == 1 and j > 0:
                                    weigh(t, j - 1)
                                if not more and k == 15 and 2 <= j < 2 * tiles:
                                    fold(j - 2)
                                if k == 12:
                                    dve.wait_ge(soft_out, t * PH + (j + 1))
                                    chain(dve.reciprocal(soft[:, j % 2, TOPK + 2:TOPK + 3],
                                                         soft[:, j % 2, TOPK + 1:TOPK + 2]))
                                if k == 13:
                                    chain(dve.tensor_scalar(g_half[:], soft[:, j % 2, 0:TOPK],
                                                            soft[:, j % 2, TOPK + 2:TOPK + 3], 0.5,
                                                            ALU.mult, ALU.mult))
                                if j < 6 or more:
                                    choice(chain, k, t * PH + (j + 2), (j + 2) % PH)
                            dve.wait_ge(dots_done, t * SLOTS + ((j + 1) * TOPK + U_RING))
                            d = dot[:, j % 2]
                            chain(dve.tensor_tensor(gelu_t[:, 0], d, d, ALU.mult))
                            chain(dve.tensor_scalar(gelu_t[:, 0], gelu_t[:, 0], GELU_C, 1.0, ALU.mult, ALU.add))
                            dve.tensor_tensor(gelu_t[:, 0], gelu_t[:, 0], d, ALU.mult).then_inc(gelu_in, 1)
                            chain(dve.tensor_tensor(xg[:], d, g_half[:], ALU.mult))
                            if j == PH - 1:
                                weigh(t, j)

                    chain = Steps(dve, own)
                    for n in range(2):
                        for k in range(TOPK):
                            choice(chain, k, n, n, behind=n > 0)
                        if n == 0 and norm:
                            norm.dve_mean(dve)
                    norm_steps = Steps(dve, dve_steps)
                    if norm:
                        norm.dve_scale(dve, norm_steps)
                    with dve.Fori(0, tiles - 1) as t:
                        dve.sem_clear(own)
                        tile(Steps(dve, own), t, True)
                    dve.sem_clear(own)
                    tile(Steps(dve, own), tiles - 1, False)
                    if next_norm:
                        next_norm.dve_mean(dve)
                        next_norm.dve_scale(dve, norm_steps)
                    for n in range(2 * tiles - 2, 2 * tiles):
                        fold(n)

                @block.tensor
                def _(pe):
                    pe.sem_inc(v_added, SLOTS)
                    pe.sem_inc(sum_taken, 1)

                    def query(n, h, free):
                        if free is not None:
                            pe.wait_ge(q_taken, free)
                        for half in range(2):
                            hp = 2 * h + half
                            for k in range(KT):
                                last = pe.matmul(q_ps[:, half * P:half * P + P],
                                                 w_q[hp // 4][:, k, hp % 4 * P:hp % 4 * P + P], xs[:, k],
                                                 start=(k == 0), stop=(k == KT - 1))
                        last.then_inc(q_product, 1)

                    def score(n, h, free):
                        pe.wait_ge(q_taken, n + 1)
                        if free is not None:
                            pe.wait_ge(s_taken, free)
                        for half in range(2):
                            last = pe.matmul(s_ps[:, half * NK:half * NK + NK], q_sb[:, half], keys[:, h, half],
                                             start=True, stop=True)
                        last.then_inc(s_product, 1)

                    def by_token(t):
                        for d in range(KT):
                            last = pe.transpose(f_tok[:, d * P:(d + 1) * P], xs[:, d], ident)
                        last.then_inc(f_ready, 1)

                    def turn(n):
                        t = n // 2
                        if n >= 2:
                            pe.wait_ge(y_added, n - 1)
                        for i in range(4):
                            last = pe.transpose(
                                ps[:, 6 + n % 2, i * P:i * P + P],
                                uT[:, n % 2 * 4 + i, first_token + t * P:first_token + (t + 1) * P], ident)
                        last.then_inc(y_turned, 1)

                    def tile(t, more):
                        for j in range(PH):
                            for k in range(TOPK):
                                if not more and k == 8 and j < 2 * tiles - 2:
                                    turn(j)
                                if next_norm and not more and (j, k) == (6, 0):
                                    next_norm.pe_sums(pe, ones[:])
                                s = j * TOPK + k
                                r = s % V_RING
                                if s == 0:
                                    pe.wait_ge(sum_taken, t + 1)
                                pe.wait_ge(v_landed[r], t * (16 * SLOTS // V_RING) + 16 * (s // V_RING + 1))
                                pe.wait_ge(diag_ready, t * SLOTS + (s + 1))
                                for half in range(2):
                                    last = pe.matmul(acc[:, half], diag[:, k], v_rows[:, r, half * 512:half * 512 + 512],
                                                     start=(s == 0), stop=(s == SLOTS - 1))
                                last.then_inc(v_added, 1)
                                if k == 2 and (j < 4 or more):
                                    if j == 4:
                                        pe.wait_ge(staged, t + 2)
                                    query(t * PH + (j + 4), (j + 4) % PH, t * PH + (j + 4))
                                if k == 5 and (j < 4 or more):
                                    score(t * PH + (j + 4), (j + 4) % PH, t * PH + (j + 4))
                            if j == 6 and more:
                                pe.wait_ge(dots_done, t * SLOTS + (SLOTS + U_RING))
                                by_token(t + 1)

                    pe.wait_ge(staged, 1)
                    for n in range(4):
                        query(n, n, n if n else None)
                        score(n, n, n if n else None)
                        if n == 1 and norm:
                            norm.pe_sums(pe, ones[:])
                    by_token(0)
                    for arrived in w_q_loaded:
                        pe.wait_ge(arrived, 16)
                    with pe.Fori(0, tiles - 1) as t:
                        tile(t, True)
                    tile(tiles - 1, False)
                    pe.wait_ge(sum_taken, tiles + 1)
                    for n in range(2 * tiles - 2, 2 * tiles):
                        turn(n)
                    pe.wait_ge(y_added, 2 * tiles)
            stack.close()
            end_phase()

        peer(0, 0, T // P, ahead=lambda bank: mix1_norm(0, bank))
        odd_stack = ExitStack()

        def osb(name, shape):
            return odd_stack.enter_context(nc.sbuf_tensor(name, shape, F32))

        N_LAT = SEG
        width = dict(ODD_PARTS)
        part_at, at = {}, 0
        for part, n in ODD_PARTS:
            part_at[part] = at
            at += KT * n
        od_w = weights
        uq_w = osb("uq_w", [P, Q_LORA // P, MLA_H * QD])
        uk_w = osb("uk_w", [P, KV_LORA // P, MLA_H, NOPE])
        uv_w = osb("uv_w", [P, KV_LORA // P, MLA_H * VD])
        work = osb("odd_work", [P, 10600])

        def od_part(part):
            at = part_at[part]
            return od_w[:, at:at + KT * width[part]].rearrange("p (k n) -> p k n", k=KT)

        at = 0
        PADDED = SEG + CONV_W - 1
        q_pad, at = view(work, at, ML_H, PADDED)
        k_pad, at = view(work, at, ML_H, 2, PADDED)
        after_pads = at
        v_tok, at = view(work, at, T // P, ML_H * P)
        o_tanh, at = view(work, at, ML_H, N_LAT)
        cq, at = view(work, at, Q_LORA // P, N_LAT)
        ckv, at = view(work, at, KV_LORA // P, T)
        k_rot, at = view(work, at, T)
        v_att, at = view(work, at, T // P, MLA_H * VD)
        g_in, g_forget = squares[:, 0], squares[:, 1]
        probs, at = view(work, 0, 2, T)
        h_sum, at = view(work, at, ML_H, N_LAT)
        cq_rms, at = view(work, at, N_LAT)
        den_abs, at = view(work, at, N_LAT)
        assert at <= after_pads
        qs_ml, at = view(od_w, part_at["v"], ML_H, N_LAT)
        ks_ml, at = view(od_w, at, ML_H, T)
        bound, mid = view(od_w, at, 2, N_LAT)
        head_rms, mid = view(od_w, mid, N_LAT)
        th, at = view(od_w, at, 2, T)
        q_att, _ = view(od_w, at, MLA_H, N_LAT)
        chain_b, at = view(od_w, at, 8, T)
        assert at <= part_at["cq"]
        k_att, at = view(od_w, part_at["cq"], MLA_H, T)
        weights_ml, at = view(od_w, at, 2, T // P, N_LAT)
        c_col, at = view(od_w, at, T // P, HALF_ROWS)
        soft_a, at = view(od_w, at, 2, 4)
        h_rec, at = view(od_w, at, N_LAT)
        assert at <= part_at["gates"] + KT * width["gates"], at
        w_out2 = od_w[:, 0:KT * D].rearrange("p (k n) -> p k n", k=KT)
        uT_flat = uT[:].rearrange("p a b -> p (a b)")
        mix2, at = view(uT_flat, 0, KT, N_LAT)
        probs_t, at = view(uT_flat, at, T // P, N_LAT)
        q_raw, at = view(uT_flat, at, 2, N_LAT)
        q_sin, at = view(uT_flat, at, 2, N_LAT)

        part_loaded = {part: sem(f"od_{part}_loaded") for part, _ in ODD_PARTS}
        mla_loaded = sem("mla_weights_loaded")
        w_out2_loaded = sem("od_out_loaded")
        mix1 = mix1_norm(1, 0)
        kv_norm = Norm("kv_norm", sem, lambda d: ckv[:, d], squares, ps[:, 0, :], rms[:],
                       lambda d: ckv[:, d], T, KV_LORA // P)
        q_norm = Norm("q_norm", sem, lambda d: cq[:, d], squares, ps[:, 7, 0:N_LAT], cq_rms,
                      lambda d: cq[:, d], N_LAT, Q_LORA // P)
        PARTS_IN_ORDER = [("gates", 1), ("v", T // P), ("o", ML_H), ("k", ML_H), ("ckv", 2),
                          ("q", ML_H), ("cq", 3), ("krope", 1)]
        PROJECTED = [(part, i) for part, count in PARTS_IN_ORDER for i in range(count)]
        UNITS1 = (PROJECTED + [("va", i) for i in range(T // P)]
                  + [(part, h) for h in range(MLA_H) for part in ("uk", "uq")])
        LAT_ONLY = ("q", "cq", "o")
        unit1 = {u: n + 1 for n, u in enumerate(UNITS1)}
        unit_out, unit_taken = sem("od_unit_out"), sem("od_unit_taken")
        pads2 = sem("od_pads_set")
        forget_abs, forget_exp = sem("forget_abs"), sem("forget_exp")
        conv_done, conv_tanh, qk_ready = sem("ml_conv_done"), sem("ml_conv_tanh"), sem("ml_qk_ready")
        c_ready, c_turned, c_col_ready = sem("ml_c_ready"), sem("ml_c_turned"), sem("ml_c_col_ready")
        stab_in, stab_ready = sem("ml_stab_in"), sem("ml_stab_ready")
        key_swapped, key_ready, k_rope_ready = sem("key_swapped"), sem("key_ready"), sem("k_rope_ready")
        q_swapped, q_ready = sem("q_swapped"), sem("q_ready")
        ml_scores, ml_spread, bound_kept = sem("ml_scores"), sem("ml_spread"), sem("ml_bound_kept")
        ml_arg, ml_exp, ml_weights = sem("ml_arg"), sem("ml_exp"), sem("ml_weights")
        ml_sums, ml_abs, ml_head = sem("ml_sums"), sem("ml_abs"), sem("ml_head")
        out_sq, out_ss, out_ms, out_root = (sem("ml_head_squares"), sem("ml_head_summed"),
                                            sem("ml_head_mean"), sem("ml_head_root"))
        ml_mixed = sem("ml_mixed")
        att_scores, att_max, att_exp = sem("att_scores"), sem("att_max"), sem("att_exp")
        att_sum_inv, att_probs = sem("att_sum_inverse"), sem("att_probs")
        att_turned, att_kept, att_out, att_mixed = (sem("att_turned"), sem("att_kept"),
                                                    sem("att_out"), sem("att_mixed"))
        odd_out, odd_added = sem("odd_out_product"), sem("odd_added")
        early1 = sem("peer1_weights_arrived")
        norm1 = peer_norm(1, slice(SEG, SEG + P), 0)
        dve_steps, act_steps = sem("odd_dve_steps"), sem("odd_act_steps")
        LAT = slice(SEG, T)
        ML_SCALE = 0.25 * P ** -0.5
        ATT_SCALE = QD ** -0.5
        M_UNITS = 2 * ML_H
        assert M_UNITS == MLA_H
        spread_ps, sums_ps, ml_scores_ps = ps[:, 1, :], [ps[:, 3, :], ps[:, 5, :]], ps[:, 6:8, :]
        att_ps = [ps[:, 2, :], ps[:, 4, :]]
        att_out_ps, head_ps = ps[0:VD, 0, 0:N_LAT], ps[:, 0, N_LAT:T]
        key_ps, c_ps = ps[0:QD, 6, 0:N_LAT], ps[:, 7, 0:T // P * HALF_ROWS]
        swap_ps = [ps[0:QD, 5, 0:N_LAT], ps[0:QD, 6, 0:N_LAT]]

        with nc.Block() as block:
            @block.sync
            def _(sp_eng):
                for part, _ in PARTS_IN_ORDER:
                    at = part_at[part]
                    sp_eng.dma_start(od_w[:, at:at + KT * width[part]],
                                     od[:, at:at + KT * width[part]]).then_inc(part_loaded[part], 16)
                sp_eng.dma_start(uv_w[:], w_uv.rearrange("p k h e -> p k (h e)")).then_inc(mla_loaded, 16)
                sp_eng.dma_start(uk_w[:], w_uk).then_inc(mla_loaded, 16)
                sp_eng.dma_start(uq_w[:], w_uq).then_inc(mla_loaded, 16)
                sp_eng.wait_ge(unit_out, unit1["q", ML_H - 1])
                sp_eng.dma_start(w_out2, od_out).then_inc(w_out2_loaded, 16)
                sp_eng.wait_ge(ml_mixed, ML_H)
                sp_eng.wait_ge(att_mixed, MLA_H)
                load_early(sp_eng, 1, early1)
                sp_eng.wait_ge(early1, 16 * EARLY)

            @block.gpsimd
            def _(pool):
                pool.wait_ge(key_ready, 1)
                for h in range(MLA_H):
                    pool.tensor_copy(k_att[NOPE:QD, h], k_rot[NOPE:QD]).then_inc(k_rope_ready, 1)

            @block.scalar
            def _(act):
                steps = Steps(act, act_steps)
                mix1.act_squares(act)
                mix1.act_root(act)
                mix1.act_affine(act, [slice(0, SEG)], lambda d, _: gain[:, 1, 0, d, 1:2],
                                lambda d, _: modc[:, 1, 0, d, 1:2])
                act.wait_ge(pads2, 2)
                gate_b = col("ml_gate_b")

                def silu_tanh(n):
                    act.wait_ge(conv_done, n + 1)
                    size = T if n < ML_H else N_LAT
                    src = ks_ml[:, n] if n < ML_H else qs_ml[:, n - ML_H]
                    act.activation(th[:, n % 2, 0:size], src, ACT.Tanh, scale=0.5).then_inc(conv_tanh, 1)

                for n, (part, i) in enumerate(UNITS1):
                    act.wait_ge(unit_out, n + 1)
                    bank = ps[:, BANK[n % 4], :]
                    if part == "gates":
                        act.activation(g_in[0:HALF_ROWS], bank[0:HALF_ROWS], ACT.Identity,
                                       bias=gate_b[0:HALF_ROWS])
                        last = act.activation(g_forget[0:HALF_ROWS], bank[64:GATE_ROWS], ACT.Identity,
                                              bias=gate_b[64:GATE_ROWS])
                    elif part == "k":
                        last = act.activation(k_pad[:, i, :, 2:2 + SEG],
                                              bank.rearrange("p (s t) -> p s t", s=2), ACT.Copy)
                    elif part == "q":
                        last = act.activation(q_pad[:, i, 2:2 + SEG], bank[:, 0:N_LAT], ACT.Copy)
                    elif part == "ckv":
                        last = act.activation(ckv[:, i], bank, ACT.Copy)
                    elif part == "krope":
                        last = act.activation(k_rot[0:QD], bank[0:QD], ACT.Copy)
                    elif part == "cq":
                        last = act.activation(cq[:, i], bank[:, 0:N_LAT], ACT.Copy)
                    elif part == "v":
                        last = act.activation(v_tok[:, i], bank, ACT.Copy)
                    elif part == "o":
                        last = act.activation(o_tanh[:, i], bank[:, 0:N_LAT], ACT.Tanh, scale=0.5)
                    elif part == "va":
                        last = act.activation(v_att[:, i], bank, ACT.Copy)
                    elif part == "uk":
                        last = act.activation(k_att[0:NOPE, i], bank[0:NOPE], ACT.Copy)
                    else:
                        if i >= 2:
                            act.wait_ge(q_ready, i - 1)
                        last = act.activation(q_raw[0:QD, i % 2], bank[0:QD, 0:N_LAT], ACT.Copy)
                    last.then_inc(unit_taken, 1)
                    if (part, i) == ("k", 0):
                        act.wait_ge(forget_abs, 1)
                        at = chain_b[0:HALF_ROWS, 0]
                        act.activation(at, at, ACT.Exp, scale=-1.0).then_inc(forget_exp, 1)
                    if part == "k":
                        silu_tanh(i)
                    if (part, i) == ("k", 2):
                        act.wait_ge(stab_in, 1)
                        at = chain_b[0:HALF_ROWS, 7, N_LAT:T]
                        act.activation(at, at, ACT.Exp).then_inc(stab_ready, 1)
                    if (part, i) == ("ckv", 1):
                        act.wait_ge(unit_taken, n + 1)
                        kv_norm.act_squares(act)
                    if part == "q":
                        silu_tanh(ML_H + i)
                    if (part, i) == ("q", 0):
                        kv_norm.act_root(act)
                    if (part, i) == ("q", 1):
                        kv_norm.act_affine(act, [slice(0, T)], lambda d, _: col("kv_norm_g")[:, d:d + 1], None)
                    if (part, i) == ("cq", 2):
                        act.wait_ge(unit_taken, n + 1)
                        q_norm.act_squares(act)
                    if (part, i) == ("va", 0):
                        q_norm.act_root(act)
                        q_norm.act_affine(act, [slice(0, N_LAT)], lambda d, _: col("q_norm_g")[:, d:d + 1], None)

                def ml_e(m):
                    act.wait_ge(ml_arg, m + 1)
                    at = weights_ml[:, m % 2]
                    act.activation(at, at, ACT.Exp).then_inc(ml_exp, 1)
                    act.activation(bound[:, m % 2], spread_ps[:, LAT], ACT.Copy).then_inc(bound_kept, 1)

                def keep_abs(m):
                    act.wait_ge(ml_sums, m + 1)
                    act.activation(den_abs, sums_ps[m % 2][:, LAT], ACT.Abs).then_inc(ml_abs, 1)

                def head_squares(h):
                    act.wait_ge(ml_head, 2 * h + 2)
                    act.activation(squares[:, 0, 0:N_LAT], h_sum[:, h], ACT.Square).then_inc(out_sq, 1)

                def head_root(h):
                    act.wait_ge(out_ms, h + 1)
                    act.activation(head_rms[:], head_rms[:], ACT.Sqrt).then_inc(out_root, 1)

                def keep_mixed(h):
                    act.wait_ge(att_out, h + 1)
                    act.activation(mix2[VD * (h % 2):VD * (h % 2) + VD, ML_H + h // 2], att_out_ps,
                                   ACT.Copy).then_inc(att_mixed, 1)

                ml_e(0)
                for m in range(M_UNITS):
                    if m >= 1:
                        keep_abs(m - 1)
                    if m in (3, 5, 7):
                        head_squares((m - 3) // 2)
                    for qt in range(2):
                        act.wait_ge(att_max, 2 * m + qt + 1)
                        act.activation(probs[:, qt], att_ps[qt], ACT.Exp, scale=ATT_SCALE,
                                       bias=soft_a[:, qt, 1:2], accum_out=soft_a[:, qt, 2:3]).then_inc(att_exp, 1)
                    for qt in range(2):
                        act.wait_ge(att_sum_inv, 2 * m + qt + 1)
                        act.activation(probs[:, qt], probs[:, qt], ACT.Copy,
                                       scale=soft_a[:, qt, 3:4]).then_inc(att_probs, 1)
                    if m + 1 < M_UNITS:
                        ml_e(m + 1)
                    if m >= 1:
                        keep_mixed(m - 1)
                    if m in (4, 6):
                        head_root((m - 4) // 2)
                    for qt in range(2):
                        act.wait_ge(att_turned, 2 * m + qt + 1)
                        act.activation(probs_t[:, :, qt * P:(qt + 1) * P],
                                       att_ps[qt].rearrange("p (a b) -> p a b", a=4),
                                       ACT.Copy).then_inc(att_kept, 1)
                keep_abs(M_UNITS - 1)
                head_root(2)
                head_squares(ML_H - 1)
                keep_mixed(M_UNITS - 1)
                head_root(ML_H - 1)
                norm1.act_squares(act, after=(odd_added, 0))
                norm1.act_root(act)
                norm1.act_affine(act, [slice(0, P)], lambda d, _: gain[:, 1, 1, d, 1:2],
                                 lambda d, _: modc[:, 1, 3, d, 1:2])

            @block.vector
            def _(dve):
                steps = Steps(dve, dve_steps)
                mix1.dve_mean(dve)
                mix1.dve_scale(dve, steps)
                q4, k4 = q_pad, k_pad
                steps(dve.memset(q4[:, :, 0:2], 0.0))
                steps(dve.memset(k4[:, :, :, 0:2], 0.0))
                dve.memset(q4[:, :, 2 + SEG:], 0.0).then_inc(pads2, 1)
                dve.memset(k4[:, :, :, 2 + SEG:], 0.0).then_inc(pads2, 1)
                rows = slice(0, HALF_ROWS)
                e, z, z2, lf, run, c, m_run, ns = (chain_b[rows, i] for i in range(8))
                dve.wait_ge(unit_taken, unit1["o", ML_H - 1])
                gf, gi = g_forget[rows], g_in[rows]
                dve.scalar_tensor_tensor(out=e, in0=gf, scalar=-1.0, in1=gf, op0=ALU.mult,
                                         op1=ALU.max).then_inc(forget_abs, 1)
                dve.wait_ge(pads2, 2)
                back = slice(32, HALF_ROWS)

                def convolve(n):
                    i = n % ML_H
                    w = col("ml_conv_w")
                    blk = ML_H + i if n < ML_H else i
                    dve.wait_ge(unit_taken, unit1["k" if n < ML_H else "q", i])
                    if n < ML_H:
                        to = ks_ml[:, i].rearrange("p (s t) -> p s t", s=2)
                        src = lambda a: k4[:, i, :, a:a + SEG]
                    else:
                        to = qs_ml[:, i]
                        src = lambda a: q4[:, i, a:a + SEG]
                    steps(dve.tensor_scalar(to, src(0), w[:, blk, 0:1], col("ml_conv_b")[:, blk:blk + 1],
                                            ALU.mult, ALU.add))
                    for a in range(1, CONV_W):
                        last = dve.scalar_tensor_tensor(out=to, in0=src(a), scalar=w[:, blk, a:a + 1],
                                                        in1=to, op0=ALU.mult, op1=ALU.add)
                        if a < CONV_W - 1:
                            steps(last)
                    last.then_inc(conv_done, 1)
                    dve.wait_ge(conv_tanh, n + 1)
                    size = T if n < ML_H else N_LAT
                    at = ks_ml[:, n] if n < ML_H else qs_ml[:, n - ML_H]
                    dve.scalar_tensor_tensor(out=at, in0=th[:, n % 2, 0:size], scalar=1.0, in1=at,
                                             op0=ALU.add, op1=ALU.mult).then_inc(qk_ready, 1)

                convolve(0)
                dve.wait_ge(forget_exp, 1)
                softplus_tail(dve, steps, e, z, z2, lf)
                steps(dve.scalar_tensor_tensor(out=lf, in0=gf, scalar=0.0, in1=lf, op0=ALU.min,
                                               op1=ALU.subtract))
                steps(dve.memset(e, 1.0))
                convolve(1)
                steps(dve.tensor_tensor_scan(out=run, data0=e, data1=lf, initial=0.0, op0=ALU.mult,
                                             op1=ALU.add))
                B = chain_b[:, 4]
                for s, first in ((0, 0.0), (1, B[back, 0:1])):
                    steps(dve.tensor_tensor_scan(
                        out=B[back, segs[s]][:, ::-1], data0=chain_b[back, 0, segs[s]][:, ::-1],
                        data1=chain_b[back, 3, segs[s]][:, ::-1], initial=first, op0=ALU.mult, op1=ALU.add))
                dve.tensor_tensor(c, gi, run, ALU.subtract).then_inc(c_ready, 1)
                convolve(2)
                dve.wait_ge(c_ready, 1)
                steps(dve.tensor_tensor_scan(out=m_run, data0=c, data1=c, initial=NEG, op0=ALU.max,
                                             op1=ALU.max))
                M, C = chain_b[:, 6], chain_b[:, 5]
                for s, first in ((0, NEG), (1, M[back, 0:1])):
                    steps(dve.tensor_tensor_scan(
                        out=M[back, segs[s]][:, ::-1], data0=C[back, segs[s]][:, ::-1],
                        data1=C[back, segs[s]][:, ::-1], initial=first, op0=ALU.max, op1=ALU.max))
                steps(dve.tensor_scalar(ns[:, 0:N_LAT], m_run[:, LAT], -1.0, None, ALU.mult))
                steps(dve.tensor_tensor(ns[:, LAT], ns[:, 0:N_LAT], run[:, LAT], ALU.subtract))
                dve.tensor_scalar(ns[:, LAT], ns[:, LAT], 80.0, None, ALU.min).then_inc(stab_in, 1)
                convolve(3)
                convolve(ML_H)
                kv_norm.dve_mean(dve)
                kv_norm.dve_scale(dve, steps)
                for n in range(ML_H + 1, 2 * ML_H):
                    convolve(n)
                q_norm.dve_mean(dve)
                q_norm.dve_scale(dve, steps)
                dve.wait_ge(key_swapped, 1)
                steps(dve.tensor_tensor(q_sin[0:QD, 0], key_ps, const("rope_sin")[0:QD], ALU.mult))
                steps(dve.tensor_tensor(k_rot[0:QD, LAT], k_rot[0:QD, LAT], const("rope_cos")[0:QD], ALU.mult))
                dve.tensor_tensor(k_rot[0:QD, LAT], k_rot[0:QD, LAT], q_sin[0:QD, 0],
                                  ALU.add).then_inc(key_ready, 1)
                dve.wait_ge(key_ready, 1)
                dve.wait_ge(c_turned, 1)
                dve.tensor_copy(c_col, c_ps.rearrange("p (a b) -> p a b", a=4)).then_inc(c_col_ready, 1)
                for h in range(MLA_H):
                    dve.wait_ge(q_swapped, h + 1)
                    b = h % 2
                    steps(dve.tensor_tensor(q_sin[0:QD, b], swap_ps[b], const("rope_sin")[0:QD], ALU.mult))
                    steps(dve.tensor_tensor(q_att[0:QD, h], q_raw[0:QD, b], const("rope_cos")[0:QD], ALU.mult))
                    dve.tensor_tensor(q_att[0:QD, h], q_att[0:QD, h], q_sin[0:QD, b], ALU.add).then_inc(q_ready, 1)
                dve.wait_ge(c_col_ready, 1)

                def ml_d(m):
                    h, d = m // 2, m % 2
                    dve.wait_ge(ml_spread, m + 1)
                    if m >= 2:
                        dve.wait_ge(ml_sums, m - 1)
                    for kt in range(T // P):
                        row = 32 * d + h
                        last = dve.tensor_scalar(weights_ml[:, m % 2, kt], spread_ps[:, 0:N_LAT],
                                                 c_col[:, kt, row:row + 1], 0.0, ALU.add, ALU.min)
                    last.then_inc(ml_arg, 1)

                def ml_p(m):
                    h, d = m // 2, m % 2
                    dve.wait_ge(ml_exp, m + 1)
                    dve.wait_ge(ml_scores, h + 1)
                    at = weights_ml[:, m % 2].rearrange("p a b -> p (a b)")
                    steps(dve.scalar_tensor_tensor(
                        out=at, in0=ml_scores_ps.rearrange("p a b -> p (a b)"), scalar=ML_SCALE, in1=at,
                        op0=ALU.mult, op1=ALU.mult))
                    late = weights_ml[:, m % 2, 2:4]
                    dve.tensor_tensor(late, late, const("causal")[:, d], ALU.mult).then_inc(ml_weights, 1)

                def ml_h(m):
                    h, d = m // 2, m % 2
                    dve.wait_ge(ml_abs, m + 1)
                    dve.wait_ge(bound_kept, m + 1)
                    steps(dve.tensor_tensor(h_rec, den_abs, bound[:, m % 2], ALU.max))
                    steps(dve.reciprocal(h_rec, h_rec))
                    to = h_sum[:, h] if d == 0 else h_rec
                    if d == 0:
                        dve.tensor_tensor(to, sums_ps[0][:, 0:N_LAT], h_rec, ALU.mult).then_inc(ml_head, 1)
                    else:
                        steps(dve.tensor_tensor(to, sums_ps[1][:, 0:N_LAT], h_rec, ALU.mult))
                        dve.tensor_tensor(h_sum[:, h], h_sum[:, h], h_rec, ALU.add).then_inc(ml_head, 1)
                    dve.wait_ge(ml_head, m + 1)

                def head_mean(h):
                    dve.wait_ge(out_ss, h + 1)
                    dve.tensor_scalar(head_rms[:], head_ps, 4.0 / P, 4.0 * EPS, ALU.mult,
                                      ALU.add).then_inc(out_ms, 1)

                def head_finish(h):
                    dve.wait_ge(out_root, h + 1)
                    steps(dve.reciprocal(head_rms[:], head_rms[:]))
                    steps(dve.scalar_tensor_tensor(out=h_sum[:, h], in0=h_sum[:, h],
                                                   scalar=col("ml_head_g")[:, h:h + 1], in1=head_rms[:],
                                                   op0=ALU.mult, op1=ALU.mult))
                    dve.scalar_tensor_tensor(out=mix2[:, h], in0=o_tanh[:, h], scalar=1.0,
                                             in1=h_sum[:, h], op0=ALU.add,
                                             op1=ALU.mult).then_inc(ml_mixed, 1)

                ml_d(0)
                for m in range(M_UNITS):
                    ml_p(m)
                    if m in (4, 6):
                        head_mean((m - 4) // 2)
                    for qt in range(2):
                        dve.wait_ge(att_scores, 2 * m + qt + 1)
                        steps(dve.reduce_max(soft_a[:, qt, 0:1], att_ps[qt], AX))
                        dve.tensor_scalar(soft_a[:, qt, 1:2], soft_a[:, qt, 0:1], -ATT_SCALE, None,
                                          ALU.mult).then_inc(att_max, 1)
                    if m >= 1:
                        ml_h(m - 1)
                    for qt in range(2):
                        dve.wait_ge(att_exp, 2 * m + qt + 1)
                        dve.reciprocal(soft_a[:, qt, 3:4], soft_a[:, qt, 2:3]).then_inc(att_sum_inv, 1)
                    if m + 1 < M_UNITS:
                        ml_d(m + 1)
                    if m in (4, 6):
                        head_finish((m - 4) // 2)
                head_mean(2)
                ml_h(M_UNITS - 1)
                head_finish(2)
                head_mean(3)
                head_finish(3)
                for tile in range(N_LAT // P):
                    at = slice(SEG + tile * P, SEG + (tile + 1) * P)
                    for n in range(KT):
                        unit = KT * tile + n
                        dve.wait_ge(odd_out, unit + 1)
                        dve.scalar_tensor_tensor(
                            out=hT[:, n, at], in0=ps[:, BANK[unit % 4], 0:P],
                            scalar=modc[:, 1, 2, n, 1:2], in1=hT[:, n, at], op0=ALU.mult,
                            op1=ALU.add).then_inc(odd_added, 1)
                        if (tile, n) == (1, 3):
                            norm1.dve_mean(dve)
                        if (tile, n) == (1, 5):
                            norm1.dve_scale(dve, steps)

            @block.tensor
            def _(pe):
                def swap_q(h):
                    pe.wait_ge(unit_taken, unit1["uq", h])
                    if h == 1:
                        pe.wait_ge(key_ready, 1)
                    if h >= 2:
                        pe.wait_ge(q_ready, h - 1)
                    pe.matmul(swap_ps[h % 2], const("rope_swap")[0:QD], q_raw[0:QD, h % 2],
                              start=True, stop=True).then_inc(q_swapped, 1)

                mix1.pe_sums(pe, ones[:])
                for n, (part, i) in enumerate(UNITS1):
                    bank = ps[:, BANK[n % 4], :]
                    if n >= 4:
                        pe.wait_ge(unit_taken, n - 3)
                    if part in width:
                        if i == 0:
                            pe.wait_ge(part_loaded[part], 16)
                        w = od_part(part)
                        rows = min(P, width[part])
                        tokens = LAT if part in LAT_ONLY else slice(0, T)
                        size = tokens.stop - tokens.start
                        for k in range(KT):
                            if n == 0:
                                pe.wait_ge(mix1.ready, k + 1)
                            if part == "v":
                                last = pe.matmul(bank, uT[:, k, i * P:(i + 1) * P], w[:, k],
                                                 start=(k == 0), stop=(k == KT - 1))
                            else:
                                last = pe.matmul(bank[0:rows, 0:size], w[:, k, i * P:i * P + rows],
                                                 uT[:, k, tokens], start=(k == 0), stop=(k == KT - 1))
                    elif part == "va":
                        if i == 0:
                            pe.wait_ge(mla_loaded, 48)
                            pe.wait_ge(kv_norm.ready, KV_LORA // P)
                        for k in range(KV_LORA // P):
                            last = pe.matmul(bank, ckv[:, k, i * P:(i + 1) * P], uv_w[:, k],
                                             start=(k == 0), stop=(k == KV_LORA // P - 1))
                    elif part == "uk":
                        for k in range(KV_LORA // P):
                            last = pe.matmul(bank[0:NOPE], uk_w[:, k, i], ckv[:, k],
                                             start=(k == 0), stop=(k == KV_LORA // P - 1))
                    else:
                        if i == 0:
                            pe.wait_ge(q_norm.ready, Q_LORA // P)
                        for k in range(Q_LORA // P):
                            last = pe.matmul(bank[0:QD, 0:N_LAT], uq_w[:, k, i * QD:(i + 1) * QD], cq[:, k],
                                             start=(k == 0), stop=(k == Q_LORA // P - 1))
                    last.then_inc(unit_out, 1)
                    if (part, i) == ("q", 0):
                        kv_norm.pe_sums(pe, ones[:])
                    if (part, i) == ("krope", 0):
                        q_norm.pe_sums(pe, ones[:])
                    if (part, i) == ("va", 0):
                        pe.wait_ge(unit_taken, unit1["krope", 0])
                        pe.matmul(key_ps, const("rope_swap")[0:QD], k_rot[0:QD, LAT], start=True,
                                  stop=True).then_inc(key_swapped, 1)
                    if (part, i) == ("va", 2):
                        pe.wait_ge(c_ready, 1)
                        pe.wait_ge(q_norm.mean, 1)
                        for kt in range(T // P):
                            last = pe.transpose(c_ps[:, kt * HALF_ROWS:(kt + 1) * HALF_ROWS],
                                                chain_b[0:HALF_ROWS, 5, kt * P:(kt + 1) * P],
                                                ident[0:HALF_ROWS, 0:HALF_ROWS])
                        last.then_inc(c_turned, 1)
                    if part == "uq" and i >= 1:
                        swap_q(i - 1)
                swap_q(MLA_H - 1)

                def spread(m):
                    if m >= 1:
                        pe.wait_ge(ml_arg, m)
                        pe.wait_ge(bound_kept, m)
                    i = ML_H * (m % 2) + m // 2
                    pe.matmul(spread_ps, const("pick")[0:HALF_ROWS, i], chain_b[0:HALF_ROWS, 7],
                              start=True, stop=True).then_inc(ml_spread, 1)

                def ml_score(h):
                    if h >= 1:
                        pe.wait_ge(ml_weights, 2 * h)
                    for kt in range(T // P):
                        last = pe.matmul(ml_scores_ps[:, kt // 2, kt % 2 * N_LAT:kt % 2 * N_LAT + N_LAT],
                                         ks_ml[:, h, kt * P:(kt + 1) * P], qs_ml[:, h], start=True, stop=True)
                    last.then_inc(ml_scores, 1)

                def attend(h):
                    pe.wait_ge(att_kept, 2 * h + 2)
                    if h >= 1:
                        pe.wait_ge(att_mixed, h)
                    if h in (3, 5, 7):
                        pe.wait_ge(out_ms, (h - 1) // 2)
                    for kt in range(T // P):
                        last = pe.matmul(att_out_ps, v_att[:, kt, h * VD:(h + 1) * VD],
                                         probs_t[:, kt], start=(kt == 0), stop=(kt == T // P - 1))
                    last.then_inc(att_out, 1)

                def head_sum(h):
                    pe.wait_ge(out_sq, h + 1)
                    pe.wait_ge(att_mixed, min(2 * h + 3, MLA_H))
                    pe.matmul(head_ps, ones[:], squares[:, 0, 0:N_LAT], start=True,
                              stop=True).then_inc(out_ss, 1)

                pe.wait_ge(unit_taken, len(UNITS1))
                pe.wait_ge(stab_ready, 1)
                pe.wait_ge(qk_ready, 2 * ML_H)
                pe.wait_ge(key_ready, 1)
                pe.wait_ge(c_col_ready, 1)
                spread(0)
                pe.wait_ge(q_ready, MLA_H)
                ml_score(0)
                pe.wait_ge(k_rope_ready, MLA_H)
                for m in range(M_UNITS):
                    h = m // 2
                    if m + 1 < M_UNITS:
                        spread(m + 1)
                    for qt in range(2):
                        if m >= 1:
                            pe.wait_ge(att_kept, 2 * m)
                        pe.matmul(att_ps[qt], q_att[0:QD, m, qt * P:(qt + 1) * P], k_att[0:QD, m],
                                  start=True, stop=True).then_inc(att_scores, 1)
                    if m >= 1:
                        attend(m - 1)
                    pe.wait_ge(ml_weights, m + 1)
                    if m % 2 == 1 and h + 1 < ML_H:
                        ml_score(h + 1)
                    if m >= 2:
                        pe.wait_ge(ml_head, m - 1)
                    for to, lhs in ((slice(0, N_LAT), None), (LAT, ones[:])):
                        for kt in range(T // P):
                            last = pe.matmul(sums_ps[m % 2][:, to],
                                             v_tok[:, kt, h * P:(h + 1) * P] if lhs is None else lhs,
                                             weights_ml[:, m % 2, kt], start=(kt == 0), stop=(kt == T // P - 1))
                    last.then_inc(ml_sums, 1)
                    if m in (3, 5, 7):
                        head_sum((m - 3) // 2)
                    for qt in range(2):
                        pe.wait_ge(att_probs, 2 * m + qt + 1)
                        for kt in range(T // P):
                            last = pe.transpose(att_ps[qt][:, kt * P:(kt + 1) * P],
                                                probs[:, qt, kt * P:(kt + 1) * P], ident)
                        last.then_inc(att_turned, 1)
                attend(M_UNITS - 1)
                head_sum(ML_H - 1)
                pe.wait_ge(w_out2_loaded, 16)
                pe.wait_ge(att_mixed, MLA_H)
                pe.wait_ge(ml_head, M_UNITS)
                ORDER = list(range(ML_H, KT)) + list(range(ML_H))
                for first in range(0, KT * N_LAT // P, 4):
                    for ks in (ORDER[:-2], ORDER[-2:]):
                        for unit in range(first, first + 4):
                            tile, n = unit // KT, unit % KT
                            if unit >= 4 and ks[0] == ORDER[0]:
                                pe.wait_ge(odd_added, unit - 3)
                            for k in ks:
                                if k < ML_H:
                                    pe.wait_ge(ml_mixed, k + 1)
                                last = pe.matmul(ps[:, BANK[n % 4], 0:P], w_out2[:, k, n * P:(n + 1) * P],
                                                 mix2[:, k, tile * P:(tile + 1) * P],
                                                 start=(k == ORDER[0]), stop=(k == ORDER[-1]))
                            if ks[-1] == ORDER[-1]:
                                last.then_inc(odd_out, 1)
                    if first == KT:
                        norm1.pe_sums(pe, ones[:])
        odd_stack.close()
        end_phase()

        def final_norm(tile, bank):
            part = slice(SEG + tile * P, SEG + (tile + 1) * P)
            return Norm(f"final_norm{tile}", sem, lambda d: hT[:, d, part], squares,
                        ps[:, bank, 0:P], rms[:, part], lambda d: uT[:, d, part], P, KT)

        peer(1, SEG, SEG // P, late=slice(SEG + P, T), ahead=lambda bank: final_norm(0, bank))

        last_norm = final_norm(1, 0)
        stored = sem("stored")
        dve_steps = sem("last_dve_steps")
        with nc.Block() as block:
            @block.scalar
            def _(act):
                last_norm.act_squares(act)
                last_norm.act_root(act)
                last_norm.act_affine(act, [slice(0, P)], lambda d, _: col("final_g")[:, d:d + 1], None)

            @block.vector
            def _(dve):
                steps = Steps(dve, dve_steps)
                last_norm.dve_mean(dve)
                last_norm.dve_scale(dve, steps)

            @block.tensor
            def _(pe):
                last_norm.pe_sums(pe, ones[:])

            @block.sync
            def _(sp_eng):
                sp_eng.dma_start(out[:, :, 0:P], uT[:, :, SEG:SEG + P]).then_inc(stored, 16)
                sp_eng.wait_ge(last_norm.ready, KT)
                sp_eng.dma_start(out[:, :, P:2 * P], uT[:, :, SEG + P:T]).then_inc(stored, 16)
                sp_eng.wait_ge(stored, 32)


def blocks_of(v):
    return v.reshape(-1, P).T


def rows_of(w):
    return np.ascontiguousarray(w.reshape(-1, P, w.shape[-1]).transpose(1, 0, 2))


def constants():
    c = np.zeros((P, N_CONSTS), np.float32)

    def put(name, value):
        at, shape = CONSTS[name]
        value = np.asarray(value, np.float64)
        value = value.reshape(value.shape[0], -1)
        c[:value.shape[0], at:at + value.shape[1]] = value

    a = 2 * np.pi * (np.outer(np.arange(64), np.arange(64)) % 64) / 64
    put("chan_dft", np.concatenate([np.kron(np.eye(2), np.cos(a)), np.kron(np.eye(2), np.sin(a))], 1))
    a = 2 * np.pi * (np.outer(np.arange(SEG), np.arange(SEG)) % SEG) / SEG
    both = np.stack([np.cos(a), -np.sin(a)]) / 128.0
    put("time_dft", both.reshape(2, 2, P, SEG).transpose(2, 0, 1, 3))
    half = ROPE // 2
    inv = (np.float32(10000.0) ** (-np.arange(0, half, 2, dtype=np.float32) / np.float32(half))).astype(np.float32)
    row = np.repeat(np.arange(SEG // 64, dtype=np.float32), 64)
    colu = np.tile(np.arange(64, dtype=np.float32), SEG // 64)
    ang = np.concatenate([row[:, None] * inv, colu[:, None] * inv], axis=-1).astype(np.float32)
    cos, sin = np.ones((QD, SEG)), np.zeros((QD, SEG))
    cos[NOPE:] = np.repeat(np.cos(ang.astype(np.float64)).T, 2, axis=0)
    sin[NOPE:] = np.repeat(np.sin(ang.astype(np.float64)).T, 2, axis=0)
    put("rope_cos", cos)
    put("rope_sin", sin)
    swap = np.zeros((QD, QD))
    for i in range(NOPE, QD, 2):
        swap[i + 1, i] = -1.0
        swap[i, i + 1] = 1.0
    put("rope_swap", swap)
    s, t = np.arange(SEG)[:, None], np.arange(SEG)[None, :]
    masks = np.stack([s <= t, s >= t]).astype(np.float64)
    put("causal", masks.reshape(2, 2, P, SEG).transpose(2, 0, 1, 3))
    pick = np.zeros((P, 2 * ML_H, P))
    for i in range(2 * ML_H):
        pick[32 * (i // ML_H) + i % ML_H, i] = 1.0
    put("pick", pick)
    put("iota", np.broadcast_to(np.arange(TOPK), (P, TOPK)))
    return c


def lay_out(x, c, ctx, c_ctx, mod_w, mod_b, norm_mix_g, norm_ffn_g, ev_w_in, ev_w_out, rg_conv_w,
            rg_conv_b, rg_wa, rg_ba, rg_wx, rg_bx, rg_lam, fn_w, fn_b, od_w_in, od_w_out,
            ml_conv_w, ml_conv_b, ml_gate_b, ml_head_g, mla_q_norm_g, mla_w_uq, mla_kv_norm_g,
            mla_w_ukv, peer_w_q, peer_keys, peer_u, peer_v, final_g):
    cols = np.zeros((P, N_COLS), np.float32)

    def put(name, value):
        at, shape = COLS[name]
        value = value.reshape(value.shape[0], -1)
        cols[:value.shape[0], at:at + value.shape[1]] = value

    put("ident", np.eye(P))
    put("cond", np.stack([blocks_of(c_ctx), blocks_of(c[0])], 2))
    put("mod_b", blocks_of(mod_b))
    put("norm_g", np.stack([norm_mix_g, norm_ffn_g], 1).reshape(-1, P).T)
    put("final_g", blocks_of(final_g))
    put("rg_conv_w", rg_conv_w[0].reshape(CONV_W, RG_H, P).transpose(2, 1, 0))
    put("rg_conv_b", blocks_of(rg_conv_b))
    put("rg_ba", blocks_of(rg_ba))
    put("rg_bx", blocks_of(rg_bx))
    put("rg_lam", blocks_of(rg_lam))
    put("fn_b", blocks_of(fn_b))
    put("ml_conv_w", ml_conv_w[0].reshape(CONV_W, 8, P).transpose(2, 1, 0))
    put("ml_conv_b", blocks_of(ml_conv_b))
    put("ml_head_g", blocks_of(ml_head_g))
    put("q_norm_g", blocks_of(mla_q_norm_g))
    put("kv_norm_g", blocks_of(mla_kv_norm_g))
    gb = np.zeros((GATE_ROWS, 1), np.float32)
    b = ml_gate_b.reshape(2, 2, ML_H)
    for d in range(2):
        for kind in range(2):
            at = 64 * kind + 32 * d
            gb[at:at + ML_H, 0] = b[d, kind]
    put("ml_gate_b", gb)

    even = np.zeros((P, N_EVEN), np.float32)
    at, _ = EVEN["fn_w"]
    even[:, :at] = np.stack([rg_wa[0], rg_wx[0]]).transpose(3, 0, 1, 2, 4).reshape(P, -1)
    even[:, at:] = fn_w[0].reshape(2, P, 64).transpose(1, 0, 2).reshape(P, -1)

    w = od_w_in[0]
    parts, at = {}, 0
    for name, n in ODD_PARTS[:4]:
        parts[name] = w[:, at:at + n]
        at += n
    gates = w[:, at:at + 16].reshape(D, 2, 2, ML_H)
    at += 16
    for name, n in ODD_PARTS[4:6]:
        parts[name] = w[:, at:at + n]
        at += n
    krope = np.zeros((D, QD), np.float32)
    krope[:, NOPE:] = w[:, at:]
    parts["krope"] = krope
    g = np.zeros((D, GATE_ROWS), np.float32)
    for kind in range(2):
        for d in range(2):
            g[:, 64 * kind + 32 * d:64 * kind + 32 * d + ML_H] = gates[:, d, kind]
    parts["gates"] = g
    od = np.concatenate([rows_of(parts[name]).reshape(P, -1) for name, _ in ODD_PARTS], 1)

    tokens = np.concatenate([ctx[0], x[0]], 0)
    ukv = rows_of(mla_w_ukv[0]).reshape(P, KV_LORA // P, MLA_H, NOPE + VD)
    return {
        "hT0": rows_of(np.ascontiguousarray(tokens.T)),
        "cols_in": cols,
        "consts_in": constants(),
        "mod_w": np.ascontiguousarray(
            mod_w.reshape(2, KT, P, N_MOD * KT // PIECE_J, PIECE_J * P).transpose(0, 3, 2, 1, 4)
        ).reshape(PIECES, P, KT, PIECE_J * P),
        "ev_in": np.ascontiguousarray(ev_w_in[0].reshape(KT, P, 7, 2 * P).transpose(2, 1, 0, 3)),
        "ev_out": rows_of(ev_w_out[0]),
        "even_in": even,
        "od": np.ascontiguousarray(od),
        "w_uq": rows_of(mla_w_uq[0]),
        "w_uk": np.ascontiguousarray(ukv[..., :NOPE]),
        "w_uv": np.ascontiguousarray(ukv[..., NOPE:]),
        "od_out": rows_of(od_w_out[0]),
        "peer_q": np.ascontiguousarray(
            peer_w_q.reshape(2, KT, P, 4, 4 * P).transpose(0, 3, 2, 1, 4)),
        "peer_keys": np.ascontiguousarray(peer_keys.transpose(0, 4, 2, 1, 3)),
        "peer_u0": peer_u[0], "peer_u1": peer_u[1], "peer_v0": peer_v[0], "peer_v1": peer_v[1],
    }


def kernel(**inputs):
    import concourse.bacc as _bacc
    from concourse import mybir as _mybir
    from concourse.bass_utils import run_bass_kernel_spmd as _run
    nc = _bacc.Bacc("TRN2", target_bir_lowering=False, num_devices=1)
    data = lay_out(**{name: np.asarray(value) for name, value in inputs.items()})
    args, arrays = {}, {}
    for name, value in data.items():
        arrays[f"in_{name}_dram"] = value
        args[name] = nc.dram_tensor(f"in_{name}_dram", value.shape, _mybir.dt.from_np(value.dtype),
                                    kind="ExternalInput").ap()
    out = nc.dram_tensor("out_0_dram", (P, KT, SEG), F32, kind="ExternalOutput").ap()
    args["peer_u"] = [args.pop("peer_u0"), args.pop("peer_u1")]
    args["peer_v"] = [args.pop("peer_v0"), args.pop("peer_v1")]
    backbone(nc, out=out, **args)
    got = _run(nc, [arrays], core_ids=[0]).results[0]["out_0_dram"]
    return np.ascontiguousarray(got.transpose(1, 0, 2).reshape(D, SEG).T).reshape(1, SEG, D)
```
